# Optimizing a Trainium2 kernel written in Bass

```python
import jax, jax.numpy as jnp
from jax import lax
import numpy as np

D_MODEL = 1024
BATCH = 1
SEQ = 256
DEPTH = 1

ATTN_HEADS = 8
ATTN_KV_HEADS = 2
ATTN_GROUP = ATTN_HEADS // ATTN_KV_HEADS
ATTN_HEAD_DIM = 64
ATTN_WIDTH = ATTN_HEADS * ATTN_HEAD_DIM
KV_WIDTH = ATTN_KV_HEADS * ATTN_HEAD_DIM
WINDOW = 128
ATTN_BLOCK = 128

HGRN_HEADS = 4
HGRN_DK = 128
HGRN_DV = 128
HGRN_WIDTH = HGRN_HEADS * HGRN_DK
HGRN_V_WIDTH = HGRN_HEADS * HGRN_DV
HGRN_CHUNK = 32

N_BRANCHES = 2
IN_WIDTH = ATTN_WIDTH + 2 * KV_WIDTH + 2 * HGRN_WIDTH + 2 * HGRN_V_WIDTH + N_BRANCHES * D_MODEL

PEER_HEADS = 8
PEER_N_KEYS = 128
PEER_N_EXPERTS = PEER_N_KEYS * PEER_N_KEYS
PEER_KEY_DIM = 128
PEER_TOPK = 16
PEER_TOKEN_BLOCK = 128

EPS = 1e-6
MASK_VALUE = -1e30


def rms_norm(x, g):
    xf = x.astype(jnp.float32)
    y = xf * lax.rsqrt(jnp.mean(xf * xf, axis=-1, keepdims=True) + EPS)
    return (y * g.astype(jnp.float32)).astype(x.dtype)

def alibi_slopes():
    return jnp.asarray(2.0 ** (-8.0 * np.arange(1, ATTN_HEADS + 1) / ATTN_HEADS), dtype=jnp.float32)

def split_combined(proj):
    sizes = (ATTN_WIDTH, KV_WIDTH, KV_WIDTH, HGRN_WIDTH, HGRN_WIDTH,
             HGRN_V_WIDTH, HGRN_V_WIDTH, D_MODEL, D_MODEL)
    offsets = np.cumsum(sizes)[:-1].tolist()
    return jnp.split(proj, offsets, axis=-1)

def sliding_window_attention(q, k, v, sinks):
    B, S = q.shape[0], q.shape[1]
    W = ATTN_BLOCK
    nb = S // W
    qb = q.reshape(B, nb, W, ATTN_KV_HEADS, ATTN_GROUP, ATTN_HEAD_DIM)

    def with_prev(t):
        tb = t.reshape(B, nb, W, ATTN_KV_HEADS, ATTN_HEAD_DIM)
        prev = jnp.concatenate([jnp.zeros_like(tb[:, :1]), tb[:, :-1]], axis=1)
        return jnp.concatenate([prev, tb], axis=2)

    kc, vc = with_prev(k), with_prev(v)
    scale = ATTN_HEAD_DIM ** -0.5
    s = jnp.einsum('bnqkgd,bnskd->bnkgqs', qb, kc,
                   preferred_element_type=jnp.float32) * scale
    qpos = jnp.arange(W)[:, None] + W
    kpos = jnp.arange(2 * W)[None, :]
    dist = qpos - kpos
    blk = jnp.arange(nb)[:, None, None]
    valid = (dist >= 0) & (dist < WINDOW) & (blk * W + kpos - W >= 0)
    slopes = alibi_slopes().reshape(ATTN_KV_HEADS, ATTN_GROUP)
    s = s - slopes[:, :, None, None] * dist.astype(jnp.float32)
    s = jnp.where(valid[None, :, None, None], s, MASK_VALUE)
    sink = jnp.broadcast_to(sinks.astype(jnp.float32).reshape(ATTN_KV_HEADS, ATTN_GROUP)[:, :, None, None],
                            s.shape[:-1] + (1,))
    p = jax.nn.softmax(jnp.concatenate([s, sink], axis=-1), axis=-1)[..., :-1]
    o = jnp.einsum('bnkgqs,bnskd->bnqkgd', p.astype(v.dtype), vc)
    return o.reshape(B, S, ATTN_WIDTH)

def hgrn2_recurrence(q, f_logit, i, lower_bound):
    B, S = q.shape[0], q.shape[1]
    C = HGRN_CHUNK
    nc = S // C
    f32 = jnp.float32
    f = lower_bound + (1.0 - lower_bound) * jax.nn.sigmoid(f_logit.astype(f32))
    k = 1.0 - f
    logf = jnp.log(f)

    def chunk(t):
        return t.reshape(B, nc, C, HGRN_HEADS, t.shape[-1])

    qc, kc, lc, vc = chunk(q.astype(f32)), chunk(k), chunk(logf), chunk(i.astype(f32))
    b = jnp.cumsum(lc, axis=2)
    q_dec = qc * jnp.exp(b)
    k_inv = kc * jnp.exp(-b)
    causal = jnp.tril(jnp.ones((C, C), dtype=bool))
    a = jnp.where(causal, jnp.einsum('bnthd,bnshd->bnhts', q_dec, k_inv), 0.0)
    o_intra = jnp.einsum('bnhts,bnshv->bnthv', a, vc)
    b_last = b[:, :, -1:]
    ds = jnp.einsum('bnshd,bnshv->bnhdv', kc * jnp.exp(b_last - b), vc)
    decay = jnp.exp(b_last[:, :, 0])

    def step(state, inp):
        dec, d = inp
        return dec[..., None] * state + d, state

    s0 = jnp.zeros((B, HGRN_HEADS, HGRN_DK, HGRN_DV), f32)
    _, s_prev = lax.scan(step, s0, (jnp.moveaxis(decay, 1, 0), jnp.moveaxis(ds, 1, 0)))
    s_prev = jnp.moveaxis(s_prev, 0, 1)
    o_inter = jnp.einsum('bnthd,bnhdv->bnthv', q_dec, s_prev)
    return (o_intra + o_inter).reshape(B, S, HGRN_HEADS, HGRN_DV)

def peer_layer(h, w_q, keys, u, v):
    B, S = h.shape[0], h.shape[1]
    q = (h @ w_q).reshape(B, S, PEER_HEADS, 2, PEER_KEY_DIM)
    sc = jnp.einsum('bshpd,phnd->bshpn', q, keys).astype(jnp.float32)
    v1, i1 = lax.top_k(sc[..., 0, :], PEER_TOPK)
    v2, i2 = lax.top_k(sc[..., 1, :], PEER_TOPK)
    cand = (v1[..., :, None] + v2[..., None, :]).reshape(B, S, PEER_HEADS, PEER_TOPK * PEER_TOPK)
    cidx = (i1[..., :, None] * PEER_N_KEYS + i2[..., None, :]).reshape(B, S, PEER_HEADS, PEER_TOPK * PEER_TOPK)
    best, pos = lax.top_k(cand, PEER_TOPK)
    idx = jnp.take_along_axis(cidx, pos, axis=-1)
    gates = jax.nn.softmax(best, axis=-1)
    T = B * S
    nblk = T // PEER_TOKEN_BLOCK
    hk = PEER_HEADS * PEER_TOPK
    hb = h.reshape(nblk, PEER_TOKEN_BLOCK, D_MODEL)
    ib = idx.reshape(nblk, PEER_TOKEN_BLOCK, hk)
    gb = gates.reshape(nblk, PEER_TOKEN_BLOCK, hk).astype(h.dtype)

    def expert_block(args):
        ht, it, gt = args
        ue = jnp.take(u, it, axis=0)
        act = jax.nn.gelu(jnp.einsum('tkd,td->tk', ue, ht), approximate=False)
        ve = jnp.take(v, it, axis=0)
        return jnp.einsum('tk,tkd->td', gt * act, ve)

    out = lax.map(expert_block, (hb, ib, gb))
    return out.reshape(B, S, D_MODEL)

def hybrid_layer(x, norm_mix_g, w_in, sinks, lower_bound, hgrn_norm_g, w_attn_proj,
                 w_hgrn_proj, w_out, norm_ffn_g, w_peer_q, peer_keys, peer_u, peer_v):
    B, S = x.shape[0], x.shape[1]
    h = rms_norm(x, norm_mix_g)
    aq, ak, av, hq, hf, hi, hg, ga, gh = split_combined(h @ w_in)
    y_attn = sliding_window_attention(aq.reshape(B, S, ATTN_HEADS, ATTN_HEAD_DIM),
                                      ak.reshape(B, S, ATTN_KV_HEADS, ATTN_HEAD_DIM),
                                      av.reshape(B, S, ATTN_KV_HEADS, ATTN_HEAD_DIM), sinks)
    o = hgrn2_recurrence(jax.nn.silu(hq).reshape(B, S, HGRN_HEADS, HGRN_DK),
                         hf.reshape(B, S, HGRN_HEADS, HGRN_DK),
                         hi.reshape(B, S, HGRN_HEADS, HGRN_DV), lower_bound)
    o = rms_norm(o, hgrn_norm_g).astype(x.dtype) * jax.nn.silu(hg.reshape(B, S, HGRN_HEADS, HGRN_DV))
    y_hgrn = o.reshape(B, S, HGRN_V_WIDTH)
    merged = jax.nn.sigmoid(ga) * (y_attn @ w_attn_proj) + jax.nn.sigmoid(gh) * (y_hgrn @ w_hgrn_proj)
    x = x + merged @ w_out
    x = x + peer_layer(rms_norm(x, norm_ffn_g), w_peer_q, peer_keys, peer_u, peer_v)
    return x

def first_inputs(seed: int = 0) -> dict:
    key = jax.random.key(seed)
    ks = jax.random.split(key, 16)
    f32 = jnp.float32
    n = jax.random.normal
    return {
        "x": n(ks[0], (BATCH, SEQ, D_MODEL), f32),
        "norm_mix_g": 1.0 + 0.02 * n(ks[1], (DEPTH, D_MODEL), f32),
        "w_in": n(ks[2], (DEPTH, D_MODEL, IN_WIDTH), f32) * D_MODEL ** -0.5,
        "attn_sinks": n(ks[3], (DEPTH, ATTN_HEADS), f32),
        "hgrn_lb_logits": 0.1 * n(ks[4], (DEPTH + 1, HGRN_WIDTH), f32),
        "hgrn_norm_g": 1.0 + 0.02 * n(ks[5], (DEPTH, HGRN_DV), f32),
        "w_attn_proj": n(ks[6], (DEPTH, ATTN_WIDTH, D_MODEL), f32) * ATTN_WIDTH ** -0.5,
        "w_hgrn_proj": n(ks[7], (DEPTH, HGRN_V_WIDTH, D_MODEL), f32) * HGRN_V_WIDTH ** -0.5,
        "w_out": n(ks[8], (DEPTH, D_MODEL, D_MODEL), f32) * D_MODEL ** -0.5,
        "norm_ffn_g": 1.0 + 0.02 * n(ks[9], (DEPTH, D_MODEL), f32),
        "w_peer_q": n(ks[10], (DEPTH, D_MODEL, PEER_HEADS * 2 * PEER_KEY_DIM), f32) * D_MODEL ** -0.5,
        "peer_keys": n(ks[11], (DEPTH, 2, PEER_HEADS, PEER_N_KEYS, PEER_KEY_DIM), f32) * PEER_KEY_DIM ** -0.5,
        "peer_u": n(ks[12], (DEPTH, PEER_N_EXPERTS, D_MODEL), f32) * D_MODEL ** -0.5,
        "peer_v": n(ks[13], (DEPTH, PEER_N_EXPERTS, D_MODEL), f32) * PEER_HEADS ** -0.5,
        "norm_final_g": 1.0 + 0.02 * n(ks[14], (D_MODEL,), f32),
    }

def first_block(x, norm_mix_g, w_in, attn_sinks, hgrn_lb_logits, hgrn_norm_g, w_attn_proj,
              w_hgrn_proj, w_out, norm_ffn_g, w_peer_q, peer_keys, peer_u, peer_v, norm_final_g):
    lower_bounds = jnp.cumsum(jax.nn.softmax(hgrn_lb_logits.astype(jnp.float32), axis=0), axis=0)
    for layer in range(DEPTH):
        x = hybrid_layer(x, norm_mix_g[layer], w_in[layer], attn_sinks[layer],
                         lower_bounds[layer].reshape(HGRN_HEADS, HGRN_DK), hgrn_norm_g[layer],
                         w_attn_proj[layer], w_hgrn_proj[layer], w_out[layer], norm_ffn_g[layer],
                         w_peer_q[layer], peer_keys[layer], peer_u[layer], peer_v[layer])
    return rms_norm(x, norm_final_g)


N_MEM = 256
D_MIX = D_MODEL
D_A = D_MIX // 4
D_B = D_MIX // 4
D_C = D_MIX // 2
H_A = 4
H_B = 4
H_C = 4
DH_A = D_A // H_A
DH_B = D_B // H_B
DH_C = D_C // H_C
CHUNK = 128
CONV_B = 31
CONV_C = 4
CONV_F = 3
N_XHEADS = 4
DH_X = D_MODEL // N_XHEADS
D_FF = ((8 * D_MODEL // 3 + 255) // 256) * 256
D_IN = 2 * D_A + 2 * D_B + 2 * D_C + 2 * H_C
RMS_EPS = 1e-6
LN_EPS = 1e-5


def rmsnorm(x, g):
    xf = x.astype(jnp.float32)
    y = xf * lax.rsqrt(jnp.mean(xf * xf, axis=-1, keepdims=True) + RMS_EPS)
    return (y * g.astype(jnp.float32)).astype(x.dtype)

def standardize(x):
    xf = x.astype(jnp.float32)
    mu = jnp.mean(xf, axis=-1, keepdims=True)
    var = jnp.mean(jnp.square(xf - mu), axis=-1, keepdims=True)
    return (xf - mu) * lax.rsqrt(var + LN_EPS)

def causal_dwconv(x, w, b):
    K, C = w.shape
    y = lax.conv_general_dilated(
        x, w[:, None, :].astype(x.dtype), window_strides=(1,),
        padding=[(K - 1, 0)], dimension_numbers=('NWC', 'WIO', 'NWC'),
        feature_group_count=C)
    return y + b.astype(x.dtype)

def gmlp_spatial_gating(u, v, ln_g, ln_b, w_s, b_s):
    Bsz, S, _ = v.shape
    vn = (standardize(v) * ln_g + ln_b).astype(v.dtype)
    vn = vn.reshape(Bsz, S // CHUNK, CHUNK, H_A, DH_A)
    mask = jnp.tril(jnp.ones((CHUNK, CHUNK), dtype=bool))
    w = jnp.where(mask, w_s, 0.0).astype(v.dtype)
    s = jnp.einsum('hts,bcshd->bcthd', w, vn) + b_s.T.astype(v.dtype)[None, None, :, :, None]
    return u * s.reshape(Bsz, S, D_A)

def conformer_conv(a, g, conv_w, conv_b, gn_g, gn_b):
    Bsz, S, _ = a.shape
    y = a * jax.nn.sigmoid(g)
    y = causal_dwconv(y, conv_w, conv_b)
    yn = standardize(y.reshape(Bsz, S, H_B, DH_B)).reshape(Bsz, S, D_B)
    y = (yn * gn_g + gn_b).astype(a.dtype)
    return jax.nn.silu(y)

def mlstm_chunkwise(q, k, v, logi, logf):
    Bsz, H, S, DH = q.shape
    NC = S // CHUNK
    q = q * (DH ** -0.5)

    def to_chunks(a):
        a = a.reshape((Bsz, H, NC, CHUNK) + a.shape[3:])
        return jnp.moveaxis(a, 2, 0)

    qc, kc, vc, ic, fc = (to_chunks(t) for t in (q, k, v, logi, logf))
    mask = jnp.tril(jnp.ones((CHUNK, CHUNK), dtype=bool))

    def step(carry, inp):
        C, n, m = carry
        qt, kt, vt, it, ft = inp
        bcum = jnp.cumsum(ft, axis=-1)
        dmat = bcum[..., :, None] - bcum[..., None, :] + it[..., None, :]
        dmat = jnp.where(mask, dmat, -jnp.inf)
        inter = bcum + m[..., None]
        m_t = jnp.maximum(inter, jnp.max(dmat, axis=-1))
        w_intra = jnp.exp(dmat - m_t[..., None])
        w_inter = jnp.exp(inter - m_t)
        scores = jnp.einsum('bhtd,bhsd->bhts', qt, kt) * w_intra
        num = (w_inter[..., None] * jnp.einsum('bhtd,bhde->bhte', qt, C)
               + jnp.einsum('bhts,bhse->bhte', scores, vt))
        den = w_inter * jnp.einsum('bhtd,bhd->bht', qt, n) + jnp.sum(scores, axis=-1)
        h = num / jnp.maximum(jnp.abs(den), jnp.exp(-m_t))[..., None]
        btot = bcum[..., -1]
        gdec = btot[..., None] - bcum + it
        m_new = jnp.maximum(btot + m, jnp.max(gdec, axis=-1))
        decay = jnp.exp(btot + m - m_new)
        wg = jnp.exp(gdec - m_new[..., None])
        C_new = decay[..., None, None] * C + jnp.einsum('bhs,bhsd,bhse->bhde', wg, kt, vt)
        n_new = decay[..., None] * n + jnp.einsum('bhs,bhsd->bhd', wg, kt)
        return (C_new, n_new, m_new), h

    init = (jnp.zeros((Bsz, H, DH, DH), jnp.float32),
            jnp.zeros((Bsz, H, DH), jnp.float32),
            jnp.zeros((Bsz, H), jnp.float32))
    _, hs = lax.scan(step, init, (qc, kc, vc, ic, fc))
    return jnp.moveaxis(hs, 0, 2).reshape(Bsz, H, S, DH)

def mlstm_group(xc, oc, gi, gf, b_igate, b_fgate, conv_w, conv_b, w_q, w_k, w_v, hn_g, skip):
    Bsz, S, _ = xc.shape
    xconv = jax.nn.silu(causal_dwconv(xc, conv_w, conv_b))
    xh = xconv.reshape(Bsz, S, H_C, DH_C)
    xv = xc.reshape(Bsz, S, H_C, DH_C)
    q = jnp.einsum('bshd,hde->bhse', xh, w_q).astype(jnp.float32)
    k = jnp.einsum('bshd,hde->bhse', xh, w_k).astype(jnp.float32)
    v = jnp.einsum('bshd,hde->bhse', xv, w_v).astype(jnp.float32)
    logi = jnp.transpose(gi.astype(jnp.float32) + b_igate.astype(jnp.float32), (0, 2, 1))
    logf = jax.nn.log_sigmoid(jnp.transpose(gf.astype(jnp.float32) + b_fgate.astype(jnp.float32), (0, 2, 1)))
    hcell = mlstm_chunkwise(q, k, v, logi, logf)
    hcell = jnp.transpose(hcell, (0, 2, 1, 3))
    hnorm = (standardize(hcell) * hn_g.reshape(H_C, DH_C)).reshape(Bsz, S, D_C).astype(xc.dtype)
    return jax.nn.sigmoid(oc) * (hnorm + skip * xconv)

def hybrid_mixer(hn, w_in, b_igate, b_fgate, ln_a_g, ln_a_b, w_s, b_s,
                 conv_b_w, conv_b_b, gn_b_g, gn_b_b, conv_c_w, conv_c_b,
                 w_q_c, w_k_c, w_v_c, hn_c_g, skip_c, w_out):
    z = hn @ w_in
    o0 = 2 * D_A
    o1 = o0 + 2 * D_B
    o2 = o1 + D_C
    o3 = o2 + D_C
    o4 = o3 + H_C
    za = jax.nn.gelu(z[..., :o0], approximate=False)
    y_a = gmlp_spatial_gating(za[..., :D_A], za[..., D_A:], ln_a_g, ln_a_b, w_s, b_s)
    zb = z[..., o0:o1]
    y_b = conformer_conv(zb[..., :D_B], zb[..., D_B:], conv_b_w, conv_b_b, gn_b_g, gn_b_b)
    y_c = mlstm_group(z[..., o1:o2], z[..., o2:o3], z[..., o3:o4], z[..., o4:],
                      b_igate, b_fgate, conv_c_w, conv_c_b, w_q_c, w_k_c, w_v_c, hn_c_g, skip_c)
    return jnp.concatenate([y_a, y_b, y_c], axis=-1) @ w_out

def cross_attention(hn, mn, w_xq, w_xkv, w_xo):
    Bsz, S, _ = hn.shape
    M = mn.shape[1]
    q = (hn @ w_xq).reshape(Bsz, S, N_XHEADS, DH_X)
    kv = mn @ w_xkv
    k = kv[..., :D_MODEL].reshape(Bsz, M, N_XHEADS, DH_X)
    v = kv[..., D_MODEL:].reshape(Bsz, M, N_XHEADS, DH_X)
    s = jnp.einsum('bshd,bmhd->bhsm', q, k).astype(jnp.float32) * (DH_X ** -0.5)
    p = jax.nn.softmax(s, axis=-1).astype(v.dtype)
    o = jnp.einsum('bhsm,bmhd->bshd', p, v).reshape(Bsz, S, D_MODEL)
    return o @ w_xo

def conv_glu(hn, w_up, conv_f_w, conv_f_b, w_down):
    up = hn @ w_up
    gate = jax.nn.gelu(causal_dwconv(up[..., :D_FF], conv_f_w, conv_f_b), approximate=False)
    return (gate * up[..., D_FF:]) @ w_down

def second_inputs(seed: int = 0) -> dict:
    key = jax.random.key(seed)
    ks = iter(jax.random.split(key, 48))

    def nrm(shape, scale):
        return jax.random.normal(next(ks), shape, jnp.float32) * scale

    L = DEPTH
    return {
        "x": nrm((BATCH, SEQ, D_MODEL), 1.0),
        "mem": nrm((BATCH, N_MEM, D_MODEL), 1.0),
        "norm_mix_g": 1.0 + nrm((L, D_MODEL), 0.02),
        "w_in": nrm((L, D_MODEL, D_IN), D_MODEL ** -0.5),
        "b_igate": nrm((L, H_C), 0.1),
        "b_fgate": jax.random.uniform(next(ks), (L, H_C), jnp.float32, 3.0, 6.0),
        "ln_a_g": 1.0 + nrm((L, D_A), 0.02),
        "ln_a_b": nrm((L, D_A), 0.02),
        "w_s": nrm((L, H_A, CHUNK, CHUNK), CHUNK ** -0.5),
        "b_s": 1.0 + nrm((L, H_A, CHUNK), 0.1),
        "conv_b_w": nrm((L, CONV_B, D_B), CONV_B ** -0.5),
        "conv_b_b": nrm((L, D_B), 0.02),
        "gn_b_g": 1.0 + nrm((L, D_B), 0.02),
        "gn_b_b": nrm((L, D_B), 0.02),
        "conv_c_w": nrm((L, CONV_C, D_C), CONV_C ** -0.5),
        "conv_c_b": nrm((L, D_C), 0.02),
        "w_q_c": nrm((L, H_C, DH_C, DH_C), DH_C ** -0.5),
        "w_k_c": nrm((L, H_C, DH_C, DH_C), DH_C ** -0.5),
        "w_v_c": nrm((L, H_C, DH_C, DH_C), DH_C ** -0.5),
        "hn_c_g": 1.0 + nrm((L, D_C), 0.02),
        "skip_c": 1.0 + nrm((L, D_C), 0.02),
        "w_out": nrm((L, D_MIX, D_MODEL), D_MIX ** -0.5),
        "norm_x_g": 1.0 + nrm((L, D_MODEL), 0.02),
        "norm_mem_g": 1.0 + nrm((L, D_MODEL), 0.02),
        "w_xq": nrm((L, D_MODEL, D_MODEL), D_MODEL ** -0.5),
        "w_xkv": nrm((L, D_MODEL, 2 * D_MODEL), D_MODEL ** -0.5),
        "w_xo": nrm((L, D_MODEL, D_MODEL), D_MODEL ** -0.5),
        "norm_ffn_g": 1.0 + nrm((L, D_MODEL), 0.02),
        "w_up": nrm((L, D_MODEL, 2 * D_FF), D_MODEL ** -0.5),
        "conv_f_w": nrm((L, CONV_F, D_FF), CONV_F ** -0.5),
        "conv_f_b": nrm((L, D_FF), 0.02),
        "w_down": nrm((L, D_FF, D_MODEL), D_FF ** -0.5),
        "final_g": 1.0 + nrm((D_MODEL,), 0.02),
    }

def second_block(x, mem, norm_mix_g, w_in, b_igate, b_fgate, ln_a_g, ln_a_b, w_s, b_s,
              conv_b_w, conv_b_b, gn_b_g, gn_b_b, conv_c_w, conv_c_b,
              w_q_c, w_k_c, w_v_c, hn_c_g, skip_c, w_out,
              norm_x_g, norm_mem_g, w_xq, w_xkv, w_xo,
              norm_ffn_g, w_up, conv_f_w, conv_f_b, w_down, final_g):
    h = x
    for l in range(DEPTH):
        hn = rmsnorm(h, norm_mix_g[l])
        h = h + hybrid_mixer(hn, w_in[l], b_igate[l], b_fgate[l], ln_a_g[l], ln_a_b[l],
                             w_s[l], b_s[l], conv_b_w[l], conv_b_b[l], gn_b_g[l], gn_b_b[l],
                             conv_c_w[l], conv_c_b[l], w_q_c[l], w_k_c[l], w_v_c[l],
                             hn_c_g[l], skip_c[l], w_out[l])
        hn = rmsnorm(h, norm_x_g[l])
        mn = rmsnorm(mem, norm_mem_g[l])
        h = h + cross_attention(hn, mn, w_xq[l], w_xkv[l], w_xo[l])
        hn = rmsnorm(h, norm_ffn_g[l])
        h = h + conv_glu(hn, w_up[l], conv_f_w[l], conv_f_b[l], w_down[l])
    return rmsnorm(h, final_g)


def setup_inputs(seed=0):
    out = dict(first_inputs(seed))
    for name, value in second_inputs(seed + 1).items():
        if name != "x":
            out[name + "_2"] = value
    return out


def reference(
    x, norm_mix_g, w_in, attn_sinks, hgrn_lb_logits, hgrn_norm_g, w_attn_proj, w_hgrn_proj,
    w_out, norm_ffn_g, w_peer_q, peer_keys, peer_u, peer_v, norm_final_g, mem_2, norm_mix_g_2,
    w_in_2, b_igate_2, b_fgate_2, ln_a_g_2, ln_a_b_2, w_s_2, b_s_2, conv_b_w_2, conv_b_b_2,
    gn_b_g_2, gn_b_b_2, conv_c_w_2, conv_c_b_2, w_q_c_2, w_k_c_2, w_v_c_2, hn_c_g_2, skip_c_2,
    w_out_2, norm_x_g_2, norm_mem_g_2, w_xq_2, w_xkv_2, w_xo_2, norm_ffn_g_2, w_up_2,
    conv_f_w_2, conv_f_b_2, w_down_2, final_g_2,
):
    x = first_block(
        x, norm_mix_g, w_in, attn_sinks, hgrn_lb_logits, hgrn_norm_g, w_attn_proj, w_hgrn_proj,
        w_out, norm_ffn_g, w_peer_q, peer_keys, peer_u, peer_v, norm_final_g,
    )
    return second_block(
        x, mem_2, norm_mix_g_2, w_in_2, b_igate_2, b_fgate_2, ln_a_g_2, ln_a_b_2, w_s_2, b_s_2,
        conv_b_w_2, conv_b_b_2, gn_b_g_2, gn_b_b_2, conv_c_w_2, conv_c_b_2, w_q_c_2, w_k_c_2,
        w_v_c_2, hn_c_g_2, skip_c_2, w_out_2, norm_x_g_2, norm_mem_g_2, w_xq_2, w_xkv_2, w_xo_2,
        norm_ffn_g_2, w_up_2, conv_f_w_2, conv_f_b_2, w_down_2, final_g_2,
    )


_drawn_inputs = setup_inputs


def setup_inputs(seed=0):
    import zlib

    import numpy as np

    out = dict(_drawn_inputs(seed))
    spreads = {}
    factors = {'hgrn_lb_logits': 3.351,
     'norm_mix_g_2': 2.989,
     'b_igate_2': 64.0,
     'ln_a_g_2': 8.0,
     'ln_a_b_2': 8.0,
     'conv_b_b_2': 4.061,
     'gn_b_g_2': 8.0,
     'gn_b_b_2': 8.0,
     'conv_c_b_2': 3.574,
     'hn_c_g_2': 7.824,
     'skip_c_2': 8.0,
     'norm_x_g_2': 8.0,
     'norm_mem_g_2': 8.0,
     'norm_ffn_g_2': 11.962,
     'conv_f_b_2': 17.227,
     'final_g_2': 7.844}
    for name, (base, spread) in spreads.items():
        noise = np.random.default_rng([zlib.crc32(name.encode()), seed]).standard_normal(out[name].shape)
        drawn = base * np.exp(spread * noise) if base else spread * noise
        out[name] = __import__('jax').numpy.asarray(drawn.astype(out[name].dtype))
    for name, factor in factors.items():
        out[name] = (out[name] * factor).astype(out[name].dtype)
    return out
```

```python
from contextlib import ExitStack

import numpy as np

import concourse.bass as bass
from concourse import mybir

ALU = mybir.AluOpType
ACT = mybir.ActivationFunctionType
F32 = mybir.dt.float32
F32R = mybir.dt.float32r
U32 = mybir.dt.uint32
I32 = mybir.dt.int32
AX = mybir.AxisListType.X

P = 128
D = 1024
T = 256
TB = 2
KD = D // P
DFF = 2816
EPS = 1e-6
LN_EPS = 1e-5
NEG = -1e30

RING = 3
UNIT = 2048

STREAMS = [
    ("w_in_t", 9, 2048),
    ("w_in_hi", 2, 2048),
    ("w_in_g", 8, 2048),
    ("w_ap", 2, 2048),
    ("w_hp", 2, 2048),
    ("w_out", 4, 2048),
    ("w_pq", 8, 2048),
    ("keys", 1, 2048),
    ("u", 64, 2048),
    ("v", 64, 2048),
    ("w2_t", 7, 2048),
    ("w2_v", 1, 2048),
    ("w2_c", 1, 1536),
    ("w2_out", 4, 2048),
    ("w_xk", 4, 2048),
    ("w_xv", 4, 2048),
    ("w_xq", 4, 2048),
    ("w_xo", 4, 2048),
    ("w_up", 22, 2048),
    ("w_down", 11, 2048),
]

VEC = [
    ("g_mix", 8), ("g_ffn", 8), ("g_mix2", 8), ("g_x2", 8), ("g_mem2", 8), ("g_ffn2", 8),
    ("lb", 8), ("g_hgrn", 1), ("cbw", 62), ("cbb", 2), ("gng", 2), ("gnb", 2),
    ("ccw", 16), ("ccb", 4), ("hng", 4), ("skip", 4), ("cfw", 66), ("cfb", 22),
    ("bi", 1), ("bf", 1), ("bs", 256), ("wgate", 64), ("wsT", 512),
]
CON = [
    ("ident", 128), ("mean128", 128), ("mean64", 128), ("ones", 128), ("dist", 256), ("wmask", 256),
    ("hmask", 128), ("causal", 128), ("sel", 512), ("iota", 128), ("iota16", 16), ("reset", 1024),
]
ROW = [("g_final", 1024), ("g_final2", 1024), ("lng", 256), ("lnb", 256), ("sinks", 8)]


def offsets(table):
    at, out = 0, {}
    for name, n in table:
        out[name] = (at, n)
        at += n
    return out, at


VOFF, NV = offsets(VEC)
COFF, NC = offsets(CON)
ROFF, NR = offsets(ROW)


class Engine:

    def __init__(self, name, sem):
        self.name, self.sem = name, sem
        self.count = 0
        self.work = []
        self.seen = {}

    def last(self):
        return (self.sem, self.count)

    def wait(self, *after):
        for sem, value in after:
            if value > self.seen.get(id(sem), 0):
                self.seen[id(sem)] = value
                self.work.append(lambda e, s=sem, v=value: e.wait_ge(s, v))

    def run(self, fn, *after):
        self.wait(*after)
        self.count += 1
        self.work.append(lambda e, f=fn, s=self.sem: f(e).then_inc(s, 1))
        return (self.sem, self.count)

    def then(self, fn, *after):
        return self.run(fn, self.last(), *after)

    def emit(self, eng):
        for f in self.work:
            f(eng)


def build(nc, x, mem, wdram, vec, con, row, out):
    ctx = ExitStack()
    with ctx:
        def sb(name, n, dt=F32, p=P):
            return ctx.enter_context(nc.sbuf_tensor(name, [p, n], dt))

        def sem(name):
            return ctx.enter_context(nc.semaphore(name))

        banks = [ctx.enter_context(nc.psum_tensor(f"bank{i}", [P, 512], F32)) for i in range(8)]
        arena = sb("arena", 32768)
        ring = [sb(f"ring{i}", UNIT) for i in range(RING)]
        vecs = sb("vecs", NV)
        cons = sb("cons", NC)
        xres = sb("xres", 2048)
        hT = sb("hT", 2048)
        lng = sb("rowsc", NR)
        small = sb("small", 768)

        pe = Engine("pe", sem("s_pe"))
        dve = Engine("dve", sem("s_dve"))
        act = Engine("act", sem("s_act"))
        pool = Engine("pool", sem("s_pool"))
        sp = Engine("sp", sem("s_sp"))
        s_ring = [sem(f"s_ring{i}") for i in range(RING)]
        s_in = sem("s_in")
        s_mem = sem("s_mem")
        s_out = sem("s_out")

        def V(name, a=0, b=None):
            o, n = VOFF[name]
            return vecs[:, o + a:o + (n if b is None else b)]

        def C(name, a=0, b=None):
            o, n = COFF[name]
            return cons[:, o + a:o + (n if b is None else b)]

        def R(name):
            o, n = ROFF[name]
            return lng[:, o:o + n]

        def view(at, n):
            return arena[:, at:at + n]

        def all_done():
            return [pe.last(), dve.last(), act.last(), pool.last()]

        n_in = [0]

        def load(dst, src):
            n_in[0] += 16
            sp.work.append(lambda e: e.dma_start(dst, src).then_inc(s_in, 16))

        for b in range(TB):
            load(xres[:, b * D:(b + 1) * D], x[b * P:(b + 1) * P, :])
        load(cons[:, :], con)
        load(vecs[:, :], vec)
        load(lng[:, :], row.partition_broadcast(P))
        loaded = (s_in, n_in[0])

        units = [(name, i, n) for name, k, n in STREAMS for i in range(k)]
        issued = [0]
        taken = [0]

        def fetch(*after):
            i = issued[0]
            if i >= len(units):
                return
            issued[0] += 1
            name, k, n = units[i]
            sp.wait(*after)
            dst, src, s = ring[i % RING][:, 0:n], wdram[name][k], s_ring[i % RING]
            sp.work.append(lambda e: e.dma_start(dst, src).then_inc(s, 16))

        for _ in range(RING):
            fetch()

        def take(name):
            i = taken[0]
            taken[0] += 1
            assert units[i][0] == name, (units[i], name)
            return ring[i % RING][:, 0:units[i][2]], (s_ring[i % RING], 16 * (i // RING + 1))

        def release(token):
            fetch(token)

        free = [[] for _ in range(8)]
        turn = [0]

        def bank():
            b = 4 + turn[0] % 4
            turn[0] += 1
            return b

        def mm_group(b, items, *after):
            waits = list(after) + free[b]
            free[b] = []

            def go(e):
                for o, l, r, st, sp_ in items:
                    ins = e.matmul(o, l, r, start=st, stop=sp_, skip_group_check=True)
                return ins

            return pe.run(go, *waits)

        def tr_group(b, items, *after):
            waits = list(after) + free[b]
            free[b] = []

            def go(e):
                for o, i in items:
                    k = i.shape[0]
                    ins = e.transpose(o, i, C("ident")[0:k, 0:k])
                return ins

            return pe.run(go, *waits)

        def ts(o, i, s1, s2, op0, op1=ALU.bypass):
            if s2 is None:
                return lambda e: e.tensor_scalar(o, i, s1, None, op0)
            return lambda e: e.tensor_scalar(o, i, s1, s2, op0, op1)

        def tt(o, a, b, op):
            return lambda e: e.tensor_tensor(o, a, b, op)

        def stt(o, a, s, b, op0, op1):
            return lambda e: e.scalar_tensor_tensor(o, a, s, b, op0, op1)

        def af(o, i, func, bias=None, scale=None, accum=None):
            kw = {}
            if bias is not None:
                kw["bias"] = bias
            if scale is not None:
                kw["scale"] = scale
            if accum is not None:
                kw["accum_out"] = accum
            return lambda e: e.activation(o, i, func, **kw)

        def cp(o, i):
            return lambda e: e.tensor_copy(o, i)

        def t3(ap, a):
            return ap.rearrange("p (a b) -> p a b", a=a)

        def t4(ap, a, b):
            return ap.rearrange("p (a b c) -> p a b c", a=a, b=b)

        hTv = t3(hT[:, :], KD)

        def inv_rms(src, scratch, st, n, eps, *after):
            act.then(af(scratch, src, ACT.Square, accum=st[:, 0:1]), *after)
            dve.then(ts(st[:, 1:2], st[:, 0:1], 1.0 / n, eps, ALU.mult, ALU.add), act.last())
            act.then(af(st[:, 1:2], st[:, 1:2], ACT.Sqrt), dve.last())
            return dve.then(lambda e: e.reciprocal(st[:, 2:3], st[:, 1:2]), act.last())

        def norm_to_T(src, gname, dst, scratch, *after):
            for b in range(TB):
                s = src[:, b * D:(b + 1) * D]
                xn = scratch[:, b * D:(b + 1) * D]
                inv_rms(s, xn, small[:, 4 * b:4 * b + 4], D, EPS, *after)
                dve.then(ts(xn, s, small[:, 4 * b + 2:4 * b + 3], None, ALU.mult), act.last())
            for k2 in range(KD // 2):
                bk = bank()
                pb = banks[bk]
                tok = tr_group(bk, [(pb[:, (kk * 2 + b) * P:(kk * 2 + b + 1) * P],
                                     scratch[:, b * D + (2 * k2 + kk) * P:b * D + (2 * k2 + kk + 1) * P])
                                    for kk in range(2) for b in range(TB)], dve.last())
                for kk in range(2):
                    k = 2 * k2 + kk
                    dve.run(ts(dst[:, k, :], pb[:, kk * 256:(kk + 1) * 256], V(gname, k, k + 1), None, ALU.mult), tok)
                free[bk] = [dve.last()]
            return dve.last()

        def lin_T(name, src, K, ready, consume, n_tiles):
            per = UNIT // (K * P)
            n = 0
            while n < n_tiles:
                w, landed = take(name)
                wv = w.rearrange("p (n k c) -> p n k c", n=per, k=K)
                for j in range(0, per, 2):
                    bk = bank()
                    pb = banks[bk]
                    items = []
                    for q in range(2):
                        for k in range(K):
                            items.append((pb[:, q * 256:(q + 1) * 256], wv[:, j + q, k, :], src[:, k, :],
                                          k == 0, k == K - 1))
                    tok = mm_group(bk, items, landed, *ready)
                    if j + 2 >= per:
                        release(tok)
                    free[bk] = consume(n, t3(pb[:, :], 2), tok)
                    n += 2

        def lin_A(name, src, K, N, ready, first=0):
            per = UNIT // N
            nh = N // 512
            after = [t for i in range(TB * nh) for t in free[first + i]]
            for k0 in range(0, K, per):
                w, landed = take(name)
                wv = t3(w, per)
                items = []
                for kk in range(per):
                    k = k0 + kk
                    for b in range(TB):
                        for h in range(nh):
                            items.append((banks[first + b * nh + h][:, :], src[:, k, b * P:(b + 1) * P],
                                          wv[:, kk, h * 512:(h + 1) * 512], k == 0, k == K - 1))

                def go(e, items=items):
                    for o, l, r, st, sp_ in items:
                        ins = e.matmul(o, l, r, start=st, stop=sp_, skip_group_check=True)
                    return ins

                tok = pe.run(go, landed, *ready, *after)
                release(tok)
            return tok

        def add_residual(tok, dst, src):
            for b in range(TB):
                for h in range(2):
                    o = b * D + h * 512
                    dve.run(tt(dst[:, o:o + 512], banks[2 * b + h][:, :], src[:, o:o + 512], ALU.add), tok)
                    free[2 * b + h] = [dve.last()]
            return dve.last()

        aqT = t3(view(0, 1280), 5)
        av = view(1280, 256)
        q_s = view(1536, 1024)
        f_s = view(2560, 1024)
        hg_s = view(3584, 1024)
        hi_s = view(4608, 1024)
        yaT = t3(view(5632, 1024), 4)
        yhT = t3(view(6656, 1024), 4)
        scr = view(7680, 2048)
        bias8 = view(9728, 2048)
        S_s = view(11776, 2048)
        S_e = view(13824, 2048)
        pT = view(15872, 3072)
        mrg = t3(view(18944, 2048), 8)
        h_b = view(20992, 1024)
        h_kinv = view(22016, 1024)
        h_kd = view(23040, 1024)
        h_kdn = view(24064, 1024)
        h_AT = view(25088, 1024)
        h_S = view(26112, 4096)
        h_sq = view(30208, 1024)
        sgt = view(31232, 1024)

        dve.wait(loaded)
        act.wait(loaded)
        pe.wait(loaded)
        pool.wait(loaded)

        t_bias = pool.last()
        for h in range(8):
            slope = float(np.float32(2.0 ** (-(h + 1))))
            t_bias = pool.run(ts(bias8[:, h * 256:(h + 1) * 256], C("dist"), -slope, None, ALU.mult))
        for h in range(8):
            t_bias = pool.run(tt(bias8[:, h * 256:(h + 1) * 256], bias8[:, h * 256:(h + 1) * 256], C("wmask"),
                                 ALU.add), t_bias)
        wsT = V("wsT")
        for h in range(4):
            t_ws = pool.run(tt(wsT[:, h * P:(h + 1) * P], wsT[:, h * P:(h + 1) * P], C("causal"), ALU.mult))

        t_h = norm_to_T(xres, "g_mix", hTv, scr)

        lbv = small[:, 16:20]
        omlb = small[:, 20:24]
        l0, l1 = V("lb", 0, 4), V("lb", 4, 8)
        sm = small[:, 24:48]
        dve.then(tt(sm[:, 0:4], l0, l1, ALU.max))
        dve.then(tt(sm[:, 4:8], l0, sm[:, 0:4], ALU.subtract))
        dve.then(tt(sm[:, 8:12], l1, sm[:, 0:4], ALU.subtract))
        act.then(af(sm[:, 12:20], sm[:, 4:12], ACT.Exp), dve.last())
        dve.then(tt(sm[:, 0:4], sm[:, 12:16], sm[:, 16:20], ALU.add), act.last())
        dve.then(lambda e: e.reciprocal(sm[:, 4:8], sm[:, 0:4]))
        dve.then(tt(lbv, sm[:, 12:16], sm[:, 4:8], ALU.mult))
        dve.then(ts(omlb, lbv, -1.0, 1.0, ALU.mult, ALU.add))

        def take_in(n, pb, tok):
            if n < 4:
                act.run(af(aqT[:, n:n + 2, :], pb, ACT.Copy), tok)
                return [act.last()]
            if n < 8:
                act.run(af(t3(q_s, 4)[:, n - 4:n - 2, :], pb, ACT.Silu), tok)
                return [act.last()]
            if n < 12:
                act.run(af(t3(f_s, 4)[:, n - 8:n - 6, :], pb, ACT.Sigmoid), tok)
                return [act.last()]
            act.run(af(t3(hg_s, 4)[:, n - 12:n - 10, :], pb, ACT.Silu), tok)
            return [act.last()]

        lin_T("w_in_t", hTv, KD, [t_h], lambda n, pb, tok: take_in(n, pb, tok), 4)
        w, landed = take("w_in_t")
        wv = w.rearrange("p (n k c) -> p n k c", n=2, k=KD)
        bk = bank()
        pb = banks[bk]
        items = [(pb[:, 0:256], wv[:, 0, k, :], hTv[:, k, :], k == 0, k == KD - 1) for k in range(KD)]
        for b in range(TB):
            items += [(pb[:, 256 + b * P:256 + (b + 1) * P], hTv[:, k, b * P:(b + 1) * P], wv[:, 1, k, :],
                       k == 0, k == KD - 1) for k in range(KD)]
        tok = mm_group(bk, items, landed)
        release(tok)
        act.run(af(aqT[:, 4, :], pb[:, 0:256], ACT.Copy), tok)
        t_kv = act.run(af(av, pb[:, 256:512], ACT.Copy), tok)
        free[bk] = [t_kv]
        lin_T("w_in_t", hTv, KD, [], lambda n, pb, tok: take_in(n + 4, pb, tok), 12)
        t_gates = act.last()
        tok = lin_A("w_in_hi", hTv, KD, 512, [])
        for b in range(TB):
            act.run(af(hi_s[:, b * 512:(b + 1) * 512], banks[b][:, :], ACT.Copy), tok)
            free[b] = [act.last()]
        t_hi = act.last()

        st = small[:, 64:128]

        def attention(blk):
            nk = P * (blk + 1)
            Sv = S_s[:, 0:8 * nk].rearrange("p (h s) -> p h s", h=8)
            Ev = S_e[:, 0:8 * nk].rearrange("p (h s) -> p h s", h=8)
            Bv = t3(bias8, 8)[:, :, 256 - nk:256]
            for h2 in range(4):
                bk = bank()
                pb = t3(banks[bk][:, :], 2)
                items = []
                for q in range(2):
                    h = 2 * h2 + q
                    kv, j = h // 4, h % 4
                    items.append((pb[:, q, 0:nk], aqT[64 * kv:64 * kv + 64, j, blk * P:(blk + 1) * P],
                                  aqT[64 * kv:64 * kv + 64, 4, 0:nk], True, True))
                tok = mm_group(bk, items, t_kv)
                dve.run(stt(Sv[:, 2 * h2:2 * h2 + 2, :], pb[:, :, 0:nk], 0.125, Bv[:, 2 * h2:2 * h2 + 2, :],
                            ALU.mult, ALU.add), tok, t_bias, *( [pe.last()] if blk else []))
                free[bk] = [dve.last()]
            mx, sk, sm_, rc = st[:, 0:8], st[:, 8:16], st[:, 16:24], st[:, 24:32]
            dve.then(lambda e: e.tensor_reduce(mx, Sv, AX, ALU.max))
            dve.then(tt(mx, mx, R("sinks"), ALU.max))
            dve.then(tt(sk, R("sinks"), mx, ALU.subtract))
            dve.then(tt(Sv, Sv, mx.unsqueeze(2).to_broadcast([P, 8, nk]), ALU.subtract))
            act.then(af(Ev, Sv, ACT.Exp), dve.last(), pe.last())
            act.then(af(sk, sk, ACT.Exp), dve.last())
            dve.then(lambda e: e.tensor_reduce(sm_, Ev, AX, ALU.add), act.last())
            dve.then(tt(sm_, sm_, sk, ALU.add))
            dve.then(lambda e: e.reciprocal(rc, sm_))
            dve.then(tt(Ev, Ev, rc.unsqueeze(2).to_broadcast([P, 8, nk]), ALU.mult))
            t_p = dve.last()
            pTv = pT[:, 0:nk * 8].rearrange("p (a h t) -> p a h t", a=blk + 1, h=8)
            for a in range(blk + 1):
                for h4 in range(2):
                    bk = bank()
                    pb = banks[bk]
                    tok = tr_group(bk, [(pb[:, q * P:(q + 1) * P], Ev[:, 4 * h4 + q, a * P:(a + 1) * P])
                                        for q in range(4)], t_p)
                    act.then(af(pTv[:, a, 4 * h4:4 * h4 + 4, :], t3(pb[:, :], 4), ACT.Copy), tok)
                    free[bk] = [act.last()]
            bk = bank()
            pb = banks[bk]
            items = []
            for h in range(8):
                kv, j = h // 4, h % 4
                for a in range(blk + 1):
                    items.append((pb[64 * kv:64 * kv + 64, j * P:(j + 1) * P],
                                  av[:, a * P + 64 * kv:a * P + 64 * kv + 64], pTv[:, a, h, :], a == 0, a == blk))
            tok = mm_group(bk, items, act.last())
            dve.then(cp(yaT[:, :, blk * P:(blk + 1) * P], t3(pb[:, :], 4)), tok)
            free[bk] = [dve.last()]
            return dve.last()

        attention(0)
        t_ya = attention(1)

        f4 = t3(f_s, 4)
        for h in range(4):
            dve.then(ts(f4[:, h, :], f4[:, h, :], omlb[:, h:h + 1], lbv[:, h:h + 1], ALU.mult, ALU.add), t_gates)
        act.then(af(scr[:, 0:1024], f_s, ACT.Ln), dve.last())
        dve.then(ts(f_s, f_s, -1.0, 1.0, ALU.mult, ALU.add), act.last())
        dve.then(lambda e: e.tensor_tensor_scan(h_b, C("reset"), scr[:, 0:1024], 0.0, ALU.mult, ALU.add), act.last())
        bl = h_b.rearrange("p (n c) -> p n c", c=32)[:, :, 31:32]
        act.then(af(scr[:, 0:1024], h_b, ACT.Exp), dve.last())
        act.then(af(h_kinv, h_b, ACT.Exp, scale=-1.0))
        dve.then(tt(q_s, q_s, scr[:, 0:1024], ALU.mult), act.last())
        dve.then(tt(h_kinv, h_kinv, f_s, ALU.mult))
        dve.then(tt(h_kd.rearrange("p (n c) -> p n c", c=32), bl.to_broadcast([P, 32, 32]),
                    h_b.rearrange("p (n c) -> p n c", c=32), ALU.subtract))
        act.then(af(h_kd, h_kd, ACT.Exp), dve.last())
        decay = small[:, 128:160]
        act.then(af(decay.unsqueeze(2), bl, ACT.Exp))
        dve.then(tt(h_kd, h_kd, f_s, ALU.mult), act.last())
        t_kd = dve.last()
        t_hz = dve.run(lambda e: e.memset(h_AT, 0.0))
        kdT = h_kdn.rearrange("p (b h d) -> p b h d", b=2, h=4)
        for b in range(TB):
            bk = bank()
            pb = banks[bk]
            tok = tr_group(bk, [(pb[:, h * P:(h + 1) * P], h_kd[:, h * T + b * P:h * T + (b + 1) * P])
                                for h in range(4)], t_kd)
            act.then(af(kdT[:, b], t3(pb[:, :], 4), ACT.Copy), tok)
            free[bk] = [act.last()]
        t_kdn = act.last()
        AT = h_AT.rearrange("p (b h t) -> p b h t", b=2, h=4)
        for b in range(TB):
            bk = bank()
            pb = banks[bk]
            tok = mm_group(bk, [(pb[:, h * P:(h + 1) * P], h_kinv[:, h * T + b * P:h * T + (b + 1) * P],
                                 q_s[:, h * T + b * P:h * T + (b + 1) * P], True, True) for h in range(4)], t_kd)
            dve.then(lambda e, b=b, pb=pb: e.copy_predicated(
                AT[:, b], C("hmask").bitcast(I32).unsqueeze(1).to_broadcast([P, 4, P]), t3(pb[:, :], 4)), tok)
            free[bk] = [dve.last()]
        t_AT = dve.last()
        Sv = h_S.rearrange("p (h n v) -> p h n v", h=4, n=8)
        hiv = hi_s.rearrange("p (b h v) -> p b h v", b=2, h=4)
        kdc = view(30208, 1024)
        for n in range(7):
            b, r = n // 4, 32 * (n % 4)
            bk = bank()
            pb = banks[bk]
            tok = mm_group(bk, [(pb[:, h * P:(h + 1) * P], kdT[r:r + 32, b, h, :], hiv[r:r + 32, b, h, :], True, True)
                                for h in range(4)], t_kdn, t_hi)
            for h in range(4):
                if n == 0:
                    ins = cp(Sv[:, h, 1, :], pb[:, h * P:(h + 1) * P])
                else:
                    ins = stt(Sv[:, h, n + 1, :], Sv[:, h, n, :], decay[:, h * 8 + n:h * 8 + n + 1],
                              pb[:, h * P:(h + 1) * P], ALU.mult, ALU.add)
                dve.run(ins, tok, t_state if n else tok)
            t_state = dve.last()
            free[bk] = [t_state]
        yo = scr[:, 0:1024]
        for h in range(4):
            bk = bank()
            pb = banks[bk]
            items = []
            for b in range(TB):
                items.append((pb[:, b * P:(b + 1) * P], hiv[:, b, h, :], AT[:, b, h, :], b == 0, False))
            for n in range(1, 8):
                items.append((pb[:, n * 32:(n + 1) * 32], Sv[:, h, n, :], q_s[:, h * T + n * 32:h * T + n * 32 + 32],
                              False, n == 7))
            tok = mm_group(bk, items, t_AT, t_state)
            dve.then(cp(yo[:, h * T:(h + 1) * T], pb[:, 0:256]), tok)
            free[bk] = [dve.last()]
        act.then(af(h_sq, yo, ACT.Square), dve.last())
        for h2 in range(2):
            bk = bank()
            pb = banks[bk]
            tok = mm_group(bk, [(pb[:, :], C("mean128"), h_sq[:, h2 * 512:(h2 + 1) * 512], True, True)], act.last())
            dve.then(ts(h_b[:, h2 * 512:(h2 + 1) * 512], pb[:, :], EPS, None, ALU.add), tok)
            free[bk] = [dve.last()]
        act.then(af(h_b, h_b, ACT.Sqrt), dve.last())
        dve.then(lambda e: e.reciprocal(h_b, h_b), act.last())
        dve.then(tt(yo, yo, h_b, ALU.mult))
        dve.then(stt(yhT.rearrange("p a b -> p (a b)"), yo, V("g_hgrn"), hg_s, ALU.mult, ALU.mult))
        t_yh = dve.last()

        gate = t3(view(9728, 4096), 16)

        def take_gate(n, pb, tok):
            act.run(af(gate[:, n:n + 2, :], pb, ACT.Sigmoid), tok, t_ya)
            return [act.last()]

        lin_T("w_in_g", hTv, KD, [], take_gate, 16)

        def merge_a(n, pb, tok):
            dve.run(tt(mrg[:, n:n + 2, :], gate[:, n:n + 2, :], pb, ALU.mult), tok, act.last())
            return [dve.last()]

        def merge_h(n, pb, tok):
            dve.run(tt(gate[:, 8 + n:10 + n, :], gate[:, 8 + n:10 + n, :], pb, ALU.mult), tok)
            bf = dve.last()
            dve.then(tt(mrg[:, n:n + 2, :], mrg[:, n:n + 2, :], gate[:, 8 + n:10 + n, :], ALU.add))
            return [bf]

        lin_T("w_ap", yaT, 4, [t_ya], merge_a, 8)
        lin_T("w_hp", yhT, 4, [t_yh], merge_h, 8)
        tok = lin_A("w_out", mrg, KD, D, [dve.last()])
        t_x = add_residual(tok, xres, xres)

        t_h = norm_to_T(xres, "g_ffn", hTv, scr, t_x)
        qT = t3(view(12288, 4096), 16)
        sc = view(16384, 2048)
        scw = view(18432, 2048)
        cand = view(20480, 2048)
        candw = view(22528, 2048)
        oh = view(24576, 2048)
        oh2 = view(26624, 2048)
        val = view(28672, 512)
        idx = view(29184, 512)
        idxf = view(29696, 512)
        best = view(30208, 256)
        posu = view(30464, 512)
        posf = view(30976, 512)
        iT = sb("iT", 3 * T)
        before_peer = all_done()

        def take_q(n, pb, tok):
            act.run(af(qT[:, n:n + 2, :], pb, ACT.Copy), tok, *before_peer)
            return [act.last()]

        lin_T("w_pq", hTv, KD, [t_h], take_q, 16)
        t_q = act.last()
        keys, landed = take("keys")
        sc_store = [sc, view(8192, 2048)]
        for b in range(TB):
            for g in range(4):
                bk = bank()
                pb = banks[bk]
                tok = mm_group(bk, [(pb[:, q * P:(q + 1) * P], qT[:, 4 * g + q, b * P:(b + 1) * P],
                                     keys[:, (4 * g + q) * P:(4 * g + q + 1) * P], True, True) for q in range(4)],
                               landed, t_q)
                act.run(af(sc_store[b][:, g * 512:(g + 1) * 512], pb[:, :], ACT.Copy), tok, *before_peer)
                free[bk] = [act.last()]
        release(tok)
        t_sc = act.last()
        dve.wait(*before_peer)

        for b in range(TB):
            scb = t3(sc_store[b], 16)
            scwv = t3(scw, 16)
            v3 = t3(val[:, 0:256], 16)
            i3 = t3(idx[:, 0:256], 16).bitcast(U32)

            def top16(src, work, vals, idxs, n, *after):
                for j in range(n):
                    dve.run(lambda e, j=j: e.max(vals[:, j, 0:8], src[:, j, :]), dve.last() if not j else after[0],
                            *after)
                t = dve.last()
                for j in range(n):
                    dve.run(lambda e, j=j: e.match_replace(work[:, j, :], vals[:, j, 0:8], src[:, j, :], -3e38), t)
                t = dve.last()
                for j in range(n):
                    dve.run(lambda e, j=j: e.max(vals[:, j, 8:16], work[:, j, :]), t)
                t = dve.last()
                for j in range(n):
                    dve.run(lambda e, j=j: e.max_index(idxs[:, j, 0:8], vals[:, j, 0:8], src[:, j, :]), t)
                    dve.run(lambda e, j=j: e.max_index(idxs[:, j, 8:16], vals[:, j, 8:16], work[:, j, :]), t)
                return dve.last()

            top16(scb, scwv, v3, i3, 16, t_sc)
            dve.then(cp(idxf[:, 0:256], idx[:, 0:256].bitcast(U32)))
            vv = val[:, 0:256].rearrange("p (h q a) -> p h q a", h=8, q=2)
            iv = idxf[:, 0:256].rearrange("p (h q a) -> p h q a", h=8, q=2)
            shape = [P, 8, 16, 16]
            c4 = t4(cand, 8, 16)
            dve.then(tt(c4, vv[:, :, 0, :].unsqueeze(3).to_broadcast(shape),
                        vv[:, :, 1, :].unsqueeze(2).to_broadcast(shape), ALU.add))
            bv = t3(best[:, 0:128], 8)
            pu = t3(posu[:, 0:128], 8).bitcast(U32)
            top16(t3(cand, 8), t3(candw, 8), bv, pu, 8, dve.last())
            pall = posu[:, 0:128].bitcast(U32)
            dve.then(lambda e: e.tensor_scalar(posu[:, 128:256].bitcast(U32), pall, 4, None, ALU.logical_shift_right))
            dve.then(lambda e: e.tensor_scalar(posu[:, 256:384].bitcast(U32), pall, 15, None, ALU.bitwise_and))
            dve.then(cp(posf[:, 0:256], posu[:, 128:384].bitcast(U32)))
            sel_i = [scw[:, 0:128], scw[:, 128:256]]
            for q in range(2):
                ps = t3(posf[:, q * P:(q + 1) * P], 8)
                o4 = t4(oh, 8, 16)
                dve.then(tt(o4, ps.unsqueeze(3).to_broadcast(shape),
                            C("iota16").unsqueeze(1).unsqueeze(1).to_broadcast(shape), ALU.is_equal))
                dve.then(tt(t4(oh2, 8, 16), o4, iv[:, :, q, :].unsqueeze(2).to_broadcast(shape), ALU.mult))
                dve.then(lambda e, q=q: e.tensor_reduce(t3(sel_i[q], 8), t4(oh2, 8, 16), AX, ALU.add))
            bex = scw[:, 256:384]
            dve.then(tt(t3(bex, 8), bv, bv[:, :, 0:1].to_broadcast([P, 8, 16]), ALU.subtract))
            act.then(af(bex, bex, ACT.Exp), dve.last())
            dve.then(lambda e: e.tensor_reduce(scw[:, 384:392], t3(bex, 8), AX, ALU.add), act.last())
            dve.then(lambda e: e.reciprocal(scw[:, 392:400], scw[:, 384:392]))
            dve.then(tt(t3(bex, 8), t3(bex, 8), scw[:, 392:400].unsqueeze(2).to_broadcast([P, 8, 16]), ALU.mult))
            bk = bank()
            pb = banks[bk]
            tok = tr_group(bk, [(pb[:, q * P:(q + 1) * P], s) for q, s in enumerate([sel_i[0], sel_i[1], bex])],
                           dve.last())
            dve.then(cp(t3(iT[:, :], 3)[:, :, b * P:(b + 1) * P], t3(pb[:, 0:384], 3)), tok)
            free[bk] = [dve.last()]
        t_route = dve.last()

        acts = t3(arena[:, :], P)
        for i in range(64):
            w, landed = take("u")
            wv = w.rearrange("p (n k c) -> p n k c", n=2, k=KD)
            bk = bank()
            pb = banks[bk]
            items = []
            for q in range(2):
                for k in range(KD):
                    items.append((pb[:, q * 256:(q + 1) * 256], wv[:, q, k, :], hTv[:, k, :], k == 0, k == KD - 1))
            tok = mm_group(bk, items, landed)
            release(tok)
            waits = []
            if 512 * (i + 1) > 8192:
                waits = [t_route, t_sc]
            act.run(af(acts[:, 2 * i:2 * i + 2, :], t3(pb[:, :], 2), ACT.Gelu), tok, *before_peer, *waits)
            free[bk] = [act.last()]
        t_acts = act.last()

        OB = 4
        oh1 = sb("oh1", 2 * OB * P)
        og = sb("og", 2 * OB * P)
        used = [t_acts, t_acts]
        for g in range(T // OB):
            s = (g % 2) * OB * P
            for q in range(OB):
                t = g * OB + q
                pool.run(ts(oh1[:, s + q * P:s + (q + 1) * P], C("iota"), iT[:, t:t + 1], None, ALU.is_equal),
                         t_route, used[g % 2])
                dve.run(ts(og[:, s + q * P:s + (q + 1) * P], C("iota"), iT[:, T + t:T + t + 1],
                           iT[:, 2 * T + t:2 * T + t + 1], ALU.is_equal, ALU.mult), t_route, used[g % 2])
            bk = bank()
            pb = banks[bk]
            tok = mm_group(bk, [(pb[:, q * P:(q + 1) * P], oh1[:, s + q * P:s + (q + 1) * P],
                                 og[:, s + q * P:s + (q + 1) * P], True, True) for q in range(OB)],
                           pool.last(), dve.last())
            used[g % 2] = tok
            av_ = acts[:, :, g * OB:(g + 1) * OB].rearrange("p i t -> p t i")
            dve.run(tt(av_, av_, t3(pb[:, :], OB), ALU.mult), tok, t_acts)
            free[bk] = [dve.last()]
        t_g = dve.last()
        after = [t for i in range(4) for t in free[i]]
        for i in range(64):
            w, landed = take("v")
            wv = t3(w, 2)
            items = []
            for q in range(2):
                n = 2 * i + q
                for b in range(TB):
                    for h in range(2):
                        items.append((banks[2 * b + h][:, :], acts[:, n, b * P:(b + 1) * P],
                                      wv[:, q, h * 512:(h + 1) * 512], n == 0, n == 127))

            def go(e, items=items):
                for o, l, r, st_, sp_ in items:
                    ins = e.matmul(o, l, r, start=st_, stop=sp_, skip_group_check=True)
                return ins

            tok = pe.run(go, landed, t_g, *after)
            release(tok)
        t_x = add_residual(tok, xres, xres)

        def final_norm(gname, scratch):
            for b in range(TB):
                s = xres[:, b * D:(b + 1) * D]
                s_ = small[:, 4 * b:4 * b + 4]
                inv_rms(s, scratch[:, b * D:(b + 1) * D], s_, D, EPS, dve.last(), pe.last())
                dve.then(ts(s, s, s_[:, 2:3], None, ALU.mult))
                dve.then(tt(s, s, R(gname), ALU.mult))
            return dve.last()

        t_x = final_norm("g_final", scr)

        uT = t3(view(0, 512), 2)
        aT = t3(view(512, 512), 2)
        gT = t3(view(1024, 512), 2)
        xcT = t3(view(1536, 1024), 4)
        ocT = t3(view(2560, 1024), 4)
        vg = view(3584, 512)
        xcv = t3(view(4608, 1024), 4)
        yT = t3(view(5632, 2048), 8)
        tmp = view(9728, 4096)
        qTm = t3(view(13824, 1024), 4)
        kTm = t3(view(14848, 1024), 4)
        vnm = view(15872, 1024)
        knm = view(16896, 512)
        rows = view(17408, 4096)
        wTm = view(21504, 1024)
        cm = view(22528, 2048)
        hm = view(24576, 1024)
        hm2 = view(25600, 1024)
        conv_o = view(26624, 512)
        conv_p = view(27136, 512)
        kmT = t3(view(0, 2048), 8)

        t_h = norm_to_T(xres, "g_mix2", hTv, scr, t_x)
        before2 = all_done()
        act.wait(*before2)
        dve.wait(*before2)
        pool.wait(*before2)

        def take2(n, pb, tok):
            if n < 2:
                act.run(af(uT, pb, ACT.Gelu), tok)
            elif n < 4:
                act.run(af(aT, pb, ACT.Copy), tok)
            elif n < 6:
                act.run(af(gT, pb, ACT.Sigmoid), tok)
            elif n < 10:
                act.run(af(xcT[:, n - 6:n - 4, :], pb, ACT.Copy), tok)
            else:
                act.run(af(ocT[:, n - 10:n - 8, :], pb, ACT.Sigmoid), tok)
            return [act.last()]

        lin_T("w2_t", hTv, KD, [t_h], take2, 14)
        t_z = act.last()
        w, landed = take("w2_v")
        wv = t3(w, KD)
        bk = bank()
        pb = banks[bk]
        tok = mm_group(bk, [(pb[:, b * 256:(b + 1) * 256], hTv[:, k, b * P:(b + 1) * P], wv[:, k, :],
                             k == 0, k == KD - 1) for b in range(TB) for k in range(KD)], landed)
        release(tok)
        act.run(af(vg, pb[:, :], ACT.Gelu), tok)
        t_vg = act.last()
        free[bk] = [t_vg]
        wg = t3(V("wgate"), KD)
        bk = bank()
        pbg = banks[bk]
        tok_g = mm_group(bk, [(pbg[0:4, q * 256:(q + 1) * 256], wg[:, k, 4 * q:4 * q + 4], hTv[:, k, :],
                               k == 0, k == KD - 1) for q in range(2) for k in range(KD)])

        def row_(i, n=T):
            return rows[0:4, i * T:i * T + n]

        li, lf, bc, Rr, pm, mm_, emm, t0, t1 = (row_(i) for i in range(9))
        dve.then(ts(li, pbg[0:4, 0:256], V("bi")[0:4, :], None, ALU.add), tok_g)
        dve.then(ts(t0, pbg[0:4, 256:512], V("bf")[0:4, :], None, ALU.add))
        free[bk] = [dve.last()]
        dve.then(ts(lf, t0, 0.0, None, ALU.min))
        dve.then(ts(t1, t0, 0.0, None, ALU.max))
        dve.then(tt(t1, lf, t1, ALU.subtract))
        act.then(af(t1, t1, ACT.Exp), dve.last())
        dve.then(ts(t1, t1, 1.0, None, ALU.add), act.last())
        act.then(af(t1, t1, ACT.Ln), dve.last())
        dve.then(tt(lf, lf, t1, ALU.subtract), act.last())
        one_row = C("ones")[0:4, :]
        for c in range(2):
            s = slice(c * P, (c + 1) * P)
            dve.then(lambda e, s=s: e.tensor_tensor_scan(bc[:, s], one_row, lf[:, s], 0.0, ALU.mult, ALU.add))
        dve.then(tt(Rr, li, bc, ALU.subtract))
        for c in range(2):
            s = slice(c * P, (c + 1) * P)
            init = 0.0 if c == 0 else mm_[:, P - 1:P]
            dve.then(lambda e, s=s, init=init: e.tensor_tensor_scan(pm[:, s], one_row, Rr[:, s], init,
                                                                    ALU.mult, ALU.max))
            dve.then(tt(mm_[:, s], bc[:, s], pm[:, s], ALU.add))
        act.then(af(emm, mm_, ACT.Exp, scale=-1.0), dve.last())
        dve.then(ts(t0[:, P:T], pm[:, P:T], -1.0, mm_[:, P - 1:P], ALU.mult, ALU.add))
        act.then(af(t0[:, P:T], t0[:, P:T], ACT.Exp), dve.last())
        t_rows = act.last()
        bk = bank()
        pb = banks[bk]
        tok = tr_group(bk, [(pb[:, c * 4:c * 4 + 4], Rr[:, c * P:(c + 1) * P]) for c in range(2)], t_rows, dve.last())
        Rc = small[:, 160:168]
        dve.then(cp(Rc, pb[:, 0:8]), tok)
        free[bk] = [dve.last()]

        def conv(eng, dst, src, w, taps):
            eng.then(ts(dst, src, w(taps - 1), None, ALU.mult))
            for j in range(taps - 1):
                sft = taps - 1 - j
                eng.then(stt(dst[:, sft:T], src[:, 0:T - sft], w(j), dst[:, sft:T], ALU.mult, ALU.add))

        dve.wait(t_z)
        for j in range(4):
            conv(dve, hm[:, j * T:(j + 1) * T], xcT[:, j, :], lambda i, j=j: V("ccw", 4 * j + i, 4 * j + i + 1), 4)
            act.then(af(xcv[:, j, :], hm[:, j * T:(j + 1) * T], ACT.Silu, bias=V("ccb", j, j + 1)), dve.last())
        t_xc = act.last()

        dve.then(tt(aT, aT, gT, ALU.mult))
        for j in range(2):
            conv(dve, conv_o[:, j * T:(j + 1) * T], aT[:, j, :], lambda i, j=j: V("cbw", 31 * j + i, 31 * j + i + 1), 31)
            dve.then(ts(conv_o[:, j * T:(j + 1) * T], conv_o[:, j * T:(j + 1) * T], V("cbb", j, j + 1), None, ALU.add))

        def standardise_T(src, n, meanmat, eps, out_, sq):
            bk = bank()
            pb = banks[bk]
            tok = mm_group(bk, [(pb[:, 0:n], meanmat, src, True, True)], dve.last())
            dve.then(tt(out_, src, pb[:, 0:n], ALU.subtract), tok)
            free[bk] = [dve.last()]
            act.then(af(sq, out_, ACT.Square), dve.last())
            bk = bank()
            pb = banks[bk]
            tok = mm_group(bk, [(pb[:, 0:n], meanmat, sq, True, True)], act.last())
            dve.then(ts(sq, pb[:, 0:n], eps, None, ALU.add), tok)
            free[bk] = [dve.last()]
            act.then(af(sq, sq, ACT.Sqrt), dve.last())
            dve.then(lambda e: e.reciprocal(sq, sq), act.last())
            dve.then(tt(out_, out_, sq, ALU.mult))
            return dve.last()

        standardise_T(conv_o, 512, C("mean64"), LN_EPS, conv_o, conv_p)
        for j in range(2):
            act.then(af(yT[:, 2 + j, :], conv_o[:, j * T:(j + 1) * T], ACT.Silu, bias=V("gnb", j, j + 1),
                        scale=V("gng", j, j + 1)), dve.last())

        stg = small[:, 176:208]
        for b in range(TB):
            s = vg[:, b * 256:(b + 1) * 256]
            o = stg[:, 16 * b:16 * b + 16]
            dve.then(lambda e, s=s, o=o: e.bn_stats(o[:, 0:6], s), t_vg)
            dve.then(lambda e, o=o: e.bn_aggr(o[:, 6:8], o[:, 0:6]))
            dve.then(ts(o[:, 8:9], o[:, 7:8], LN_EPS, None, ALU.add))
            act.then(af(o[:, 8:9], o[:, 8:9], ACT.Sqrt), dve.last())
            dve.then(lambda e, o=o: e.reciprocal(o[:, 9:10], o[:, 8:9]), act.last())
            dve.then(ts(s, s, o[:, 6:7], o[:, 9:10], ALU.subtract, ALU.mult))
            dve.then(tt(s, s, R("lng"), ALU.mult))
            dve.then(tt(s, s, R("lnb"), ALU.add))
        bk = bank()
        pb = banks[bk]
        items = []
        for h in range(4):
            for b in range(TB):
                o = (h // 2) * 256 + b * P
                items.append((pb[64 * (h % 2):64 * (h % 2) + 64, o:o + P], vg[:, b * 256 + h * 64:b * 256 + h * 64 + 64],
                              wsT[:, h * P:(h + 1) * P], True, True))
        tok = mm_group(bk, items, dve.last(), t_ws)
        bsv = t3(V("bs"), 2)
        for b in range(TB):
            dve.then(tt(yT[:, 0:2, b * P:(b + 1) * P], t3(pb[:, :], 2)[:, :, b * P:(b + 1) * P], bsv, ALU.add), tok)
        free[bk] = [dve.last()]
        dve.then(tt(yT[:, 0:2, :], yT[:, 0:2, :], uT, ALU.mult), t_z)

        w, landed = take("w2_c")
        wc = w.rearrange("p (q h e) -> p q h e", q=3, h=4)
        for q, (dst, src) in enumerate([(qTm, xcv), (kTm, xcv)]):
            for j in range(2):
                bk = bank()
                pb = banks[bk]
                tok = mm_group(bk, [(pb[:, i * 256:(i + 1) * 256], wc[:, q, 2 * j + i, :], src[:, 2 * j + i, :],
                                     True, True) for i in range(2)], landed, t_xc)
                act.run(af(dst[:, 2 * j:2 * j + 2, :], t3(pb[:, :], 2), ACT.Copy,
                           scale=float(np.float32(P ** -0.5)) if q == 0 else 1.0), tok)
                free[bk] = [act.last()]
        for b in range(TB):
            bk = bank()
            pb = banks[bk]
            tok = mm_group(bk, [(pb[:, h * P:(h + 1) * P], xcT[:, h, b * P:(b + 1) * P], wc[:, 2, h, :], True, True)
                                for h in range(4)], t_xc)
            act.run(af(vnm[:, b * 512:(b + 1) * 512], pb[:, :], ACT.Copy), tok)
            free[bk] = [act.last()]
        bk = bank()
        pb = banks[bk]
        tok = mm_group(bk, [(pb[:, h * P:(h + 1) * P], xcv[:, h, 0:P], wc[:, 1, h, :], True, True) for h in range(4)])
        release(tok)
        act.run(af(knm, pb[:, :], ACT.Copy), tok)
        free[bk] = [act.last()]
        t_qkv = act.last()

        for h in range(4):
            selh = C("sel", h * P, (h + 1) * P)[0:4, :]
            bk = bank()
            pb = banks[bk]
            tok = mm_group(bk, [(pb[:, 0:256], selh, pm, True, True), (pb[:, 256:384], selh, t0[:, P:T], True, True)],
                           t_rows)
            wt = wTm[:, 0:256]
            for c in range(2):
                s = slice(c * P, (c + 1) * P)
                dve.then(ts(wt[:, s], pb[:, s], Rc[:, 4 * c + h:4 * c + h + 1], None, ALU.subtract), tok, pe.last())
            winter = wTm[:, 256:384]
            dve.then(cp(winter, pb[:, 256:384]))
            free[bk] = [dve.last()]
            dve.then(ts(wt, wt, 0.0, None, ALU.max))
            act.then(af(wt, wt, ACT.Exp, scale=-1.0), dve.last())
            for c in range(2):
                s = slice(c * P, (c + 1) * P)
                dve.then(tt(wt[:, s], wt[:, s], C("causal"), ALU.mult), act.last())
            ksc = cm[:, 0:128]
            dve.then(ts(ksc, knm[:, h * P:(h + 1) * P], wt[:, P - 1:P], None, ALU.mult), t_qkv, pe.last())
            qw = cm[:, 128:256]
            dve.then(tt(qw, qTm[:, h, P:T], winter, ALU.mult))
            bk = bank()
            pb = banks[bk]
            tok = mm_group(bk, [(pb[:, 0:P], ksc, vnm[:, h * P:(h + 1) * P], True, True),
                                (pb[:, P:2 * P], ksc, C("ones"), True, True)], dve.last())
            cn = cm[:, 256:512]
            dve.then(cp(cn, pb[:, 0:256]), tok)
            free[bk] = [dve.last()]
            bk = bank()
            pb = banks[bk]
            tok = mm_group(bk, [(pb[:, c * P:(c + 1) * P], kTm[:, h, c * P:(c + 1) * P], qTm[:, h, c * P:(c + 1) * P],
                                 True, True) for c in range(2)])
            dve.then(tt(wt, wt, pb[:, 0:256], ALU.mult), tok)
            free[bk] = [dve.last()]
            bk = bank()
            pb = banks[bk]
            items = []
            for c in range(2):
                s = slice(c * P, (c + 1) * P)
                s2 = slice(256 + c * P, 256 + (c + 1) * P)
                items.append((pb[:, s], vnm[:, c * 512 + h * P:c * 512 + (h + 1) * P], wt[:, s], True, c == 0))
                if c:
                    items.append((pb[:, s], cn[:, 0:P], qw, False, True))
                items.append((pb[:, s2], C("ones"), wt[:, s], True, c == 0))
                if c:
                    items.append((pb[:, s2], cn[:, P:2 * P], qw, False, True))
            tok = mm_group(bk, items, dve.last())
            bk2 = bank()
            pb2 = banks[bk2]
            tok2 = mm_group(bk2, [(pb2[:, 0:256], selh, emm, True, True)])
            den = tmp[:, 0:256]
            dve.then(ts(den, pb[:, 256:512], -1.0, None, ALU.mult), tok)
            dve.then(tt(den, den, pb[:, 256:512], ALU.max))
            dve.then(tt(den, den, pb2[:, 0:256], ALU.max), tok2)
            free[bk2] = [dve.last()]
            dve.then(lambda e: e.reciprocal(den, den))
            dve.then(tt(hm[:, h * T:(h + 1) * T], pb[:, 0:256], den, ALU.mult))
            free[bk] = [dve.last()]
        for j in range(2):
            standardise_T(hm[:, j * 512:(j + 1) * 512], 512, C("mean128"), LN_EPS, hm[:, j * 512:(j + 1) * 512],
                          hm2[:, j * 512:(j + 1) * 512])
        for h in range(4):
            o = hm[:, h * T:(h + 1) * T]
            o2 = hm2[:, h * T:(h + 1) * T]
            dve.then(ts(o2, xcv[:, h, :], V("skip", h, h + 1), None, ALU.mult))
            dve.then(stt(o2, o, V("hng", h, h + 1), o2, ALU.mult, ALU.add))
            dve.then(tt(yT[:, 4 + h, :], o2, ocT[:, h, :], ALU.mult))
        tok = lin_A("w2_out", yT, KD, D, [dve.last(), act.last()])
        t_x = add_residual(tok, xres, xres)

        memx = view(16384, 2048)
        mT = t3(view(18432, 2048), 8)
        mscr = view(20480, 2048)
        done = all_done()
        sp.wait(*done)
        for b in range(TB):
            sp.work.append(lambda e, b=b: e.dma_start(memx[:, b * D:(b + 1) * D],
                                                      mem[b * P:(b + 1) * P, :]).then_inc(s_mem, 16))
        xs = view(9728, 2048)
        t_mT = norm_to_T(memx, "g_mem2", mT, mscr, (s_mem, 32), *done)
        t_h = norm_to_T(xres, "g_x2", hTv, xs, t_x)
        kT2 = t3(view(0, 2048), 8)
        v2 = view(2048, 2048)
        qT2 = t3(view(4096, 2048), 8)
        p2 = view(6144, 1024)
        pT2 = view(7168, 2048)
        oT2 = t3(view(12288, 2048), 8)

        def to(dst):
            def f(n, pb, tok):
                act.run(af(dst[:, n:n + 2, :], pb, ACT.Copy), tok, *done)
                return [act.last()]
            return f

        lin_T("w_xk", mT, KD, [t_mT], to(kT2), 8)
        tok = lin_A("w_xv", mT, KD, D, [])
        for b in range(TB):
            for h in range(2):
                act.run(af(v2[:, b * D + h * 512:b * D + (h + 1) * 512], banks[2 * b + h][:, :], ACT.Copy), tok)
                free[2 * b + h] = [act.last()]
        lin_T("w_xq", hTv, KD, [t_h], to(qT2), 8)
        t_kvq = act.last()
        sx = small[:, 224:256]
        t_pT = pe.last()
        for b in range(TB):
            Pv = t3(p2, 4)
            for h2 in range(2):
                bk = bank()
                pb = banks[bk]
                tok = mm_group(bk, [(pb[:, q * 256:(q + 1) * 256], qT2[:, 2 * (2 * h2 + q) + k, b * P:(b + 1) * P],
                                     kT2[:, 2 * (2 * h2 + q) + k, :], k == 0, k == 1)
                                    for q in range(2) for k in range(2)], t_kvq)
                dve.then(ts(Pv[:, 2 * h2:2 * h2 + 2, :], t3(pb[:, :], 2), 1.0 / 16.0, None, ALU.mult), tok, t_pT)
                free[bk] = [dve.last()]
            mx, sm_, rc = sx[:, 0:4], sx[:, 4:8], sx[:, 8:12]
            dve.then(lambda e, Pv=Pv: e.tensor_reduce(mx, Pv, AX, ALU.max))
            dve.then(tt(Pv, Pv, mx.unsqueeze(2).to_broadcast([P, 4, 256]), ALU.subtract))
            act.then(af(p2, p2, ACT.Exp), dve.last())
            dve.then(lambda e, Pv=Pv: e.tensor_reduce(sm_, Pv, AX, ALU.add), act.last())
            dve.then(lambda e: e.reciprocal(rc, sm_))
            dve.then(tt(Pv, Pv, rc.unsqueeze(2).to_broadcast([P, 4, 256]), ALU.mult))
            pTv = pT2.rearrange("p (a h t) -> p a h t", a=2, h=4)
            for a in range(2):
                bk = bank()
                pb = banks[bk]
                t_pT = tr_group(bk, [(pb[:, h * P:(h + 1) * P], Pv[:, h, a * P:(a + 1) * P]) for h in range(4)],
                                dve.last())
                act.then(af(pTv[:, a, :, b * P:(b + 1) * P], t3(pb[:, :], 4), ACT.Copy), t_pT)
                free[bk] = [act.last()]
        return_ = None
        t_p = act.last()
        for h in range(4):
            bk = bank()
            pb = banks[bk]
            tok = mm_group(bk, [(pb[:, j * 256:(j + 1) * 256],
                                 v2[:, a * D + (2 * h + j) * P:a * D + (2 * h + j + 1) * P],
                                 pTv[:, a, h, :], a == 0, a == 1) for j in range(2) for a in range(2)], t_p)
            dve.then(cp(oT2[:, 2 * h:2 * h + 2, :], t3(pb[:, :], 2)), tok)
            free[bk] = [dve.last()]
        tok = lin_A("w_xo", oT2, KD, D, [dve.last()])
        t_x = add_residual(tok, xres, xres)

        t_h = norm_to_T(xres, "g_ffn2", hTv, xs, t_x)
        done = all_done()
        act.wait(*done)
        dve.wait(*done)
        aF = t3(view(0, 22 * T), 22)
        gF = view(16384, 4 * T)
        cF = view(17408, 4 * T)

        def ffn(n, pb, tok):
            j = n // 2
            s = (j % 4) * T
            g, c = gF[:, s:s + T], cF[:, s:s + T]
            act.then(af(g, pb[:, 0, :], ACT.Copy), tok, *([t_ffn[j - 4]] if j >= 4 else []))
            dve.wait(act.last())
            conv(dve, c, g, lambda i: V("cfw", 3 * j + i, 3 * j + i + 1), 3)
            act.then(af(g, c, ACT.Gelu, bias=V("cfb", j, j + 1)), dve.last())
            dve.then(tt(aF[:, j, :], g, pb[:, 1, :], ALU.mult), act.last())
            t_ffn.append(dve.last())
            return [dve.last()]

        t_ffn = []
        lin_T("w_up", hTv, KD, [t_h], ffn, 44)
        tok = lin_A("w_down", aF, 22, D, [dve.last()])
        add_residual(tok, xres, xres)
        t_x = final_norm("g_final2", xs)
        sp.wait(t_x)
        for b in range(TB):
            sp.work.append(lambda e, b=b: e.dma_start(out[b * P:(b + 1) * P, :],
                                                      xres[:, b * D:(b + 1) * D]).then_inc(s_out, 16))
        sp.work.append(lambda e: e.wait_ge(s_out, 32))
        assert taken[0] == len(units)

        block = ctx.enter_context(nc.Block())

        @block.sync
        def _(e):
            sp.emit(e)

        @block.tensor
        def _(e):
            pe.emit(e)

        @block.vector
        def _(e):
            dve.emit(e)

        @block.scalar
        def _(e):
            act.emit(e)

        @block.gpsimd
        def _(e):
            pool.emit(e)


def constants():
    c = np.zeros((P, NC), np.float32)

    def put(name, a):
        o, n = COFF[name]
        c[0:a.shape[0], o:o + n] = a

    i = np.arange(P)
    put("ident", np.eye(P, dtype=np.float32))
    put("mean128", np.full((P, P), 1.0 / 128, np.float32))
    put("mean64", ((i[:, None] // 64 == i[None, :] // 64) / 64.0).astype(np.float32))
    put("ones", np.ones((P, P), np.float32))
    dist = i[:, None] + P - np.arange(256)[None, :]
    put("dist", dist.astype(np.float32))
    put("wmask", np.where((dist >= 0) & (dist < P), 0.0, NEG).astype(np.float32))
    causal = i[:, None] <= i[None, :]
    put("hmask", (causal & (i[:, None] // 32 == i[None, :] // 32)).astype(np.float32))
    put("causal", causal.astype(np.float32))
    sel = np.zeros((4, 4, P), np.float32)
    for h in range(4):
        sel[h, h] = 1.0
    put("sel", sel.reshape(4, 512))
    put("iota", np.broadcast_to(np.arange(P, dtype=np.float32), (P, P)))
    put("iota16", np.broadcast_to(np.arange(16, dtype=np.float32), (P, 16)))
    put("reset", np.broadcast_to((np.arange(1024) % 32 != 0).astype(np.float32), (P, 1024)))
    return c


def tiles_T(w, per):
    K, N = w.shape[0] // P, w.shape[1] // P
    a = w.reshape(K, P, N, P).transpose(2, 1, 0, 3)
    return np.ascontiguousarray(a.reshape(N // per, per, P, K * P).transpose(0, 2, 1, 3).reshape(N // per, P, -1))


def tiles_A(w):
    K, N = w.shape[0] // P, w.shape[1]
    per = UNIT // N
    return np.ascontiguousarray(w.reshape(K // per, per, P, N).transpose(0, 2, 1, 3).reshape(K // per, P, per * N))


def cols(v, n):
    return np.asarray(v, np.float32).reshape(n, P).T


def layout(a):
    w = a["w_in"][0]
    heads = [c for j in range(4) for h in (j, j + 4) for c in range(h * 64, h * 64 + 64)]
    av = tiles_T(w[:, 640:768], 1)
    ak = tiles_T(w[:, 512:640], 1)
    s = {}
    s["w_in_t"] = np.concatenate([
        tiles_T(w[:, heads], 2), np.concatenate([ak, av], 2), tiles_T(w[:, 768:1792], 2), tiles_T(w[:, 2304:2816], 2)])
    s["w_in_hi"] = tiles_A(w[:, 1792:2304])
    s["w_in_g"] = tiles_T(w[:, 2816:4864], 2)
    s["w_ap"] = tiles_T(a["w_attn_proj"][0][heads], 4)
    s["w_hp"] = tiles_T(a["w_hgrn_proj"][0], 4)
    s["w_out"] = tiles_A(a["w_out"][0])
    s["w_pq"] = tiles_T(a["w_peer_q"][0], 2)
    s["keys"] = np.ascontiguousarray(a["peer_keys"][0].transpose(3, 1, 0, 2).reshape(1, P, 2048))
    u = a["peer_u"][0].reshape(P, 64, 2, KD, P)
    s["u"] = np.ascontiguousarray(u.transpose(1, 4, 2, 3, 0).reshape(64, P, 2048))
    s["v"] = np.ascontiguousarray(a["peer_v"][0].reshape(P, 64, 2048).transpose(1, 0, 2))
    w = a["w_in_2"][0]
    s["w2_t"] = tiles_T(np.concatenate([w[:, 0:256], w[:, 512:2048]], 1), 2)
    s["w2_v"] = np.ascontiguousarray(w[:, 256:512].reshape(1, KD, P, 256).transpose(0, 2, 1, 3).reshape(1, P, 2048))
    s["w2_c"] = np.concatenate([a[n][0].transpose(1, 0, 2).reshape(P, 512) for n in ("w_q_c_2", "w_k_c_2", "w_v_c_2")],
                               1).reshape(1, P, 1536)
    s["w2_out"] = tiles_A(a["w_out_2"][0])
    s["w_xk"] = tiles_T(a["w_xkv_2"][0][:, 0:D], 2)
    s["w_xv"] = tiles_A(a["w_xkv_2"][0][:, D:2 * D])
    s["w_xq"] = tiles_T(a["w_xq_2"][0], 2)
    s["w_xo"] = tiles_A(a["w_xo_2"][0])
    g, p_ = tiles_T(a["w_up_2"][0][:, 0:DFF], 1), tiles_T(a["w_up_2"][0][:, DFF:], 1)
    s["w_up"] = np.concatenate([g, p_], 2)
    s["w_down"] = tiles_A(a["w_down_2"][0])

    v = np.zeros((P, NV), np.float32)

    def put(name, x):
        o, n = VOFF[name]
        v[0:x.shape[0], o:o + n] = x

    for name, key in (("g_mix", "norm_mix_g"), ("g_ffn", "norm_ffn_g"), ("g_mix2", "norm_mix_g_2"),
                      ("g_x2", "norm_x_g_2"), ("g_mem2", "norm_mem_g_2"), ("g_ffn2", "norm_ffn_g_2")):
        put(name, cols(a[key][0], 8))
    put("lb", cols(a["hgrn_lb_logits"].reshape(-1), 8))
    put("g_hgrn", cols(a["hgrn_norm_g"][0], 1))
    put("cbw", a["conv_b_w_2"][0].reshape(31, 2, P).transpose(2, 1, 0).reshape(P, 62))
    for name, key, n in (("cbb", "conv_b_b_2", 2), ("gng", "gn_b_g_2", 2), ("gnb", "gn_b_b_2", 2),
                         ("ccb", "conv_c_b_2", 4), ("hng", "hn_c_g_2", 4), ("skip", "skip_c_2", 4),
                         ("cfb", "conv_f_b_2", 22)):
        put(name, cols(a[key][0], n))
    put("ccw", a["conv_c_w_2"][0].reshape(4, 4, P).transpose(2, 1, 0).reshape(P, 16))
    put("cfw", a["conv_f_w_2"][0].reshape(3, 22, P).transpose(2, 1, 0).reshape(P, 66))
    put("bi", a["b_igate_2"][0].reshape(4, 1))
    put("bf", a["b_fgate_2"][0].reshape(4, 1))
    bs = a["b_s_2"][0].reshape(2, 2, 1, P)
    put("bs", np.broadcast_to(bs, (2, 2, 64, P)).transpose(1, 2, 0, 3).reshape(P, 256))
    put("wgate", w[:, 2048:2056].reshape(KD, P, 8).transpose(1, 0, 2).reshape(P, 64))
    put("wsT", a["w_s_2"][0].transpose(2, 0, 1).reshape(P, 512))
    row = np.concatenate([a["norm_final_g"], a["final_g_2"], a["ln_a_g_2"][0], a["ln_a_b_2"][0],
                          a["attn_sinks"][0]]).astype(np.float32)
    return s, v, row


def kernel(**inputs):
    import numpy as _np
    import concourse.bacc as _bacc
    from concourse import mybir as _mybir
    from concourse.bass_utils import run_bass_kernel_spmd as _run

    a = {k: _np.asarray(v) for k, v in inputs.items()}
    s, v, row = layout(a)
    nc = _bacc.Bacc("TRN2", target_bir_lowering=False, num_devices=1)
    arrays = {"x": _np.ascontiguousarray(a["x"][0]), "mem": _np.ascontiguousarray(a["mem_2"][0]),
              "vec": v, "con": constants(), "row": row}
    arrays.update(s)
    aps = {k: nc.dram_tensor(f"in_{k}", list(z.shape), _mybir.dt.float32, kind="ExternalInput").ap()
           for k, z in arrays.items()}
    out = nc.dram_tensor("out", [T, D], _mybir.dt.float32, kind="ExternalOutput").ap()
    build(nc, aps["x"], aps["mem"], {k: aps[k] for k in s}, aps["vec"], aps["con"], aps["row"], out)
    r = _run(nc, [{f"in_{k}": z for k, z in arrays.items()}], core_ids=[0])
    return r.results[0]["out"].reshape(1, T, D)
```

```python
from contextlib import ExitStack

import numpy as np

import concourse.bass as bass
from concourse import mybir

ALU = mybir.AluOpType
ACT = mybir.ActivationFunctionType
F32 = mybir.dt.float32
F32R = mybir.dt.float32r
U32 = mybir.dt.uint32
I32 = mybir.dt.int32
AX = mybir.AxisListType.X

P = 128
D = 1024
T = 256
TB = 2
KD = D // P
DFF = 2816
EPS = 1e-6
LN_EPS = 1e-5
NEG = -1e30

UNIT = 1024
NRAW = 4
NSPL = 3
POOL_OF = 1000000
OB = 4

STREAMS = [
    ("w_in_t", 18),
    ("w_in_hi", 4),
    ("w_in_g", 16),
    ("w_ap", 4),
    ("w_hp", 4),
    ("w_out", 8),
    ("w_pq", 16),
    ("u", 128),
    ("v", 128),
    ("w2_t", 14),
    ("w2_v", 2),
    ("w_xk", 8),
    ("w_xv", 8),
    ("w2_out", 8),
    ("w_xq", 8),
    ("w_xo", 8),
    ("w_up", 44),
    ("w_down", 22),
]

KEEP = [
    ("ident", 128), ("iota", 128), ("iota16", 16),
    ("g_mix", 8), ("g_ffn", 8), ("g_mix2", 8), ("g_x2", 8), ("g_mem2", 8), ("g_ffn2", 8),
    ("cfw", 66), ("cfb", 22),
]
CON1 = [("hmask", 128), ("mean128", 128), ("reset", 1024), ("lb", 8), ("g_hgrn", 1), ("sinks", 8)]
CON0 = [("dist", 256), ("wmask", 256)]
CON2 = [
    ("mean64", 128), ("mean128", 128), ("ones", 128), ("causal", 128), ("sel", 512), ("lng", 256), ("lnb", 256),
    ("wsT", 512), ("bs", 256), ("wgate", 64), ("cbw", 62), ("cbb", 2), ("gng", 2), ("gnb", 2), ("ccw", 16),
    ("ccb", 4), ("hng", 4), ("skip", 4), ("bi", 1), ("bf", 1),
]


def offsets(table):
    at, out = 0, {}
    for name, n in table:
        out[name] = (at, n)
        at += n
    return out, at


KOFF, NKEEP = offsets(KEEP)
OFF0, NCON0 = offsets(CON0)
OFF1, NCON1 = offsets(CON1)
OFF2, NCON2 = offsets(CON2)


class Engine:

    def __init__(self, name, sem):
        self.name, self.sem = name, sem
        self.count = 0
        self.work = []
        self.seen = {}

    def last(self):
        return (self.sem, self.count)

    def wait(self, *after):
        for sem, value in after:
            if value > self.seen.get(id(sem), 0):
                self.seen[id(sem)] = value
                self.work.append(lambda e, s=sem, v=value: e.wait_ge(s, v))

    def run(self, fn, *after):
        self.wait(*after)
        self.count += 1
        self.work.append(lambda e, f=fn, s=self.sem: f(e).then_inc(s, 1))
        return (self.sem, self.count)

    def then(self, fn, *after):
        return self.run(fn, self.last(), *after)

    def emit(self, eng):
        for f in self.work:
            f(eng)


def build(nc, x, mem, wdram, keep_d, con0_d, con1_d, con2_d, keys_d, w2c_d, gf_d, gf2_d, out):
    ctx = ExitStack()
    with ctx:
        def sb(name, n, dt=F32, c=ctx):
            return c.enter_context(nc.sbuf_tensor(name, [P, n], dt))

        def sem(name):
            return ctx.enter_context(nc.semaphore(name))

        banks = [ctx.enter_context(nc.psum_tensor(f"bank{i}", [P, 512], F32)) for i in range(8)]
        raw = [sb(f"raw{i}", UNIT) for i in range(NRAW)]
        whi = [sb(f"whi{i}", UNIT, F32R) for i in range(NSPL)]
        wlo = [sb(f"wlo{i}", UNIT, F32R) for i in range(NSPL)]
        keep = sb("keep", NKEEP)
        xres = sb("xres", 2048)
        hTh = sb("hTh", 2048, F32R)
        hTl = sb("hTl", 2048, F32R)
        small = sb("small", 256)
        iT = sb("iT", 3 * T)
        oh1 = sb("oh1", 2 * OB * P)
        og = sb("og", 2 * OB * 64)
        with ExitStack() as c:
            A1 = sb("A1", 24576, c=c)
            R1 = (sb("R1h", 4096, F32R, c), sb("R1l", 4096, F32R, c))
        with ExitStack() as c:
            A2 = sb("A2", 32768, c=c)
        with ExitStack() as c:
            A3 = sb("A3", 24576, c=c)
            R3 = (sb("R3h", 4096, F32R, c), sb("R3l", 4096, F32R, c))
        A4 = sb("A4", 8192)
        R4 = (sb("R4h", 5632, F32R), sb("R4l", 5632, F32R))

        pe = Engine("pe", sem("s_pe"))
        dve = Engine("dve", sem("s_dve"))
        act = Engine("act", sem("s_act"))
        pool = Engine("pool", sem("s_pool"))
        sp = Engine("sp", sem("s_sp"))
        s_raw = [sem(f"s_raw{i}") for i in range(NRAW)]
        s_in, s_keep, s_con0, s_con1, s_con2, s_keys, s_w2c, s_gf, s_gf2, s_mem, s_out = (
            sem(n) for n in ("s_in", "s_keep", "s_con0", "s_con1", "s_con2", "s_keys", "s_w2c", "s_gf", "s_gf2",
                             "s_mem", "s_out"))

        def pick(tile, at, table):
            def f(name, a=0, b=None):
                o, n = table[name]
                return tile[:, at + o + a:at + o + (n if b is None else b)]
            return f

        K_ = pick(keep, 0, KOFF)

        def all_done():
            return [pe.last(), dve.last(), act.last(), pool.last()]

        def load(s, dst, src, *after):
            sp.wait(*after)
            sp.work.append(lambda e: e.dma_start(dst, src).then_inc(s, 16))

        units = [(name, i) for name, k in STREAMS for i in range(k)]
        fetched, cut, taken = [0], [0], [0]
        lo_done, hi_done, used = {}, {}, {}

        def fetch():
            i = fetched[0]
            if i >= len(units):
                return
            fetched[0] += 1
            name, k = units[i]
            if i >= NRAW:
                sp.wait(lo_done[i - NRAW])
            dst, src, s = raw[i % NRAW][:, :], wdram[name][k], s_raw[i % NRAW]
            sp.work.append(lambda e: e.dma_start(dst, src).then_inc(s, 16))

        def divide():
            i = cut[0]
            if i >= len(units):
                return
            cut[0] += 1
            r, h, l = raw[i % NRAW][:, :], whi[i % NSPL][:, :], wlo[i % NSPL][:, :]
            landed = (s_raw[i % NRAW], 16 * (i // NRAW + 1))
            before = [used[i - NSPL]] if i >= NSPL else []
            hi_done[i] = act.run(af(h, r, ACT.Copy), landed, *before)
            eng = pool if i % POOL_OF == POOL_OF - 1 else dve
            lo_done[i] = eng.run(tt(l, r, h.bitcast(F32), ALU.subtract), hi_done[i])
            fetch()

        def take(name):
            i = taken[0]
            taken[0] += 1
            assert units[i][0] == name, (units[i], name)
            while cut[0] <= i + NSPL - 1:
                if cut[0] >= NSPL and cut[0] - NSPL not in used:
                    break
                if cut[0] >= len(units):
                    break
                divide()
            return (whi[i % NSPL][:, :], wlo[i % NSPL][:, :]), [hi_done[i], lo_done[i]]

        def release(token):
            used[taken[0] - 1] = token

        free = [[] for _ in range(8)]
        turn = [0]

        held = set()

        def bank():
            while 4 + turn[0] % 4 in held:
                turn[0] += 1
            b = 4 + turn[0] % 4
            turn[0] += 1
            return b

        def products(items):
            def go(e):
                for o, l, r, st, sp_ in items:
                    ins = e.matmul(o, l, r, start=st, stop=sp_, skip_group_check=True)
                return ins
            return go

        def mm_group(b, items, *after):
            waits = list(after) + free[b]
            free[b] = []
            return pe.run(products(items), *waits)

        def tr_group(b, items, *after):
            waits = list(after) + free[b]
            free[b] = []

            def go(e):
                for o, i in items:
                    k = i.shape[0]
                    ins = e.transpose(o, i, K_("ident")[0:k, 0:k])
                return ins

            return pe.run(go, *waits)

        def three(o, a, b, start, stop):
            return [(o, a[0], b[0], start, False), (o, a[0], b[1], False, False), (o, a[1], b[0], False, stop)]

        def ts(o, i, s1, s2, op0, op1=ALU.bypass):
            if s2 is None:
                return lambda e: e.tensor_scalar(o, i, s1, None, op0)
            return lambda e: e.tensor_scalar(o, i, s1, s2, op0, op1)

        def tt(o, a, b, op):
            return lambda e: e.tensor_tensor(o, a, b, op)

        def stt(o, a, s, b, op0, op1):
            return lambda e: e.scalar_tensor_tensor(o, a, s, b, op0, op1)

        def af(o, i, func, bias=None, scale=None, accum=None):
            kw = {}
            if bias is not None:
                kw["bias"] = bias
            if scale is not None:
                kw["scale"] = scale
            if accum is not None:
                kw["accum_out"] = accum
            return lambda e: e.activation(o, i, func, **kw)

        def cp(o, i):
            return lambda e: e.tensor_copy(o, i)

        def t3(ap, a):
            return ap.rearrange("p (a b) -> p a b", a=a)

        def t4(ap, a, b):
            return ap.rearrange("p (a b c) -> p a b c", a=a, b=b)

        def parts(dst, src, *after):
            h = act.run(af(dst[0], src, ACT.Copy), *after)
            return dve.run(tt(dst[1], src, dst[0].bitcast(F32), ALU.subtract), h)

        def two(ap, n):
            return [t3(a, n) for a in ap]

        def sub(ap, a, b):
            return [z[:, a:b] for z in ap]

        hTv = (t3(hTh[:, :], KD), t3(hTl[:, :], KD))

        side = []

        def step(n=1):
            for _ in range(n):
                while side:
                    try:
                        next(side[0])
                        break
                    except StopIteration:
                        side.pop(0)

        def drain():
            while side:
                step()

        def inv_rms(src, scratch, st, n, eps, *after):
            a = act.run(af(scratch, src, ACT.Square, accum=st[:, 0:1]), *after)
            d = dve.run(ts(st[:, 1:2], st[:, 0:1], 1.0 / n, eps, ALU.mult, ALU.add), a)
            a = act.run(af(st[:, 1:2], st[:, 1:2], ACT.Sqrt), d)
            return dve.run(lambda e: e.reciprocal(st[:, 2:3], st[:, 1:2]), a)

        def norm_to_T(src, gname, dst, scratch, *after):
            ready = []
            for b in range(TB):
                s = src[:, b * D:(b + 1) * D]
                xn = scratch[:, b * D:(b + 1) * D]
                t = inv_rms(s, xn, small[:, 4 * b:4 * b + 4], D, EPS, *after)
                ready.append(dve.run(ts(xn, s, small[:, 4 * b + 2:4 * b + 3], None, ALU.mult), t))
            for k2 in range(KD // 2):
                bk = bank()
                pb = banks[bk]
                tok = tr_group(bk, [(pb[:, (kk * 2 + b) * P:(kk * 2 + b + 1) * P],
                                     scratch[:, b * D + (2 * k2 + kk) * P:b * D + (2 * k2 + kk + 1) * P])
                                    for kk in range(2) for b in range(TB)], ready[1])
                ks = [(dst[0][:, 2 * k2 + kk, :], dst[1][:, 2 * k2 + kk, :], pb[:, kk * 256:(kk + 1) * 256],
                       K_(gname, 2 * k2 + kk, 2 * k2 + kk + 1)) for kk in range(2)]
                for hi, lo, p_, g in ks:
                    h = act.run(af(hi, p_, ACT.Copy, scale=g), tok)
                for hi, lo, p_, g in ks:
                    dve.run(stt(lo, p_, g, hi.bitcast(F32), ALU.mult, ALU.subtract), h)
                free[bk] = [dve.last()]
            return dve.last()

        def lin_T(name, src, K, ready, consume, n_tiles, steps=1):
            per = UNIT // (K * P)
            n, tok = 0, None
            items, waits = [], []
            while n < n_tiles:
                w, there = take(name)
                wv = [z.rearrange("p (n k c) -> p n k c", n=per, k=K) for z in w]
                for j in range(per):
                    if n % 2 == 0:
                        bk = bank()
                        held.add(bk)
                        pb = banks[bk]
                    o = pb[:, (n % 2) * 256:(n % 2 + 1) * 256]
                    items = []
                    for k in range(K):
                        items += three(o, [z[:, j, k, :] for z in wv], [z[:, k, :] for z in src], k == 0, k == K - 1)
                    tok = mm_group(bk, items, *there, *ready)
                    if n % 2:
                        free[bk] = consume(n - 1, t3(pb[:, :], 2), tok)
                        held.discard(bk)
                    n += 1
                release(tok)
                step(steps)

        def lin_A(name, src, K, N, ready, steps=1):
            per = UNIT // N
            nh = N // 512
            after = [t for i in range(TB * nh) for t in free[i]]
            for k0 in range(0, K, per):
                w, there = take(name)
                wv = [t3(z, per) for z in w]
                items = []
                for kk in range(per):
                    k = k0 + kk
                    for b in range(TB):
                        for h in range(nh):
                            items += three(banks[b * nh + h][:, :], [z[:, k, b * P:(b + 1) * P] for z in src],
                                           [z[:, kk, h * 512:(h + 1) * 512] for z in wv], k == 0, k == K - 1)
                tok = pe.run(products(items), *there, *ready, *after)
                release(tok)
                step(steps)
            return tok

        def add_residual(tok, dst, src):
            for b in range(TB):
                for h in range(2):
                    o = b * D + h * 512
                    dve.run(tt(dst[:, o:o + 512], banks[2 * b + h][:, :], src[:, o:o + 512], ALU.add), tok)
                    free[2 * b + h] = [dve.last()]
            return dve.last()

        def a1(at, n):
            return A1[:, at:at + n]

        aqT = t3(a1(0, 1280), 5)
        av = a1(1280, 256)
        q_s = a1(1536, 1024)
        f_s = a1(2560, 1024)
        hg_s = a1(3584, 1024)
        hi_s = a1(4608, 1024)
        scr = a1(5632, 2048)
        bias8 = a1(7680, 2048)
        S_s = a1(9728, 2048)
        S_e = a1(11776, 2048)
        pT = a1(13824, 2048)
        h_S = a1(15872, 4096)
        ga = t3(a1(19968, 2048), 8)
        c0_at = 19968
        c1_at = 22016
        gh_at = 7680
        h_b = a1(9728, 1024)
        h_kinv = a1(10752, 1024)
        h_kd = a1(11776, 1024)
        h_kdn = a1(12800, 1024)
        h_AT = a1(13824, 1024)
        h_sq = a1(14848, 1024)
        gh = t3(a1(gh_at, 2048), 8)
        yaT = two(sub(R1, 0, 1024), 4)
        yhT = two(sub(R1, 1024, 2048), 4)
        mrg = two(sub(R1, 2048, 4096), 8)
        C0 = pick(A1, c0_at, OFF0)
        C1 = pick(A1, c1_at, OFF1)
        assert c1_at + NCON1 <= 24576

        for b in range(TB):
            load(s_in, xres[:, b * D:(b + 1) * D], x[b * P:(b + 1) * P, :])
        load(s_keep, keep[:, :], keep_d)
        for _ in range(2):
            fetch()
        load(s_con0, A1[:, c0_at:c0_at + NCON0], con0_d)
        load(s_con1, A1[:, c1_at:c1_at + NCON1], con1_d)
        for _ in range(NRAW - 2):
            fetch()

        for h in range(8):
            slope = float(np.float32(2.0 ** (-(h + 1))))
            t_bias = pool.run(ts(bias8[:, h * 256:(h + 1) * 256], C0("dist"), -slope, None, ALU.mult), (s_con0, 16))
        for h in range(8):
            t_bias = pool.run(tt(bias8[:, h * 256:(h + 1) * 256], bias8[:, h * 256:(h + 1) * 256], C0("wmask"),
                                 ALU.add), t_bias)

        act.wait((s_in, 32))
        dve.wait((s_in, 32))
        pe.wait((s_keep, 16))
        act.wait((s_keep, 16))
        dve.wait((s_keep, 16))
        t_h = norm_to_T(xres, "g_mix", hTv, scr)

        lbv = small[:, 16:20]
        omlb = small[:, 20:24]
        l0, l1 = C1("lb", 0, 4), C1("lb", 4, 8)
        sm = small[:, 24:48]
        dve.then(tt(sm[:, 0:4], l0, l1, ALU.max), (s_con1, 16))
        dve.then(tt(sm[:, 4:8], l0, sm[:, 0:4], ALU.subtract))
        dve.then(tt(sm[:, 8:12], l1, sm[:, 0:4], ALU.subtract))
        act.then(af(sm[:, 12:20], sm[:, 4:12], ACT.Exp), dve.last())
        dve.then(tt(sm[:, 0:4], sm[:, 12:16], sm[:, 16:20], ALU.add), act.last())
        dve.then(lambda e: e.reciprocal(sm[:, 4:8], sm[:, 0:4]))
        dve.then(tt(lbv, sm[:, 12:16], sm[:, 4:8], ALU.mult))
        t_lb = dve.then(ts(omlb, lbv, -1.0, 1.0, ALU.mult, ALU.add))
        pe.wait((s_con1, 16))

        marks = {}

        def take_q_(n, pb, tok):
            return [act.run(af(aqT[:, n:n + 2, :], pb, ACT.Copy), tok)]

        lin_T("w_in_t", hTv, KD, [t_h], take_q_, 4)
        bk = bank()
        pb = banks[bk]
        w, there = take("w_in_t")
        wv = [t3(z, KD) for z in w]
        items = []
        for k in range(KD):
            items += three(pb[:, 0:256], [z[:, k, :] for z in wv], [z[:, k, :] for z in hTv], k == 0, k == KD - 1)
        release(mm_group(bk, items, *there))
        w, there = take("w_in_t")
        wv = [t3(z, KD) for z in w]
        items = []
        for b in range(TB):
            for k in range(KD):
                items += three(pb[:, 256 + b * P:256 + (b + 1) * P], [z[:, k, b * P:(b + 1) * P] for z in hTv],
                               [z[:, k, :] for z in wv], k == 0, k == KD - 1)
        tok = mm_group(bk, items, *there)
        release(tok)
        act.run(af(aqT[:, 4, :], pb[:, 0:256], ACT.Copy), tok)
        t_kv = act.run(af(av, pb[:, 256:512], ACT.Copy), tok)
        free[bk] = [t_kv]

        def take_in(n, pb, tok):
            dst, func = [(q_s, ACT.Silu), (f_s, ACT.Sigmoid), (hg_s, ACT.Silu)][n // 4]
            n = n % 4
            return [act.run(af(t3(dst, 4)[:, n:n + 2, :], pb, func), tok)]

        st = small[:, 64:96]

        def attention(blk):
            nk = P * (blk + 1)
            Sv = S_s[:, 0:8 * nk].rearrange("p (h s) -> p h s", h=8)
            Ev = S_e[:, 0:8 * nk].rearrange("p (h s) -> p h s", h=8)
            Bv = t3(bias8, 8)[:, :, 256 - nk:256]
            for h2 in range(4):
                bk = bank()
                pb = t3(banks[bk][:, :], 2)
                items = []
                for q in range(2):
                    h = 2 * h2 + q
                    kv, j = h // 4, h % 4
                    items.append((pb[:, q, 0:nk], aqT[64 * kv:64 * kv + 64, j, blk * P:(blk + 1) * P],
                                  aqT[64 * kv:64 * kv + 64, 4, 0:nk], True, True))
                tok = mm_group(bk, items, t_kv)
                dve.run(stt(Sv[:, 2 * h2:2 * h2 + 2, :], pb[:, :, 0:nk], 0.125, Bv[:, 2 * h2:2 * h2 + 2, :],
                            ALU.mult, ALU.add), tok, t_bias)
                free[bk] = [dve.last()]
            yield
            mx, sk, sm_, rc = st[:, 0:8], st[:, 8:16], st[:, 16:24], st[:, 24:32]
            dve.then(lambda e: e.tensor_reduce(mx, Sv, AX, ALU.max))
            dve.then(tt(mx, mx, C1("sinks"), ALU.max))
            dve.then(tt(sk, C1("sinks"), mx, ALU.subtract))
            dve.then(tt(Sv, Sv, mx.unsqueeze(2).to_broadcast([P, 8, nk]), ALU.subtract))
            act.run(af(Ev, Sv, ACT.Exp), dve.last(), pe.last())
            act.run(af(sk, sk, ACT.Exp), dve.last())
            yield
            dve.then(lambda e: e.tensor_reduce(sm_, Ev, AX, ALU.add), act.last())
            dve.then(tt(sm_, sm_, sk, ALU.add))
            dve.then(lambda e: e.reciprocal(rc, sm_))
            t_p = dve.then(tt(Ev, Ev, rc.unsqueeze(2).to_broadcast([P, 8, nk]), ALU.mult))
            yield
            for kv in range(2):
                pTv = pT[:, kv * 1024:kv * 1024 + nk * 4].rearrange("p (a h t) -> p a h t", a=blk + 1, h=4)
                t_tr = []
                for a in range(blk + 1):
                    bk = bank()
                    pb = banks[bk]
                    tok = tr_group(bk, [(pb[:, q * P:(q + 1) * P], Ev[:, 4 * kv + q, a * P:(a + 1) * P])
                                        for q in range(4)], t_p)
                    t_tr = act.run(af(pTv[:, a, :, :], t3(pb[:, :], 4), ACT.Copy), tok)
                    free[bk] = [t_tr]
                yield
            bo = bank()
            po = banks[bo]
            items = []
            for kv in range(2):
                pTv = pT[:, kv * 1024:kv * 1024 + nk * 4].rearrange("p (a h t) -> p a h t", a=blk + 1, h=4)
                for j in range(4):
                    for a in range(blk + 1):
                        items.append((po[64 * kv:64 * kv + 64, j * P:(j + 1) * P],
                                      av[:, a * P + 64 * kv:a * P + 64 * kv + 64], pTv[:, a, j, :], a == 0, a == blk))
            tok = mm_group(bo, items, t_tr)
            dst = [z[:, :, blk * P:(blk + 1) * P] for z in yaT]
            marks["ya"] = parts(dst, t3(po[:, :], 4), tok)
            free[bo] = [marks["ya"]]
            yield

        def hgrn(t_gates, t_hi):
            t_ya = marks["ya"]
            f4 = t3(f_s, 4)
            for h in range(4):
                dve.run(ts(f4[:, h, :], f4[:, h, :], omlb[:, h:h + 1], lbv[:, h:h + 1], ALU.mult, ALU.add),
                        t_gates, t_lb)
            a = act.run(af(scr[:, 0:1024], f_s, ACT.Ln), dve.last(), t_h, pe.last())
            dve.then(ts(f_s, f_s, -1.0, 1.0, ALU.mult, ALU.add), a)
            d = dve.run(lambda e: e.tensor_tensor_scan(h_b, C1("reset"), scr[:, 0:1024], 0.0, ALU.mult, ALU.add), a,
                        t_ya)
            yield
            bl = h_b.rearrange("p (n c) -> p n c", c=32)[:, :, 31:32]
            eb = scr[:, 1024:2048]
            a1_ = act.run(af(eb, h_b, ACT.Exp), d)
            a2_ = act.run(af(h_kinv, h_b, ACT.Exp, scale=-1.0))
            decay = small[:, 128:160]
            act.run(af(decay.unsqueeze(2), bl, ACT.Exp))
            dve.run(tt(h_kd.rearrange("p (n c) -> p n c", c=32), bl.to_broadcast([P, 32, 32]),
                       h_b.rearrange("p (n c) -> p n c", c=32), ALU.subtract), d)
            a3_ = act.run(af(h_kd, h_kd, ACT.Exp), dve.last())
            yield
            dve.run(tt(q_s, q_s, eb, ALU.mult), a1_)
            t_kq = dve.run(tt(h_kinv, h_kinv, f_s, ALU.mult), a2_)
            t_kd = dve.run(tt(h_kd, h_kd, f_s, ALU.mult), a3_)
            t_hz = dve.run(lambda e: e.memset(h_AT, 0.0), t_ya)
            yield
            kdT = h_kdn.rearrange("p (b h d) -> p b h d", b=2, h=4)
            for b in range(TB):
                bk = bank()
                pb = banks[bk]
                tok = tr_group(bk, [(pb[:, h * P:(h + 1) * P], h_kd[:, h * T + b * P:h * T + (b + 1) * P])
                                    for h in range(4)], t_kd)
                t_kdn = act.run(af(kdT[:, b], t3(pb[:, :], 4), ACT.Copy), tok)
                free[bk] = [t_kdn]
            AT = h_AT.rearrange("p (b h t) -> p b h t", b=2, h=4)
            for b in range(TB):
                bk = bank()
                pb = banks[bk]
                tok = mm_group(bk, [(pb[:, h * P:(h + 1) * P], h_kinv[:, h * T + b * P:h * T + (b + 1) * P],
                                     q_s[:, h * T + b * P:h * T + (b + 1) * P], True, True) for h in range(4)],
                               t_kq)
                t_AT = dve.run(lambda e, b=b, pb=pb: e.copy_predicated(
                    AT[:, b], C1("hmask").bitcast(I32).unsqueeze(1).to_broadcast([P, 4, P]), t3(pb[:, :], 4)),
                    tok, t_hz)
                free[bk] = [t_AT]
            yield
            Sv = h_S.rearrange("p (h n v) -> p h n v", h=4, n=8)
            hiv = hi_s.rearrange("p (b h v) -> p b h v", b=2, h=4)
            for n in range(7):
                b, r = n // 4, 32 * (n % 4)
                bk = bank()
                pb = banks[bk]
                tok = mm_group(bk, [(pb[:, h * P:(h + 1) * P], kdT[r:r + 32, b, h, :], hiv[r:r + 32, b, h, :],
                                     True, True) for h in range(4)], t_kdn, t_hi)
                for h in range(4):
                    if n == 0:
                        ins = cp(Sv[:, h, 1, :], pb[:, h * P:(h + 1) * P])
                    else:
                        ins = stt(Sv[:, h, n + 1, :], Sv[:, h, n, :], decay[:, h * 8 + n:h * 8 + n + 1],
                                  pb[:, h * P:(h + 1) * P], ALU.mult, ALU.add)
                    dve.run(ins, tok, t_state if n else tok)
                t_state = dve.last()
                free[bk] = [t_state]
                if n % 2:
                    yield
            yo = scr[:, 0:1024]
            for h in range(4):
                bk = bank()
                pb = banks[bk]
                items = []
                for b in range(TB):
                    items.append((pb[:, b * P:(b + 1) * P], hiv[:, b, h, :], AT[:, b, h, :], b == 0, False))
                for n in range(1, 8):
                    items.append((pb[:, n * 32:(n + 1) * 32], Sv[:, h, n, :],
                                  q_s[:, h * T + n * 32:h * T + n * 32 + 32], False, n == 7))
                tok = mm_group(bk, items, t_AT, t_state)
                dve.run(cp(yo[:, h * T:(h + 1) * T], pb[:, 0:256]), tok)
                free[bk] = [dve.last()]
            a = act.run(af(h_sq, yo, ACT.Square), dve.last())
            yield
            for h2 in range(2):
                bk = bank()
                pb = banks[bk]
                tok = mm_group(bk, [(pb[:, :], C1("mean128"), h_sq[:, h2 * 512:(h2 + 1) * 512], True, True)], a)
                d = dve.run(ts(h_b[:, h2 * 512:(h2 + 1) * 512], pb[:, :], EPS, None, ALU.add), tok)
                free[bk] = [d]
            a = act.run(af(h_b, h_b, ACT.Sqrt), d)
            dve.run(tt(yo, yo, hg_s, ALU.mult), t_gates)
            dve.run(lambda e: e.reciprocal(h_b, h_b), a)
            dve.then(stt(yo, yo, C1("g_hgrn"), h_b, ALU.mult, ALU.mult))
            marks["yh"] = parts([z.rearrange("p a b -> p (a b)") for z in yhT], yo, dve.last())
            yield

        side.append(attention(0))
        side.append(attention(1))
        lin_T("w_in_t", hTv, KD, [], take_in, 12)
        t_gates = act.last()
        tok = lin_A("w_in_hi", hTv, KD, 512, [])
        for b in range(TB):
            t_hi = act.run(af(hi_s[:, b * 512:(b + 1) * 512], banks[b][:, :], ACT.Copy), tok)
            free[b] = [t_hi]
        drain()
        t_ya = marks["ya"]
        side.append(hgrn(t_gates, t_hi))
        step()

        def take_gate(n, pb, tok):
            dst = ga[:, n:n + 2, :] if n < 8 else gh[:, n - 8:n - 6, :]
            return [act.run(af(dst, pb, ACT.Sigmoid), tok, t_ya)]

        lin_T("w_in_g", hTv, KD, [], take_gate, 16)
        t_sig = act.last()

        def merge_a(n, pb, tok):
            return [dve.run(tt(ga[:, n:n + 2, :], ga[:, n:n + 2, :], pb, ALU.mult), tok, t_sig)]

        def merge_h(n, pb, tok):
            bf = dve.run(tt(gh[:, n:n + 2, :], gh[:, n:n + 2, :], pb, ALU.mult), tok)
            dve.then(tt(ga[:, n:n + 2, :], ga[:, n:n + 2, :], gh[:, n:n + 2, :], ALU.add))
            marks["mrg"] = parts([z[:, n:n + 2, :] for z in mrg], ga[:, n:n + 2, :], dve.last())
            return [bf]

        lin_T("w_ap", yaT, 4, [t_ya], merge_a, 8)
        drain()
        lin_T("w_hp", yhT, 4, [marks["yh"]], merge_h, 8)
        tok = lin_A("w_out", mrg, KD, D, [marks["mrg"]])
        t_x = add_residual(tok, xres, xres)

        t_h = norm_to_T(xres, "g_ffn", hTv, scr, t_x)
        before_peer = all_done()

        def a2(at, n):
            return A2[:, at:at + n]

        qT = t3(a2(11776, 4096), 16)
        sc_store = [a2(15872, 2048), a2(17920, 2048)]
        scw = a2(19968, 2048)
        cand = a2(22016, 2048)
        candw = a2(24064, 2048)
        oh = a2(26112, 2048)
        oh2 = a2(28160, 2048)
        keys = a2(26112, 2048)
        val = a2(30208, 256)
        idx = a2(30464, 256)
        idxf = a2(30720, 256)
        best = a2(30976, 128)
        posu = a2(31104, 384)
        posf = a2(31488, 256)
        route_from = 11776
        load(s_keys, keys, keys_d, *before_peer)
        dve.wait(*before_peer)
        act.wait(*before_peer)

        def take_q(n, pb, tok):
            return [act.run(af(qT[:, n:n + 2, :], pb, ACT.Copy), tok)]

        lin_T("w_pq", hTv, KD, [t_h], take_q, 16)
        t_q = act.last()
        t_sc = []
        for b in range(TB):
            for g in range(4):
                bk = bank()
                pb = banks[bk]
                tok = mm_group(bk, [(pb[:, q * P:(q + 1) * P], qT[:, 4 * g + q, b * P:(b + 1) * P],
                                     keys[:, (4 * g + q) * P:(4 * g + q + 1) * P], True, True) for q in range(4)],
                               t_q, (s_keys, 16))
                act.run(af(sc_store[b][:, g * 512:(g + 1) * 512], pb[:, :], ACT.Copy), tok)
                free[bk] = [act.last()]
            t_sc.append(act.last())

        def top16(src, work, vals, idxs, n, *after):
            for j in range(n):
                t1 = dve.run(lambda e, j=j: e.max(vals[:, j, 0:8], src[:, j, :]), *after)
                if j % 4 == 3:
                    yield
            for j in range(n):
                t = dve.run(lambda e, j=j: e.match_replace(work[:, j, :], vals[:, j, 0:8], src[:, j, :], -3e38), t1)
                if j % 4 == 3:
                    yield
            for j in range(n):
                t2 = dve.run(lambda e, j=j: e.max(vals[:, j, 8:16], work[:, j, :]), t)
                if j % 4 == 3:
                    yield
            for j in range(n):
                dve.run(lambda e, j=j: e.max_index(idxs[:, j, 0:8], vals[:, j, 0:8], src[:, j, :]), t2)
                dve.run(lambda e, j=j: e.max_index(idxs[:, j, 8:16], vals[:, j, 8:16], work[:, j, :]), t2)
                if j % 2:
                    yield

        def routing(b):
            scb = t3(sc_store[b], 16)
            scwv = t3(scw, 16)
            v3 = t3(val, 16)
            i3 = t3(idx, 16).bitcast(U32)
            yield from top16(scb, scwv, v3, i3, 16, t_sc[1], dve.last())
            dve.then(cp(idxf, idx.bitcast(U32)))
            vv = val.rearrange("p (h q a) -> p h q a", h=8, q=2)
            iv = idxf.rearrange("p (h q a) -> p h q a", h=8, q=2)
            shape = [P, 8, 16, 16]
            dve.then(tt(t4(cand, 8, 16), vv[:, :, 0, :].unsqueeze(3).to_broadcast(shape),
                        vv[:, :, 1, :].unsqueeze(2).to_broadcast(shape), ALU.add))
            yield
            bv = t3(best, 8)
            pu = t3(posu[:, 0:128], 8).bitcast(U32)
            yield from top16(t3(cand, 8), t3(candw, 8), bv, pu, 8, dve.last())
            pall = posu[:, 0:128].bitcast(U32)
            dve.then(ts(posu[:, 128:256].bitcast(U32), pall, 4, None, ALU.logical_shift_right))
            dve.run(ts(posu[:, 256:384].bitcast(U32), pall, 15, None, ALU.bitwise_and))
            dve.then(cp(posf, posu[:, 128:384].bitcast(U32)))
            bex = scw[:, 256:384]
            dve.run(tt(t3(bex, 8), bv, bv[:, :, 0:1].to_broadcast([P, 8, 16]), ALU.subtract))
            t_e = act.run(af(bex, bex, ACT.Exp), dve.last())
            yield
            sel_i = [scw[:, 0:128], scw[:, 128:256]]
            for q in range(2):
                ps = t3(posf[:, q * P:(q + 1) * P], 8)
                o4 = t4(oh, 8, 16)
                dve.then(tt(o4, ps.unsqueeze(3).to_broadcast(shape),
                            K_("iota16").unsqueeze(1).unsqueeze(1).to_broadcast(shape), ALU.is_equal))
                dve.then(tt(t4(oh2, 8, 16), o4, iv[:, :, q, :].unsqueeze(2).to_broadcast(shape), ALU.mult))
                yield
                dve.then(lambda e, q=q: e.tensor_reduce(t3(sel_i[q], 8), t4(oh2, 8, 16), AX, ALU.add))
                yield
            dve.then(lambda e: e.tensor_reduce(scw[:, 384:392], t3(bex, 8), AX, ALU.add), t_e)
            dve.then(lambda e: e.reciprocal(scw[:, 392:400], scw[:, 384:392]))
            dve.then(tt(t3(bex, 8), t3(bex, 8), scw[:, 392:400].unsqueeze(2).to_broadcast([P, 8, 16]), ALU.mult))
            t_r = dve.last()
            yield
            bk = bank()
            pb = banks[bk]
            tok = tr_group(bk, [(pb[:, q * P:(q + 1) * P], s) for q, s in enumerate([sel_i[0], sel_i[1], bex])], t_r)
            marks["route"] = dve.run(cp(t3(iT[:, :], 3)[:, :, b * P:(b + 1) * P], t3(pb[:, 0:384], 3)), tok)
            free[bk] = [marks["route"]]
            yield

        acts = t3(A2[:, :], P)

        oh_used = [[], []]

        def gates(half, t_acts):
            lo = 64 * half
            for g in range(T // OB):
                z = g % 2
                for q in range(OB):
                    t = g * OB + q
                    t_p = pool.run(ts(oh1[:, (z * OB + q) * P:(z * OB + q + 1) * P], K_("iota"), iT[:, t:t + 1], None,
                                      ALU.is_equal), marks["route"], *oh_used[z])
                for q in range(OB):
                    t = g * OB + q
                    t_d = dve.run(ts(og[:, (z * OB + q) * 64:(z * OB + q + 1) * 64], K_("iota", lo, lo + 64),
                                     iT[:, T + t:T + t + 1], iT[:, 2 * T + t:2 * T + t + 1], ALU.is_equal, ALU.mult),
                                  *oh_used[z])
                if g >= 1:
                    yield
                bk = bank()
                pb = banks[bk]
                tok = mm_group(bk, [(pb[:, q * 64:(q + 1) * 64], oh1[:, (z * OB + q) * P:(z * OB + q + 1) * P],
                                     og[:, (z * OB + q) * 64:(z * OB + q + 1) * 64], True, True) for q in range(OB)],
                               t_p, t_d)
                oh_used[z] = [tok]
                sl = acts[:, lo:lo + 64, g * OB:(g + 1) * OB].rearrange("p i t -> p t i")
                marks[f"g{half}"] = dve.run(tt(sl, sl, t3(pb[:, 0:64 * OB], OB), ALU.mult), tok, t_acts)
                free[bk] = [dve.last()]
            yield

        side.append(routing(0))
        side.append(routing(1))

        def gelu(n, pb, tok):
            waits = [t_sc[1]] if 256 * (n + 2) > route_from else []
            if 256 * (n + 2) > 15872:
                drain_routing()
                waits.append(marks["route"])
            return [act.run(af(acts[:, n:n + 2, :], pb, ACT.Gelu), tok, *waits)]

        def drain_routing():
            if "routed" not in marks:
                drain()
                marks["routed"] = 1

        lin_T("u", hTv, KD, [], gelu, 62, steps=2)
        drain_routing()
        lin_T("u", hTv, KD, [], lambda n, pb, tok: gelu(n + 62, pb, tok), 2)
        side.append(gates(0, act.last()))
        lin_T("u", hTv, KD, [], lambda n, pb, tok: gelu(n + 64, pb, tok), 64)
        t_acts = act.last()
        t_hused = pe.last()
        drain()
        side.append(gates(1, t_acts))

        after = [t for i in range(4) for t in free[i]]
        acth = (t3(hTh[:, :], 8), t3(hTl[:, :], 8))
        act_used, act_there = {}, {}

        def cut_acts(n):
            if n > 127:
                return
            before = [act_used[n - 8]] if n >= 8 else [t_hused]
            half = marks["g0"] if n < 64 else marks["g1"]
            act_there[n] = parts([z[:, n % 8, :] for z in acth], acts[:, n, :], half, *before)

        for n in range(2):
            cut_acts(n)
        CON2_AT = 0
        for n in range(128):
            w, there = take("v")
            if n == 62:
                drain()
            cut_acts(n + 2)
            items = []
            for b in range(TB):
                for h in range(2):
                    items += three(banks[2 * b + h][:, :], [z[:, n % 8, b * P:(b + 1) * P] for z in acth],
                                   [z[:, h * 512:(h + 1) * 512] for z in w], n == 0, n == 127)
            tok = pe.run(products(items), *there, act_there[n], *after)
            act_used[n] = tok
            release(tok)
            step()
            if n == 36:
                t_gone = [tok, act_there[n]]
                load(s_con2, A3[:, 0:NCON2], con2_d, *t_gone)
                load(s_gf, A3[:, NCON2:NCON2 + D], gf_d.partition_broadcast(P))
                load(s_w2c, A3[:, NCON2 + D:NCON2 + D + 1536], w2c_d)
                for b in range(TB):
                    load(s_mem, A3[:, NCON2 + 2560 + b * D:NCON2 + 2560 + (b + 1) * D], mem[b * P:(b + 1) * P, :])
        t_x = add_residual(tok, xres, xres)
        at0 = NCON2 + D + 1536
        assert at0 + 2048 <= 256 * 36

        def a3(at, n):
            assert at0 + at + n <= 24576, (at, n)
            return A3[:, at0 + at:at0 + at + n]

        C2 = pick(A3, 0, OFF2)
        gfin = A3[:, NCON2:NCON2 + D]
        wc = A3[:, NCON2 + D:NCON2 + D + 1536].rearrange("p (q h e) -> p q h e", q=3, h=4)
        memx = a3(0, 2048)
        kT2 = t3(memx, 8)
        mscr = a3(2048, 2048)
        v2 = mscr
        scr3 = a3(4096, 2048)
        hm = a3(4096, 1024)
        hm2 = a3(5120, 1024)
        uT = t3(a3(6144, 512), 2)
        aT = t3(a3(6656, 512), 2)
        gT = t3(a3(7168, 512), 2)
        xcT = t3(a3(7680, 1024), 4)
        ocT = t3(a3(8704, 1024), 4)
        vg = a3(9728, 512)
        xcv = t3(a3(10240, 1024), 4)
        qTm = t3(a3(11264, 1024), 4)
        kTm = t3(a3(12288, 1024), 4)
        vnm = a3(13312, 1024)
        knm = a3(14336, 512)
        rows = a3(14848, 2304)
        wTm = a3(17152, 384)
        cm = a3(17536, 512)
        conv_o = A3[:, NCON2:NCON2 + 512]
        conv_p = A3[:, NCON2 + 512:NCON2 + 1024]
        den_t = hm2[:, 0:256]
        yT = two(sub(R3, 0, 2048), 8)
        mT = two(sub(R3, 2048, 4096), 8)

        def final_norm(g, scratch, *after):
            out_ = []
            for b in range(TB):
                s = xres[:, b * D:(b + 1) * D]
                s_ = small[:, 4 * b:4 * b + 4]
                t = inv_rms(s, scratch[:, b * D:(b + 1) * D], s_, D, EPS, *after)
                out_.append(dve.run(stt(s, s, s_[:, 2:3], g, ALU.mult, ALU.mult), t))
            return out_

        t_x = final_norm(gfin, scr3, t_x, (s_gf, 16))
        act.wait((s_con2, 16))
        dve.wait((s_con2, 16))
        pool.wait((s_con2, 16))
        pe.wait((s_con2, 16))
        wsT = C2("wsT")
        for h in range(4):
            t_ws = pool.run(tt(wsT[:, h * P:(h + 1) * P], wsT[:, h * P:(h + 1) * P], C2("causal"), ALU.mult))
        t_h = norm_to_T(xres, "g_mix2", hTv, scr3, *t_x)
        before2 = all_done()

        wg = t3(C2("wgate"), KD)
        bg = bank()
        pbg = banks[bg]
        hT32 = t3(hTh[:, :].bitcast(F32), KD)
        hL32 = t3(hTl[:, :].bitcast(F32), KD)
        tok_g = mm_group(bg, [(pbg[0:4, q * 256:(q + 1) * 256], wg[:, k, 4 * q:4 * q + 4], hh[:, k, :],
                               k == 0 and j == 0, k == KD - 1 and j == 1)
                              for q in range(2) for k in range(KD) for j, hh in enumerate((hT32, hL32))], t_h)

        def row_(i, n=T):
            return rows[0:4, i * T:i * T + n]

        li, lf, bc, Rr, pm, mm_, emm, t0, t1 = (row_(i) for i in range(9))
        Rc = small[:, 160:168]

        def gate_rows():
            dve.run(ts(li, pbg[0:4, 0:256], C2("bi")[0:4, :], None, ALU.add), tok_g)
            d = dve.run(ts(t0, pbg[0:4, 256:512], C2("bf")[0:4, :], None, ALU.add))
            free[bg] = [d]
            dve.then(ts(lf, t0, 0.0, None, ALU.min))
            dve.run(ts(t1, t0, 0.0, None, ALU.max))
            dve.then(tt(t1, lf, t1, ALU.subtract))
            act.run(af(t1, t1, ACT.Exp), dve.last())
            dve.then(ts(t1, t1, 1.0, None, ALU.add), act.last())
            act.run(af(t1, t1, ACT.Ln), dve.last())
            dve.then(tt(lf, lf, t1, ALU.subtract), act.last())
            one_row = C2("ones")[0:4, :]
            for c in range(2):
                s = slice(c * P, (c + 1) * P)
                dve.then(lambda e, s=s: e.tensor_tensor_scan(bc[:, s], one_row, lf[:, s], 0.0, ALU.mult, ALU.add))
            dve.then(tt(Rr, li, bc, ALU.subtract))
            for c in range(2):
                s = slice(c * P, (c + 1) * P)
                init = 0.0 if c == 0 else mm_[:, P - 1:P]
                dve.then(lambda e, s=s, init=init: e.tensor_tensor_scan(pm[:, s], one_row, Rr[:, s], init,
                                                                        ALU.mult, ALU.max))
                dve.then(tt(mm_[:, s], bc[:, s], pm[:, s], ALU.add))
            act.run(af(emm, mm_, ACT.Exp, scale=-1.0), dve.last())
            dve.then(ts(t0[:, P:T], pm[:, P:T], -1.0, mm_[:, P - 1:P], ALU.mult, ALU.add))
            marks["rows"] = act.run(af(t0[:, P:T], t0[:, P:T], ACT.Exp), dve.last())
            bk = bank()
            pb = banks[bk]
            tok = tr_group(bk, [(pb[:, c * 4:c * 4 + 4], Rr[:, c * P:(c + 1) * P]) for c in range(2)], dve.last())
            dve.run(cp(Rc, pb[:, 0:8]), tok)
            free[bk] = [dve.last()]

        act.wait(*before2)
        dve.wait(*before2)
        gate_rows()

        def take2(n, pb, tok):
            if n < 4:
                marks["xc"] = act.run(af(xcT[:, n:n + 2, :], pb, ACT.Copy), tok)
            elif n < 6:
                marks["a"] = act.run(af(aT, pb, ACT.Copy), tok)
            elif n < 8:
                marks["g"] = act.run(af(gT, pb, ACT.Sigmoid), tok)
            elif n < 12:
                act.run(af(ocT[:, n - 8:n - 6, :], pb, ACT.Sigmoid), tok)
            else:
                act.run(af(uT, pb, ACT.Gelu), tok)
            return [act.last()]

        def conv(eng, dst, src, w, taps, *after):
            eng.then(ts(dst, src, w(taps - 1), None, ALU.mult), *after)
            for j in range(taps - 1):
                sft = taps - 1 - j
                eng.then(stt(dst[:, sft:T], src[:, 0:T - sft], w(j), dst[:, sft:T], ALU.mult, ALU.add))

        def standardise_T(src, n, meanmat, eps, out_, sq, ready):
            bk = bank()
            pb = banks[bk]
            tok = mm_group(bk, [(pb[:, 0:n], meanmat, src, True, True)], ready)
            d = dve.run(tt(out_, src, pb[:, 0:n], ALU.subtract), tok)
            free[bk] = [d]
            a = act.run(af(sq, out_, ACT.Square), d)
            yield
            bk = bank()
            pb = banks[bk]
            tok = mm_group(bk, [(pb[:, 0:n], meanmat, sq, True, True)], a)
            d = dve.run(ts(sq, pb[:, 0:n], eps, None, ALU.add), tok)
            free[bk] = [d]
            a = act.run(af(sq, sq, ACT.Sqrt), d)
            yield
            dve.run(lambda e: e.reciprocal(sq, sq), a)
            marks["std"] = dve.then(tt(out_, out_, sq, ALU.mult))

        def mixer_a():
            stg = small[:, 176:208]
            t_vg = marks["vg"]
            for b in range(TB):
                s = vg[:, b * 256:(b + 1) * 256]
                o = stg[:, 16 * b:16 * b + 16]
                dve.run(lambda e, s=s, o=o: e.bn_stats(o[:, 0:6], s), t_vg)
                dve.then(lambda e, o=o: e.bn_aggr(o[:, 6:8], o[:, 0:6]))
                dve.then(ts(o[:, 8:9], o[:, 7:8], LN_EPS, None, ALU.add))
                act.run(af(o[:, 8:9], o[:, 8:9], ACT.Sqrt), dve.last())
                dve.run(lambda e, o=o: e.reciprocal(o[:, 9:10], o[:, 8:9]), act.last())
                dve.then(ts(s, s, o[:, 6:7], o[:, 9:10], ALU.subtract, ALU.mult))
                dve.then(tt(s, s, C2("lng"), ALU.mult))
                dve.then(tt(s, s, C2("lnb"), ALU.add))
            yield
            bk = bank()
            pb = banks[bk]
            items = []
            for h in range(4):
                for b in range(TB):
                    o = (h // 2) * 256 + b * P
                    items.append((pb[64 * (h % 2):64 * (h % 2) + 64, o:o + P],
                                  vg[:, b * 256 + h * 64:b * 256 + h * 64 + 64], wsT[:, h * P:(h + 1) * P],
                                  True, True))
            tok = mm_group(bk, items, dve.last(), t_ws)
            bsv = t3(C2("bs"), 2)
            ya = t3(vg, 2)
            for b in range(TB):
                dve.run(tt(ya[:, :, b * P:(b + 1) * P], t3(pb[:, :], 2)[:, :, b * P:(b + 1) * P], bsv, ALU.add), tok)
            free[bk] = [dve.last()]
            dve.then(tt(ya, ya, uT, ALU.mult), marks["z"])
            parts([z[:, 0:2, :] for z in yT], ya, dve.last())
            yield

        def mixer_b():
            dve.run(tt(aT, aT, gT, ALU.mult), marks["g"], marks["a"])
            for j in range(2):
                o = conv_o[:, j * T:(j + 1) * T]
                w = lambda i, j=j: C2("cbw", 31 * j + i, 31 * j + i + 1)
                dve.then(ts(o, aT[:, j, :], w(30), C2("cbb", j, j + 1), ALU.mult, ALU.add))
                for i in range(30):
                    sft = 30 - i
                    dve.then(stt(o[:, sft:T], aT[:, j, 0:T - sft], w(i), o[:, sft:T], ALU.mult, ALU.add))
                    if i % 6 == 5:
                        yield
            yield from standardise_T(conv_o, 512, C2("mean64"), LN_EPS, conv_o, conv_p, dve.last())
            for j in range(2):
                act.run(af(conv_o[:, j * T:(j + 1) * T], conv_o[:, j * T:(j + 1) * T], ACT.Silu,
                           bias=C2("gnb", j, j + 1), scale=C2("gng", j, j + 1)), marks["std"])
            parts([z[:, 2:4, :] for z in yT], t3(conv_o, 2), act.last())
            yield

        def mixer_c():
            for j in range(4):
                conv(dve, hm[:, j * T:(j + 1) * T], xcT[:, j, :],
                     lambda i, j=j: C2("ccw", 4 * j + i, 4 * j + i + 1), 4, marks["xc"])
                t_xc = act.run(af(xcv[:, j, :], hm[:, j * T:(j + 1) * T], ACT.Silu, bias=C2("ccb", j, j + 1)),
                               dve.last())
                if j % 2:
                    yield
            for q, dst in enumerate([qTm, kTm]):
                for j in range(2):
                    bk = bank()
                    pb = banks[bk]
                    tok = mm_group(bk, [(pb[:, i * 256:(i + 1) * 256], wc[:, q, 2 * j + i, :], xcv[:, 2 * j + i, :],
                                         True, True) for i in range(2)], (s_w2c, 16), t_xc)
                    act.run(af(dst[:, 2 * j:2 * j + 2, :], t3(pb[:, :], 2), ACT.Copy,
                               scale=float(np.float32(P ** -0.5)) if q == 0 else 1.0), tok)
                    free[bk] = [act.last()]
            for b in range(TB):
                bk = bank()
                pb = banks[bk]
                tok = mm_group(bk, [(pb[:, h * P:(h + 1) * P], xcT[:, h, b * P:(b + 1) * P], wc[:, 2, h, :],
                                     True, True) for h in range(4)], t_xc)
                act.run(af(vnm[:, b * 512:(b + 1) * 512], pb[:, :], ACT.Copy), tok)
                free[bk] = [act.last()]
            bk = bank()
            pb = banks[bk]
            tok = mm_group(bk, [(pb[:, h * P:(h + 1) * P], xcv[:, h, 0:P], wc[:, 1, h, :], True, True)
                                for h in range(4)])
            act.run(af(knm, pb[:, :], ACT.Copy), tok)
            free[bk] = [act.last()]
            t_qkv = act.last()
            yield
            for h in range(4):
                selh = C2("sel", h * P, (h + 1) * P)[0:4, :]
                bk = bank()
                pb = banks[bk]
                tok = mm_group(bk, [(pb[:, 0:256], selh, pm, True, True),
                                    (pb[:, 256:384], selh, t0[:, P:T], True, True)], marks["rows"])
                t_prev = tok
                wt = wTm[:, 0:256]
                for c in range(2):
                    s = slice(c * P, (c + 1) * P)
                    d = dve.run(ts(wt[:, s], pb[:, s], Rc[:, 4 * c + h:4 * c + h + 1], 0.0, ALU.subtract, ALU.max),
                                tok, t_prev)
                winter = wTm[:, 256:384]
                a = act.run(af(wt, wt, ACT.Exp, scale=-1.0), d)
                dve.run(cp(winter, pb[:, 256:384]))
                free[bk] = [dve.last()]
                for c in range(2):
                    s = slice(c * P, (c + 1) * P)
                    dve.run(tt(wt[:, s], wt[:, s], C2("causal"), ALU.mult), a, dve.last())
                ksc = cm[:, 0:128]
                dve.then(ts(ksc, knm[:, h * P:(h + 1) * P], wt[:, P - 1:P], None, ALU.mult), t_qkv)
                qw = cm[:, 128:256]
                dve.run(tt(qw, qTm[:, h, P:T], winter, ALU.mult))
                t_kq = dve.last()
                yield
                bk = bank()
                pb = banks[bk]
                tok = mm_group(bk, [(pb[:, 0:P], ksc, vnm[:, h * P:(h + 1) * P], True, True),
                                    (pb[:, P:2 * P], ksc, C2("ones"), True, True)], t_kq)
                cn = cm[:, 256:512]
                dve.run(cp(cn, pb[:, 0:256]), tok)
                free[bk] = [dve.last()]
                bk = bank()
                pb = banks[bk]
                tok = mm_group(bk, [(pb[:, c * P:(c + 1) * P], kTm[:, h, c * P:(c + 1) * P],
                                     qTm[:, h, c * P:(c + 1) * P], True, True) for c in range(2)])
                dve.run(tt(wt, wt, pb[:, 0:256], ALU.mult), tok)
                free[bk] = [dve.last()]
                t_wt = dve.last()
                yield
                bk = bank()
                pb = banks[bk]
                items = []
                for c in range(2):
                    s = slice(c * P, (c + 1) * P)
                    s2 = slice(256 + c * P, 256 + (c + 1) * P)
                    items.append((pb[:, s], vnm[:, c * 512 + h * P:c * 512 + (h + 1) * P], wt[:, s], True, c == 0))
                    if c:
                        items.append((pb[:, s], cn[:, 0:P], qw, False, True))
                    items.append((pb[:, s2], C2("ones"), wt[:, s], True, c == 0))
                    if c:
                        items.append((pb[:, s2], cn[:, P:2 * P], qw, False, True))
                tok = mm_group(bk, items, t_wt)
                bk2 = bank()
                pb2 = banks[bk2]
                tok2 = mm_group(bk2, [(pb2[:, 0:256], selh, emm, True, True)])
                den = den_t
                dve.run(ts(den, pb[:, 256:512], -1.0, None, ALU.mult), tok)
                dve.then(tt(den, den, pb[:, 256:512], ALU.max))
                dve.then(tt(den, den, pb2[:, 0:256], ALU.max), tok2)
                free[bk2] = [dve.last()]
                dve.then(lambda e: e.reciprocal(den, den))
                dve.then(tt(hm[:, h * T:(h + 1) * T], pb[:, 0:256], den, ALU.mult))
                free[bk] = [dve.last()]
                yield
            for j in range(2):
                yield from standardise_T(hm[:, j * 512:(j + 1) * 512], 512, C2("mean128"), LN_EPS,
                                         hm[:, j * 512:(j + 1) * 512], hm2[:, j * 512:(j + 1) * 512], dve.last())
            for h in range(4):
                o = hm[:, h * T:(h + 1) * T]
                o2 = hm2[:, h * T:(h + 1) * T]
                dve.then(ts(o2, xcv[:, h, :], C2("skip", h, h + 1), None, ALU.mult))
                dve.then(stt(o2, o, C2("hng", h, h + 1), o2, ALU.mult, ALU.add))
                dve.then(tt(o2, o2, ocT[:, h, :], ALU.mult))
            parts([z[:, 4:8, :] for z in yT], t3(hm2, 4), dve.last())
            yield

        lin_T("w2_t", hTv, KD, [], take2, 4)
        side.append(mixer_c())
        lin_T("w2_t", hTv, KD, [], lambda n, pb, tok: take2(n + 4, pb, tok), 10)
        marks["z"] = act.last()
        for b_ in [bank()]:
            pb = banks[b_]
            for i in range(2):
                w, there = take("w2_v")
                wv = [t3(z, 4) for z in w]
                items = []
                for b in range(TB):
                    for k in range(4):
                        items += three(pb[:, b * 256:(b + 1) * 256],
                                       [z[:, 4 * i + k, b * P:(b + 1) * P] for z in hTv], [z[:, k, :] for z in wv],
                                       i == 0 and k == 0 and b == 0, i == 1 and k == 3)
                tok = mm_group(b_, items, *there)
                release(tok)
            marks["vg"] = act.run(af(vg, pb[:, :], ACT.Gelu), tok)
            free[b_] = [marks["vg"]]
        t_mT = norm_to_T(memx, "g_mem2", mT, mscr, (s_mem, 32))
        side.append(mixer_b())
        side.append(mixer_a())

        def to(dst):
            def f(n, pb, tok):
                return [act.run(af(dst[:, n:n + 2, :], pb, ACT.Copy), tok)]
            return f

        lin_T("w_xk", mT, KD, [t_mT], to(kT2), 8, steps=2)
        tok = lin_A("w_xv", mT, KD, D, [], steps=2)
        for b in range(TB):
            for h in range(2):
                act.run(af(v2[:, b * D + h * 512:b * D + (h + 1) * 512], banks[2 * b + h][:, :], ACT.Copy), tok)
                free[2 * b + h] = [act.last()]
        drain()
        tok = lin_A("w2_out", yT, KD, D, [dve.last(), act.last()])
        t_x = add_residual(tok, xres, xres)

        done = all_done()
        xs = a3(4096, 2048)
        qT2 = t3(a3(6144, 2048), 8)
        p2 = a3(8192, 1024)
        pT2 = a3(9216, 2048)
        oT2 = yT
        t_h = norm_to_T(xres, "g_x2", hTv, xs, t_x, *done)
        lin_T("w_xq", hTv, KD, [t_h], to(qT2), 8)
        t_kvq = act.last()
        sx = small[:, 224:236]
        Pv = t3(p2, 4)
        pTv = pT2.rearrange("p (a h t) -> p a h t", a=2, h=4)
        t_pT = pe.last()
        for b in range(TB):
            for h2 in range(2):
                bk = bank()
                pb = banks[bk]
                tok = mm_group(bk, [(pb[:, q * 256:(q + 1) * 256], qT2[:, 2 * (2 * h2 + q) + k, b * P:(b + 1) * P],
                                     kT2[:, 2 * (2 * h2 + q) + k, :], k == 0, k == 1)
                                    for q in range(2) for k in range(2)], t_kvq)
                dve.run(ts(Pv[:, 2 * h2:2 * h2 + 2, :], t3(pb[:, :], 2), 1.0 / 16.0, None, ALU.mult), tok, t_pT)
                free[bk] = [dve.last()]
            mx, sm_, rc = sx[:, 0:4], sx[:, 4:8], sx[:, 8:12]
            dve.then(lambda e: e.tensor_reduce(mx, Pv, AX, ALU.max))
            dve.then(tt(Pv, Pv, mx.unsqueeze(2).to_broadcast([P, 4, 256]), ALU.subtract))
            act.run(af(p2, p2, ACT.Exp), dve.last())
            dve.then(lambda e: e.tensor_reduce(sm_, Pv, AX, ALU.add), act.last())
            dve.then(lambda e: e.reciprocal(rc, sm_))
            dve.then(tt(Pv, Pv, rc.unsqueeze(2).to_broadcast([P, 4, 256]), ALU.mult))
            for a in range(2):
                bk = bank()
                pb = banks[bk]
                t_pT = tr_group(bk, [(pb[:, h * P:(h + 1) * P], Pv[:, h, a * P:(a + 1) * P]) for h in range(4)],
                                dve.last())
                act.run(af(pTv[:, a, :, b * P:(b + 1) * P], t3(pb[:, :], 4), ACT.Copy), t_pT)
                free[bk] = [act.last()]
        t_p = act.last()
        for h in range(4):
            bk = bank()
            pb = banks[bk]
            tok = mm_group(bk, [(pb[:, j * 256:(j + 1) * 256],
                                 v2[:, a * D + (2 * h + j) * P:a * D + (2 * h + j + 1) * P],
                                 pTv[:, a, h, :], a == 0, a == 1) for j in range(2) for a in range(2)], t_p)
            parts([z[:, 2 * h:2 * h + 2, :] for z in oT2], t3(pb[:, :], 2), tok)
            free[bk] = [dve.last()]
        tok = lin_A("w_xo", oT2, KD, D, [dve.last()])
        t_x = add_residual(tok, xres, xres)

        done = all_done()
        xs = A4[:, 0:2048]
        gF = A4[:, 2048:3072]
        cF = A4[:, 3072:4096]
        gfin2 = A4[:, 4096:5120]
        aF = two((R4[0][:, :], R4[1][:, :]), 22)
        load(s_gf2, gfin2, gf2_d.partition_broadcast(P), *done)
        t_h = norm_to_T(xres, "g_ffn2", hTv, xs, t_x, *done)

        t_ffn = []

        def ffn(n, pb, tok):
            j = n // 2
            s = (j % 4) * T
            g, c = gF[:, s:s + T], cF[:, s:s + T]
            before = [t_ffn[j - 4]] if j >= 4 else []
            a = act.run(af(g, pb[:, 0, :], ACT.Copy), tok, *before)
            conv(dve, c, g, lambda i: K_("cfw", 3 * j + i, 3 * j + i + 1), 3, a)
            a = act.run(af(g, c, ACT.Gelu, bias=K_("cfb", j, j + 1)), dve.last())
            d = dve.run(tt(c, g, pb[:, 1, :], ALU.mult), a)
            t_ffn.append(parts([z[:, j, :] for z in aF], c, d))
            return [d]

        lin_T("w_up", hTv, KD, [t_h], ffn, 44)
        tok = lin_A("w_down", aF, 22, D, [dve.last()])
        t_x = add_residual(tok, xres, xres)
        t_x = final_norm(gfin2, xs, t_x, (s_gf2, 16))
        for b in range(TB):
            load(s_out, out[b * P:(b + 1) * P, :], xres[:, b * D:(b + 1) * D], t_x[b])
        sp.work.append(lambda e: e.wait_ge(s_out, 32))
        assert taken[0] == len(units) == cut[0]

        block = ctx.enter_context(nc.Block())

        @block.sync
        def _(e):
            sp.emit(e)

        @block.tensor
        def _(e):
            pe.emit(e)

        @block.vector
        def _(e):
            dve.emit(e)

        @block.scalar
        def _(e):
            act.emit(e)

        @block.gpsimd
        def _(e):
            pool.emit(e)


def fill(table, n, values):
    c = np.zeros((P, n), np.float32)
    for name, a in values.items():
        o, w = table[name]
        c[0:a.shape[0], o:o + w] = a
    return c


def shape_constants():
    i = np.arange(P)
    dist = i[:, None] + P - np.arange(256)[None, :]
    causal = i[:, None] <= i[None, :]
    sel = np.zeros((4, 4, P), np.float32)
    for h in range(4):
        sel[h, h] = 1.0
    return {
        "ident": np.eye(P), "mean128": np.full((P, P), 1.0 / 128),
        "mean64": (i[:, None] // 64 == i[None, :] // 64) / 64.0, "ones": np.ones((P, P)), "dist": dist,
        "wmask": np.where((dist >= 0) & (dist < P), 0.0, NEG),
        "hmask": causal & (i[:, None] // 32 == i[None, :] // 32), "causal": causal, "sel": sel.reshape(4, 512),
        "iota": np.broadcast_to(np.arange(P), (P, P)), "iota16": np.broadcast_to(np.arange(16), (P, 16)),
        "reset": np.broadcast_to(np.arange(1024) % 32 != 0, (P, 1024)),
    }


def tiles_T(w):
    K, N = w.shape[0] // P, w.shape[1] // P
    per = UNIT // (K * P)
    a = w.reshape(K, P, N, P).transpose(2, 1, 0, 3)
    return np.ascontiguousarray(a.reshape(N // per, per, P, K * P).transpose(0, 2, 1, 3).reshape(N // per, P, -1))


def tiles_A(w):
    K, N = w.shape[0] // P, w.shape[1]
    per = UNIT // N
    return np.ascontiguousarray(w.reshape(K // per, per, P, N).transpose(0, 2, 1, 3).reshape(K // per, P, per * N))


def cols(v, n):
    return np.asarray(v).reshape(n, P).T


def rep(v):
    return np.broadcast_to(v, (P, v.shape[-1]))


def layout(a):
    w = a["w_in"][0]
    heads = [c for j in range(4) for h in (j, j + 4) for c in range(h * 64, h * 64 + 64)]
    s = {}
    s["w_in_t"] = tiles_T(np.concatenate([w[:, heads], w[:, 512:1792], w[:, 2304:2816]], 1))
    s["w_in_hi"] = tiles_A(w[:, 1792:2304])
    s["w_in_g"] = tiles_T(w[:, 2816:4864])
    s["w_ap"] = tiles_T(a["w_attn_proj"][0][heads])
    s["w_hp"] = tiles_T(a["w_hgrn_proj"][0])
    s["w_out"] = tiles_A(a["w_out"][0])
    s["w_pq"] = tiles_T(a["w_peer_q"][0])
    u = a["peer_u"][0].reshape(P, P, KD, P)
    s["u"] = np.ascontiguousarray(u.transpose(1, 3, 2, 0).reshape(P, P, 1024))
    s["v"] = np.ascontiguousarray(a["peer_v"][0].reshape(P, P, 1024).transpose(1, 0, 2))
    w2 = a["w_in_2"][0]
    s["w2_t"] = tiles_T(np.concatenate([w2[:, 1024:1536], w2[:, 512:1024], w2[:, 1536:2048], w2[:, 0:256]], 1))
    s["w2_v"] = tiles_A(w2[:, 256:512])
    s["w2_out"] = tiles_A(a["w_out_2"][0])
    s["w_xk"] = tiles_T(a["w_xkv_2"][0][:, 0:D])
    s["w_xv"] = tiles_A(a["w_xkv_2"][0][:, D:2 * D])
    s["w_xq"] = tiles_T(a["w_xq_2"][0])
    s["w_xo"] = tiles_A(a["w_xo_2"][0])
    up = tiles_T(a["w_up_2"][0])
    s["w_up"] = np.ascontiguousarray(up.reshape(2, 22, P, UNIT).transpose(1, 0, 2, 3).reshape(44, P, UNIT))
    s["w_down"] = tiles_A(a["w_down_2"][0])

    c = shape_constants()
    v = {
        "g_mix": cols(a["norm_mix_g"], 8), "g_ffn": cols(a["norm_ffn_g"], 8), "g_mix2": cols(a["norm_mix_g_2"], 8),
        "g_x2": cols(a["norm_x_g_2"], 8), "g_mem2": cols(a["norm_mem_g_2"], 8), "g_ffn2": cols(a["norm_ffn_g_2"], 8),
        "lb": cols(a["hgrn_lb_logits"], 8), "g_hgrn": cols(a["hgrn_norm_g"], 1),
        "cbw": a["conv_b_w_2"][0].reshape(31, 2, P).transpose(2, 1, 0).reshape(P, 62),
        "cbb": cols(a["conv_b_b_2"], 2), "gng": cols(a["gn_b_g_2"], 2), "gnb": cols(a["gn_b_b_2"], 2),
        "ccw": a["conv_c_w_2"][0].reshape(4, 4, P).transpose(2, 1, 0).reshape(P, 16),
        "ccb": cols(a["conv_c_b_2"], 4), "hng": cols(a["hn_c_g_2"], 4), "skip": cols(a["skip_c_2"], 4),
        "cfw": a["conv_f_w_2"][0].reshape(3, 22, P).transpose(2, 1, 0).reshape(P, 66),
        "cfb": cols(a["conv_f_b_2"], 22), "bi": a["b_igate_2"].reshape(4, 1), "bf": a["b_fgate_2"].reshape(4, 1),
        "bs": np.broadcast_to(a["b_s_2"][0].reshape(2, 2, 1, P), (2, 2, 64, P)).transpose(1, 2, 0, 3).reshape(P, 256),
        "wgate": w2[:, 2048:2056].reshape(KD, P, 8).transpose(1, 0, 2).reshape(P, 64),
        "wsT": a["w_s_2"][0].transpose(2, 0, 1).reshape(P, 512),
        "lng": rep(a["ln_a_g_2"]), "lnb": rep(a["ln_a_b_2"]), "sinks": rep(a["attn_sinks"]),
    }
    v.update(c)
    o = {}
    for name, table, off, n in (("keep", KEEP, KOFF, NKEEP), ("con0", CON0, OFF0, NCON0), ("con1", CON1, OFF1, NCON1),
                                ("con2", CON2, OFF2, NCON2)):
        o[name] = fill(off, n, {k: v[k] for k, _ in table})
    o["keys"] = np.ascontiguousarray(a["peer_keys"][0].transpose(3, 1, 0, 2).reshape(P, 2048))
    o["w2c"] = np.concatenate([a[n][0].transpose(1, 0, 2).reshape(P, 512)
                               for n in ("w_q_c_2", "w_k_c_2", "w_v_c_2")], 1)
    o["gf"] = a["norm_final_g"]
    o["gf2"] = a["final_g_2"]
    return s, o


def kernel(**inputs):
    import numpy as _np
    import concourse.bacc as _bacc
    from concourse import mybir as _mybir
    from concourse.bass_utils import run_bass_kernel_spmd as _run

    a = {k: _np.asarray(v) for k, v in inputs.items()}
    s, o = layout(a)
    nc = _bacc.Bacc("TRN2", target_bir_lowering=False, num_devices=1)
    arrays = {"x": _np.ascontiguousarray(a["x"][0]), "mem": _np.ascontiguousarray(a["mem_2"][0])}
    arrays.update(o)
    arrays.update(s)
    aps = {k: nc.dram_tensor(f"in_{k}", list(z.shape), _mybir.dt.float32, kind="ExternalInput").ap()
           for k, z in arrays.items()}
    out = nc.dram_tensor("out", [T, D], _mybir.dt.float32, kind="ExternalOutput").ap()
    build(nc, aps["x"], aps["mem"], {k: aps[k] for k in s}, aps["keep"], aps["con0"], aps["con1"], aps["con2"],
          aps["keys"], aps["w2c"], aps["gf"], aps["gf2"], out)
    r = _run(nc, [{f"in_{k}": z for k, z in arrays.items()}], core_ids=[0])
    return r.results[0]["out"].reshape(1, T, D)
```

```python
from contextlib import ExitStack

import numpy as np

import concourse.bass as bass
from concourse import mybir

ALU = mybir.AluOpType
ACT = mybir.ActivationFunctionType
F32 = mybir.dt.float32
F32R = mybir.dt.float32r
BF16 = mybir.dt.bfloat16
U32 = mybir.dt.uint32
I32 = mybir.dt.int32
AX = mybir.AxisListType.X

P = 128
D = 1024
T = 256
TB = 2
KD = D // P
DFF = 2816
EPS = 1e-6
LN_EPS = 1e-5
NEG = -1e30

UNIT = 1024
NRAW = 4
NSPL = 3
OB = 4

STREAMS = [
    ("w_in_t", 18),
    ("w_in_hi", 4),
    ("w_in_g", 16),
    ("w_ap", 4),
    ("w_hp", 4),
    ("w_out", 8),
    ("w_pq", 16),
    ("u", 128),
    ("v", 128),
    ("w_xk", 6),
    ("w2_t", 8),
    ("w2_v", 2),
    ("w2_u", 2),
    ("w_xv", 8),
    ("w2_o", 4),
    ("w2_out", 8),
    ("w_xk2", 2),
    ("w_xq", 8),
    ("w_xo", 8),
    ("w_up", 44),
    ("w_down", 22),
]

KEEP = [
    ("ident", 128), ("iota", 128), ("iota16", 16),
    ("g_mix", 8), ("g_ffn", 8), ("g_mix2", 8), ("g_x2", 8), ("g_mem2", 8), ("g_ffn2", 8),
    ("cfw", 66), ("cfb", 22),
]
CON1 = [("hmask", 128), ("mean128", 128), ("reset", 1024), ("lb", 8), ("g_hgrn", 1), ("sinks", 8)]
CON0 = [("dist", 256), ("wmask", 256)]
CON2 = [
    ("mean64", 128), ("mean128", 128), ("ones", 128), ("causal", 128), ("sel", 512), ("lng", 256), ("lnb", 256),
    ("wsT", 512), ("bs", 256), ("wgate", 288), ("cbw", 62), ("cbb", 2), ("gng", 2), ("gnb", 2), ("ccw", 16),
    ("ccb", 4), ("hng", 4), ("skip", 4), ("bi", 1), ("bf", 1),
]


def offsets(table):
    at, out = 0, {}
    for name, n in table:
        out[name] = (at, n)
        at += n
    return out, at


KOFF, NKEEP = offsets(KEEP)
OFF0, NCON0 = offsets(CON0)
OFF1, NCON1 = offsets(CON1)
OFF2, NCON2 = offsets(CON2)


class Engine:

    def __init__(self, name, sem):
        self.name, self.sem = name, sem
        self.count = 0
        self.work = []
        self.seen = {}

    def last(self):
        return (self.sem, self.count)

    def wait(self, *after):
        for sem, value in after:
            if value > self.seen.get(id(sem), 0):
                self.seen[id(sem)] = value
                self.work.append(lambda e, s=sem, v=value: e.wait_ge(s, v))

    def run(self, fn, *after):
        self.wait(*after)
        self.count += 1
        self.work.append(lambda e, f=fn, s=self.sem: f(e).then_inc(s, 1))
        return (self.sem, self.count)

    def then(self, fn, *after):
        return self.run(fn, self.last(), *after)

    def emit(self, eng):
        for f in self.work:
            f(eng)


def build(nc, x, mem, wdram, keep_d, con0_d, con1_d, con2_d, keys_d, w2c_d, gf_d, gf2_d, out):
    ctx = ExitStack()
    with ctx:
        def sb(name, n, dt=F32, c=ctx):
            return c.enter_context(nc.sbuf_tensor(name, [P, n], dt))

        def sem(name):
            return ctx.enter_context(nc.semaphore(name))

        banks = [ctx.enter_context(nc.psum_tensor(f"bank{i}", [P, 512], F32)) for i in range(8)]
        raw = [sb(f"raw{i}", UNIT) for i in range(NRAW)]
        whi = [sb(f"whi{i}", UNIT, F32R) for i in range(NSPL)]
        wlo = [sb(f"wlo{i}", UNIT, F32R) for i in range(NSPL)]
        keep = sb("keep", NKEEP)
        xres = sb("xres", 2048)
        hTh = sb("hTh", 2048, F32R)
        hTl = sb("hTl", 2048, F32R)
        small = sb("small", 256)
        iT = sb("iT", 3 * T)
        oh1 = sb("oh1", 2 * OB * P, BF16)
        wgp = (sb("wgh", 8 * 36, F32R), sb("wgl", 8 * 36, F32R))
        og_eq = sb("og_eq", OB * 64, BF16)
        og = sb("og", 2 * 3 * OB * 64, BF16)
        gate3 = sb("gate3", 3 * T, BF16)
        col_b = sb("col_b", T, BF16)
        iota_b = sb("iota_b", P, BF16)
        with ExitStack() as c:
            A1 = sb("A1", 24576, c=c)
            R1 = (sb("R1h", 4096, F32R, c), sb("R1l", 4096, F32R, c))
        with ExitStack() as c:
            A2 = sb("A2", 32768, c=c)
        with ExitStack() as c:
            R3 = (sb("R3h", 4096, F32R, c), sb("R3l", 4096, F32R, c))
            A3 = sb("A3", 24576, c=c)
        A4 = sb("A4", 8192)
        R4 = (sb("R4h", 5632, F32R), sb("R4l", 5632, F32R))

        pe = Engine("pe", sem("s_pe"))
        dve = Engine("dve", sem("s_dve"))
        act = Engine("act", sem("s_act"))
        pool = Engine("pool", sem("s_pool"))
        sp = Engine("sp", sem("s_sp"))
        s_raw = [sem(f"s_raw{i}") for i in range(NRAW)]
        s_in, s_in2, s_keep, s_con0, s_con1, s_con2, s_keys, s_w2c, s_gf, s_gf2, s_mem, s_out = (
            sem(n) for n in ("s_in", "s_in2", "s_keep", "s_con0", "s_con1", "s_con2", "s_keys", "s_w2c", "s_gf", "s_gf2",
                             "s_mem", "s_out"))

        def pick(tile, at, table):
            def f(name, a=0, b=None):
                o, n = table[name]
                return tile[:, at + o + a:at + o + (n if b is None else b)]
            return f

        K_ = pick(keep, 0, KOFF)

        def all_done():
            return [pe.last(), dve.last(), act.last(), pool.last()]

        def load(s, dst, src, *after):
            sp.wait(*after)
            sp.work.append(lambda e: e.dma_start(dst, src).then_inc(s, 16))

        units = [(name, i) for name, k in STREAMS for i in range(k)]
        fetched, cut, taken = [0], [0], [0]
        lo_done, hi_done, used = {}, {}, {}
        pool_of = [0]

        def fetch():
            i = fetched[0]
            if i >= len(units):
                return
            fetched[0] += 1
            name, k = units[i]
            if i >= NRAW:
                sp.wait(lo_done[i - NRAW])
            dst, src, s = raw[i % NRAW][:, :], wdram[name][k], s_raw[i % NRAW]
            sp.work.append(lambda e: e.dma_start(dst, src).then_inc(s, 16))

        def divide():
            i = cut[0]
            if i >= len(units):
                return
            cut[0] += 1
            r, h, l = raw[i % NRAW][:, :], whi[i % NSPL][:, :], wlo[i % NSPL][:, :]
            landed = (s_raw[i % NRAW], 16 * (i // NRAW + 1))
            before = [used[i - NSPL]] if i >= NSPL else []
            hi_done[i] = act.run(af(h, r, ACT.Copy), landed, *before)
            eng = pool if pool_of[0] and i % pool_of[0] == pool_of[0] - 1 else dve
            lo_done[i] = eng.run(tt(l, r, h.bitcast(F32), ALU.subtract), hi_done[i])
            fetch()

        def ahead(n):
            while cut[0] < min(taken[0] + n, len(units)) and (cut[0] < NSPL or cut[0] - NSPL in used):
                divide()

        def take(name):
            i = taken[0]
            taken[0] += 1
            assert units[i][0] == name, (units[i], name)
            ahead(NSPL - 1)
            return (whi[i % NSPL][:, :], wlo[i % NSPL][:, :]), [hi_done[i], lo_done[i]]

        def release(token, n=1):
            for i in range(n):
                used[taken[0] - 1 - i] = token

        free = [[] for _ in range(8)]
        turn = [0]

        held = set()

        def bank():
            while 4 + turn[0] % 4 in held:
                turn[0] += 1
            b = 4 + turn[0] % 4
            turn[0] += 1
            return b

        def products(items):
            def go(e):
                for o, l, r, st, sp_ in items:
                    ins = e.matmul(o, l, r, start=st, stop=sp_, skip_group_check=True)
                return ins
            return go

        def mm_group(b, items, *after):
            waits = list(after) + free[b]
            free[b] = []
            return pe.run(products(items), *waits)

        def tr_group(b, items, *after):
            waits = list(after) + free[b]
            free[b] = []

            def go(e):
                for o, i in items:
                    k = i.shape[0]
                    ins = e.transpose(o, i, K_("ident")[0:k, 0:k])
                return ins

            return pe.run(go, *waits)

        def three(o, a, b, start, stop):
            return [(o, a[0], b[0], start, False), (o, a[0], b[1], False, False), (o, a[1], b[0], False, stop)]

        def ts(o, i, s1, s2, op0, op1=ALU.bypass):
            if s2 is None:
                return lambda e: e.tensor_scalar(o, i, s1, None, op0)
            return lambda e: e.tensor_scalar(o, i, s1, s2, op0, op1)

        def tt(o, a, b, op):
            return lambda e: e.tensor_tensor(o, a, b, op)

        def stt(o, a, s, b, op0, op1):
            return lambda e: e.scalar_tensor_tensor(o, a, s, b, op0, op1)

        def af(o, i, func, bias=None, scale=None, accum=None):
            kw = {}
            if bias is not None:
                kw["bias"] = bias
            if scale is not None:
                kw["scale"] = scale
            if accum is not None:
                kw["accum_out"] = accum
            return lambda e: e.activation(o, i, func, **kw)

        def cp(o, i):
            return lambda e: e.tensor_copy(o, i)

        def t3(ap, a):
            return ap.rearrange("p (a b) -> p a b", a=a)

        def t4(ap, a, b):
            return ap.rearrange("p (a b c) -> p a b c", a=a, b=b)

        def parts(dst, src, *after):
            h = act.run(af(dst[0], src, ACT.Copy), *after)
            return dve.run(tt(dst[1], src, dst[0].bitcast(F32), ALU.subtract), h)

        def two(ap, n):
            return [t3(a, n) for a in ap]

        def sub(ap, a, b):
            return [z[:, a:b] for z in ap]

        hTv = (t3(hTh[:, :], KD), t3(hTl[:, :], KD))

        side, side_b, side_c, side_d = [], [], [], []
        lists, later, unit_no = [side, side_d, side_c, side_b], [], [0]

        def step(n=1):
            unit_no[0] += 1
            for due in [z for z in later if z[0] <= unit_no[0]]:
                later.remove(due)
                due[1]()
            for _ in range(n):
                for z in lists:
                    went = False
                    while z and not went:
                        try:
                            next(z[0])
                            went = True
                        except StopIteration:
                            z.pop(0)

        def drain():
            while any(lists):
                step()

        normed = {}
        t_half = pool.run(lambda e: e.memset(small[:, 250:251], -0.5))

        def squares(src, b, h, scratch, *after):
            o = b * D + h * 512
            return act.run(af(scratch[:, o:o + 512], src[:, o:o + 512], ACT.Square, scale=float(D ** -0.5),
                              accum=small[:, 4 * b + h:4 * b + h + 1]), *after)

        def inv_rms(b, *after):
            st = small[:, 4 * b:4 * b + 4]
            d = dve.run(ts(st[:, 3:4], st[:, 0:1], st[:, 1:2], EPS, ALU.add, ALU.add), *after)
            return pool.run(tt(st[:, 2:3], st[:, 3:4], small[:, 250:251], ALU.pow), d, t_half)

        def norm_to_T(src, gname, dst, scratch, sums, bks=(0, 1, 2, 3), early=2):
            g = norm_steps(src, gname, dst, scratch, sums, bks, 1, early)
            for _ in g:
                pass
            return normed[gname]

        def norm_steps(src, gname, dst, scratch, sums, bks, pause=1, early=0, slow=False):
            ready = []
            for b in range(TB):
                t = inv_rms(b, sums[b])
                for c in range(4):
                    o = b * D + c * 256
                    ready.append(dve.run(ts(scratch[:, o:o + 256], src[:, o:o + 256], small[:, 4 * b + 2:4 * b + 3],
                                            None, ALU.mult), t))
                if slow:
                    yield
            for _ in range(pause):
                yield
            for b in range(TB):
                toks = []
                for k2 in range(4):
                    toks.append(tr_group(bks[k2], [(banks[bks[k2]][:, (kk * 2 + b) * P:(kk * 2 + b + 1) * P],
                                                    scratch[:, b * D + (2 * k2 + kk) * P:b * D + (2 * k2 + kk + 1) * P])
                                                   for kk in range(2)], ready[4 * b + k2]))
            yield
            out_ = []
            if early:
                ahead(early)
            for k2 in range(4):
                pb = banks[bks[k2]]
                ks = [(dst[0][:, 2 * k2 + kk, :], dst[1][:, 2 * k2 + kk, :], pb[:, kk * 256:(kk + 1) * 256],
                       K_(gname, 2 * k2 + kk, 2 * k2 + kk + 1)) for kk in range(2)]
                for hi, lo, p_, g in ks:
                    h = act.run(af(hi, p_, ACT.Copy, scale=g), toks[k2])
                for hi, lo, p_, g in ks:
                    dve.run(stt(lo, p_, g, hi.bitcast(F32), ALU.mult, ALU.subtract), h)
                free[bks[k2]] = [dve.last()]
                out_.append(dve.last())
                if slow:
                    yield
            normed[gname] = out_

        def lin_T(name, src, K, ready, consume, n_tiles, steps=(1,)):
            per = UNIT // (K * P)
            n, tok = 0, None
            items, waits = [], []
            while n < n_tiles:
                w, there = take(name)
                wv = [z.rearrange("p (n k c) -> p n k c", n=per, k=K) for z in w]
                for j in range(per):
                    if n % 2 == 0:
                        bk = bank()
                        held.add(bk)
                        pb = banks[bk]
                    o = pb[:, (n % 2) * 256:(n % 2 + 1) * 256]
                    items = []
                    cuts = len(ready) if n == 0 and ready else 1
                    for k in range(K):
                        items += three(o, [z[:, j, k, :] for z in wv], [z[:, k, :] for z in src], k == 0, k == K - 1)
                        if (k + 1) % (K // cuts) == 0:
                            tok = mm_group(bk, items, *there, *(ready[k // (K // cuts):][:1]))
                            items = []
                    if n % 2:
                        free[bk] = consume(n - 1, t3(pb[:, :], 2), tok)
                        held.discard(bk)
                    n += 1
                release(tok)
                step(steps[taken[0] % len(steps)])

        def lin_A(name, src, K, N, ready, steps=(1,)):
            per = UNIT // N
            nh = N // 512
            after = [t for i in range(TB * nh) for t in free[i]]
            blocks, waits = [[], []], list(after)
            for k0 in range(0, K, per):
                waits += ready(k0) if callable(ready) else ready
                w, there = take(name)
                wv = [t3(z, per) for z in w]
                waits += there
                for b in range(TB):
                    for kk in range(per):
                        k = k0 + kk
                        for h in range(nh):
                            blocks[b] += three(banks[b * nh + h][:, :], [z[:, k, b * P:(b + 1) * P] for z in src],
                                               [z[:, kk, h * 512:(h + 1) * 512] for z in wv], k == 0, k == K - 1)
                if k0 + 2 * per == K:
                    continue
                if k0 + per == K:
                    toks = [pe.run(products(blocks[b]), *waits) for b in range(TB)]
                    release(toks[1], 2)
                else:
                    release(pe.run(products(blocks[0] + blocks[1]), *waits))
                blocks, waits = [[], []], []
                step(steps[taken[0] % len(steps)])
            return toks

        def add_residual(toks, scratch, *after):
            sums = []
            for b in range(TB):
                for h in range(2):
                    o = b * D + h * 512
                    d = dve.run(tt(xres[:, o:o + 512], banks[2 * b + h][:, :], xres[:, o:o + 512], ALU.add), toks[b])
                    free[2 * b + h] = [d]
                    a = squares(xres, b, h, scratch, d, *after)
                sums.append(a)
            return sums

        def a1(at, n):
            return A1[:, at:at + n]

        aqT = t3(a1(0, 1280), 5)
        av = a1(1280, 256)
        q_s = a1(1536, 1024)
        f_s = a1(2560, 1024)
        hg_s = a1(3584, 1024)
        hi_s = a1(4608, 1024)
        scr = a1(5632, 2048)
        bias8 = a1(7680, 2048)
        S_s = a1(9728, 2048)
        S_e = a1(11776, 2048)
        pT = a1(13824, 2048)
        h_S = a1(15872, 4096)
        ga = t3(a1(19968, 2048), 8)
        c0_at = 19968
        c1_at = 22016
        gh_at = 7680
        h_b = a1(9728, 1024)
        h_kinv = a1(10752, 1024)
        h_kd = a1(11776, 1024)
        h_kdn = a1(12800, 1024)
        h_AT = a1(13824, 1024)
        h_sq = a1(14848, 1024)
        gh = t3(a1(gh_at, 2048), 8)
        yaT = two(sub(R1, 0, 1024), 4)
        yhT = two(sub(R1, 1024, 2048), 4)
        mrg = two(sub(R1, 2048, 4096), 8)
        C0 = pick(A1, c0_at, OFF0)
        C1 = pick(A1, c1_at, OFF1)
        assert c1_at + NCON1 <= 24576

        load(s_in, xres[:, 0:D], x[0:P, :])
        load(s_in2, xres[:, D:2 * D], x[P:2 * P, :])
        load(s_keep, keep[:, :], keep_d)
        for _ in range(2):
            fetch()
        load(s_con0, A1[:, c0_at:c0_at + NCON0], con0_d)
        load(s_con1, A1[:, c1_at:c1_at + NCON1], con1_d)
        for _ in range(NRAW - 2):
            fetch()

        dve.wait((s_in, 16), (s_in2, 16))
        pe.wait((s_keep, 16))
        dve.wait((s_keep, 16))
        x_sums = []
        for b, landed in enumerate([(s_in, 16), (s_in2, 16)]):
            for h in range(2):
                t_sq = squares(xres, b, h, scr, landed)
            x_sums.append(t_sq)
        act.wait((s_keep, 16))
        t_h = norm_to_T(xres, "g_mix", hTv, scr, x_sums)

        for h in range(8):
            slope = float(np.float32(2.0 ** (-(h + 1))))
            t_bias = pool.run(ts(bias8[:, h * 256:(h + 1) * 256], C0("dist"), -slope, None, ALU.mult), (s_con0, 16))
        for h in range(8):
            t_bias = pool.run(tt(bias8[:, h * 256:(h + 1) * 256], bias8[:, h * 256:(h + 1) * 256], C0("wmask"),
                                 ALU.add), t_bias)

        lbv = small[:, 16:20]
        omlb = small[:, 20:24]
        l0, l1 = C1("lb", 0, 4), C1("lb", 4, 8)
        sm = small[:, 24:48]
        dve.then(tt(sm[:, 0:4], l0, l1, ALU.max), (s_con1, 16))
        dve.then(tt(sm[:, 4:8], l0, sm[:, 0:4], ALU.subtract))
        dve.then(tt(sm[:, 8:12], l1, sm[:, 0:4], ALU.subtract))
        act.then(af(sm[:, 12:20], sm[:, 4:12], ACT.Exp), dve.last())
        dve.then(tt(sm[:, 0:4], sm[:, 12:16], sm[:, 16:20], ALU.add), act.last())
        dve.then(lambda e: e.reciprocal(sm[:, 4:8], sm[:, 0:4]))
        dve.then(tt(lbv, sm[:, 12:16], sm[:, 4:8], ALU.mult))
        t_lb = dve.then(ts(omlb, lbv, -1.0, 1.0, ALU.mult, ALU.add))
        pe.wait((s_con1, 16))

        marks = {}

        def take_q_(n, pb, tok):
            return [act.run(af(aqT[:, n:n + 2, :], pb, ACT.Copy), tok)]

        lin_T("w_in_t", hTv, KD, t_h, take_q_, 4)
        bk = bank()
        pb = banks[bk]
        w, there = take("w_in_t")
        wv = [t3(z, KD) for z in w]
        items = []
        for k in range(KD):
            items += three(pb[:, 0:256], [z[:, k, :] for z in wv], [z[:, k, :] for z in hTv], k == 0, k == KD - 1)
        release(mm_group(bk, items, *there))
        w, there = take("w_in_t")
        wv = [t3(z, KD) for z in w]
        items = []
        for b in range(TB):
            for k in range(KD):
                items += three(pb[:, 256 + b * P:256 + (b + 1) * P], [z[:, k, b * P:(b + 1) * P] for z in hTv],
                               [z[:, k, :] for z in wv], k == 0, k == KD - 1)
        tok = mm_group(bk, items, *there)
        release(tok)
        act.run(af(aqT[:, 4, :], pb[:, 0:256], ACT.Copy), tok)
        t_kv = act.run(af(av, pb[:, 256:512], ACT.Copy), tok)
        free[bk] = [t_kv]

        def take_in(n, pb, tok):
            dst, func = [(q_s, ACT.Silu), (f_s, ACT.Sigmoid), (hg_s, ACT.Silu)][n // 4]
            n = n % 4
            return [act.run(af(t3(dst, 4)[:, n:n + 2, :], pb, func), tok)]

        st = small[:, 64:96]

        def attention(blk):
            nk = P * (blk + 1)
            Sv = S_s[:, 0:8 * nk].rearrange("p (h s) -> p h s", h=8)
            Ev = S_e[:, 0:8 * nk].rearrange("p (h s) -> p h s", h=8)
            Bv = t3(bias8, 8)[:, :, 256 - nk:256]
            for h2 in range(4):
                bk = bank()
                pb = t3(banks[bk][:, :], 2)
                items = []
                for q in range(2):
                    h = 2 * h2 + q
                    kv, j = h // 4, h % 4
                    items.append((pb[:, q, 0:nk], aqT[64 * kv:64 * kv + 64, j, blk * P:(blk + 1) * P],
                                  aqT[64 * kv:64 * kv + 64, 4, 0:nk], True, True))
                tok = mm_group(bk, items, t_kv)
                dve.run(stt(Sv[:, 2 * h2:2 * h2 + 2, :], pb[:, :, 0:nk], 0.125, Bv[:, 2 * h2:2 * h2 + 2, :],
                            ALU.mult, ALU.add), tok, t_bias)
                free[bk] = [dve.last()]
            yield
            mx, sk, sm_, rc = st[:, 0:8], st[:, 8:16], st[:, 16:24], st[:, 24:32]
            dve.then(lambda e: e.tensor_reduce(mx, Sv, AX, ALU.max))
            dve.then(tt(mx, mx, C1("sinks"), ALU.max))
            dve.then(tt(sk, C1("sinks"), mx, ALU.subtract))
            dve.then(ts(mx, mx, -1.0, None, ALU.mult))
            t_m = [dve.last(), pe.last()]
            act.run(af(sk, sk, ACT.Exp), *t_m)
            for h in range(4):
                act.run(af(Ev[:, h, :], Sv[:, h, :], ACT.Exp, bias=mx[:, h:h + 1], accum=sm_[:, h:h + 1]))
            yield
            for h in range(4, 8):
                act.run(af(Ev[:, h, :], Sv[:, h, :], ACT.Exp, bias=mx[:, h:h + 1], accum=sm_[:, h:h + 1]))
            t_e = act.last()
            yield
            dve.run(tt(sm_, sm_, sk, ALU.add), t_e)
            dve.then(lambda e: e.reciprocal(rc, sm_))
            t_p = dve.then(tt(Ev, Ev, rc.unsqueeze(2).to_broadcast([P, 8, nk]), ALU.mult))
            yield
            yield
            for kv in range(2):
                pTv = pT[:, kv * 1024:kv * 1024 + nk * 4].rearrange("p (a h t) -> p a h t", a=blk + 1, h=4)
                t_tr = []
                for a in range(blk + 1):
                    bk = bank()
                    pb = banks[bk]
                    tok = tr_group(bk, [(pb[:, q * P:(q + 1) * P], Ev[:, 4 * kv + q, a * P:(a + 1) * P])
                                        for q in range(4)], t_p)
                    t_tr = act.run(af(pTv[:, a, :, :], t3(pb[:, :], 4), ACT.Copy), tok)
                    free[bk] = [t_tr]
                yield
            bo = bank()
            po = banks[bo]
            items = []
            for kv in range(2):
                pTv = pT[:, kv * 1024:kv * 1024 + nk * 4].rearrange("p (a h t) -> p a h t", a=blk + 1, h=4)
                for j in range(4):
                    for a in range(blk + 1):
                        items.append((po[64 * kv:64 * kv + 64, j * P:(j + 1) * P],
                                      av[:, a * P + 64 * kv:a * P + 64 * kv + 64], pTv[:, a, j, :], a == 0, a == blk))
            tok = mm_group(bo, items, t_tr)
            dst = [z[:, :, blk * P:(blk + 1) * P] for z in yaT]
            marks["ya"] = parts(dst, t3(po[:, :], 4), tok)
            free[bo] = [marks["ya"]]
            yield

        def hgrn(t_gates, t_hi):
            t_ya = marks["ya"]
            f4 = t3(f_s, 4)
            for h in range(4):
                dve.run(ts(f4[:, h, :], f4[:, h, :], omlb[:, h:h + 1], lbv[:, h:h + 1], ALU.mult, ALU.add),
                        t_gates, t_lb)
            a = act.run(af(scr[:, 0:1024], f_s, ACT.Ln), dve.last(), pe.last())
            dve.then(ts(f_s, f_s, -1.0, 1.0, ALU.mult, ALU.add), a)
            d = dve.run(lambda e: e.tensor_tensor_scan(h_b, C1("reset"), scr[:, 0:1024], 0.0, ALU.mult, ALU.add), a,
                        t_ya)
            yield
            bl = h_b.rearrange("p (n c) -> p n c", c=32)[:, :, 31:32]
            eb = scr[:, 1024:2048]
            a1_ = act.run(af(eb, h_b, ACT.Exp), d)
            a2_ = act.run(af(h_kinv, h_b, ACT.Exp, scale=-1.0))
            decay = small[:, 128:160]
            act.run(af(decay.unsqueeze(2), bl, ACT.Exp))
            dve.run(tt(h_kd.rearrange("p (n c) -> p n c", c=32), bl.to_broadcast([P, 32, 32]),
                       h_b.rearrange("p (n c) -> p n c", c=32), ALU.subtract), d)
            a3_ = act.run(af(h_kd, h_kd, ACT.Exp), dve.last())
            yield
            yield
            dve.run(tt(q_s, q_s, eb, ALU.mult), a1_)
            t_kq = dve.run(tt(h_kinv, h_kinv, f_s, ALU.mult), a2_)
            t_kd = dve.run(tt(h_kd, h_kd, f_s, ALU.mult), a3_)
            t_hz = dve.run(lambda e: e.memset(h_AT, 0.0), t_ya)
            yield
            yield
            kdT = h_kdn.rearrange("p (b h d) -> p b h d", b=2, h=4)
            for b in range(TB):
                bk = bank()
                pb = banks[bk]
                tok = tr_group(bk, [(pb[:, h * P:(h + 1) * P], h_kd[:, h * T + b * P:h * T + (b + 1) * P])
                                    for h in range(4)], t_kd)
                t_kdn = act.run(af(kdT[:, b], t3(pb[:, :], 4), ACT.Copy), tok)
                free[bk] = [t_kdn]
            AT = h_AT.rearrange("p (b h t) -> p b h t", b=2, h=4)
            for b in range(TB):
                bk = bank()
                pb = banks[bk]
                tok = mm_group(bk, [(pb[:, h * P:(h + 1) * P], h_kinv[:, h * T + b * P:h * T + (b + 1) * P],
                                     q_s[:, h * T + b * P:h * T + (b + 1) * P], True, True) for h in range(4)],
                               t_kq)
                t_AT = dve.run(lambda e, b=b, pb=pb: e.copy_predicated(
                    AT[:, b], C1("hmask").bitcast(I32).unsqueeze(1).to_broadcast([P, 4, P]), t3(pb[:, :], 4)),
                    tok, t_hz)
                free[bk] = [t_AT]
            yield
            Sv = h_S.rearrange("p (h n v) -> p h n v", h=4, n=8)
            hiv = hi_s.rearrange("p (b h v) -> p b h v", b=2, h=4)
            for n in range(7):
                b, r = n // 4, 32 * (n % 4)
                bk = bank()
                pb = banks[bk]
                tok = mm_group(bk, [(pb[:, h * P:(h + 1) * P], kdT[r:r + 32, b, h, :], hiv[r:r + 32, b, h, :],
                                     True, True) for h in range(4)], t_kdn, t_hi)
                for h in range(4):
                    if n == 0:
                        ins = cp(Sv[:, h, 1, :], pb[:, h * P:(h + 1) * P])
                    else:
                        ins = stt(Sv[:, h, n + 1, :], Sv[:, h, n, :], decay[:, h * 8 + n:h * 8 + n + 1],
                                  pb[:, h * P:(h + 1) * P], ALU.mult, ALU.add)
                    dve.run(ins, tok, t_state if n else tok)
                t_state = dve.last()
                free[bk] = [t_state]
                yield
            yo = scr[:, 0:1024]
            for h in range(4):
                bk = bank()
                pb = banks[bk]
                items = []
                for b in range(TB):
                    items.append((pb[:, b * P:(b + 1) * P], hiv[:, b, h, :], AT[:, b, h, :], b == 0, False))
                for n in range(1, 8):
                    items.append((pb[:, n * 32:(n + 1) * 32], Sv[:, h, n, :],
                                  q_s[:, h * T + n * 32:h * T + n * 32 + 32], False, n == 7))
                tok = mm_group(bk, items, t_AT, t_state)
                dve.run(cp(yo[:, h * T:(h + 1) * T], pb[:, 0:256]), tok)
                free[bk] = [dve.last()]
            a = act.run(af(h_sq, yo, ACT.Square), dve.last())
            yield
            yield
            for h2 in range(2):
                bk = bank()
                pb = banks[bk]
                tok = mm_group(bk, [(pb[:, :], C1("mean128"), h_sq[:, h2 * 512:(h2 + 1) * 512], True, True)], a)
                d = dve.run(ts(h_b[:, h2 * 512:(h2 + 1) * 512], pb[:, :], EPS, None, ALU.add), tok)
                free[bk] = [d]
            act.run(af(h_b, h_b, ACT.Ln), d)
            a = act.then(af(h_b, h_b, ACT.Exp, scale=-0.5))
            dve.run(tt(yo, yo, hg_s, ALU.mult), t_gates)
            yield
            dve.run(stt(yo, yo, C1("g_hgrn"), h_b, ALU.mult, ALU.mult), a, dve.last())
            marks["yh"] = parts([z.rearrange("p a b -> p (a b)") for z in yhT], yo, dve.last())
            yield

        side.append(attention(0))
        side.append(attention(1))
        lin_T("w_in_t", hTv, KD, [], take_in, 12)
        t_gates = act.last()
        tok = lin_A("w_in_hi", hTv, KD, 512, [])
        for b in range(TB):
            t_hi = act.run(af(hi_s[:, b * 512:(b + 1) * 512], banks[b][:, :], ACT.Copy), tok[b])
            free[b] = [t_hi]
        drain()
        t_ya = marks["ya"]
        side.append(hgrn(t_gates, t_hi))
        step()

        def take_gate(n, pb, tok):
            dst = ga[:, n:n + 2, :] if n < 8 else gh[:, n - 8:n - 6, :]
            return [act.run(af(dst, pb, ACT.Sigmoid), tok, t_ya)]

        lin_T("w_in_g", hTv, KD, [], take_gate, 16)
        t_sig = act.last()

        t_mrg = []

        def merge_a(n, pb, tok):
            return [dve.run(tt(ga[:, n:n + 2, :], ga[:, n:n + 2, :], pb, ALU.mult), tok, t_sig)]

        def merge_h(n, pb, tok):
            bf = dve.run(tt(gh[:, n:n + 2, :], gh[:, n:n + 2, :], pb, ALU.mult), tok)
            dve.then(tt(ga[:, n:n + 2, :], ga[:, n:n + 2, :], gh[:, n:n + 2, :], ALU.add))
            t_mrg.append(parts([z[:, n:n + 2, :] for z in mrg], ga[:, n:n + 2, :], dve.last()))
            return [bf]

        lin_T("w_ap", yaT, 4, [t_ya], merge_a, 8)
        drain()
        lin_T("w_hp", yhT, 4, [marks["yh"]], merge_h, 8)
        tok = lin_A("w_out", mrg, KD, D, lambda k: [t_mrg[k // 2]])
        x_sums = add_residual(tok, scr)

        t_h = norm_to_T(xres, "g_ffn", hTv, scr, x_sums)
        before_peer = all_done()

        def a2(at, n):
            return A2[:, at:at + n]

        qT = t3(a2(11776, 4096), 16)
        sc_store = [a2(15872, 2048), a2(17920, 2048)]
        scw = a2(19968, 2048)
        cand = a2(22016, 2048)
        candw = a2(24064, 2048)
        oh = a2(26112, 2048)
        oh2 = a2(28160, 2048)
        keys = a2(26112, 2048)
        val = a2(30208, 256)
        idx = a2(30464, 256)
        idxf = a2(30720, 256)
        best = a2(30976, 128)
        posu = a2(31104, 384)
        posf = a2(31488, 256)
        route_from = 11776
        load(s_keys, keys, keys_d, *before_peer)
        dve.wait(*before_peer)
        act.wait(*before_peer)

        def take_q(n, pb, tok):
            return [act.run(af(qT[:, n:n + 2, :], pb, ACT.Copy), tok)]

        lin_T("w_pq", hTv, KD, t_h, take_q, 16)
        t_q = act.last()
        t_sc = []
        for b in range(TB):
            for g in range(4):
                bk = bank()
                pb = banks[bk]
                tok = mm_group(bk, [(pb[:, q * P:(q + 1) * P], qT[:, 4 * g + q, b * P:(b + 1) * P],
                                     keys[:, (4 * g + q) * P:(4 * g + q + 1) * P], True, True) for q in range(4)],
                               t_q, (s_keys, 16))
                act.run(af(sc_store[b][:, g * 512:(g + 1) * 512], pb[:, :], ACT.Copy), tok)
                free[bk] = [act.last()]
            t_sc.append(act.last())

        def top16(src, work, vals, idxs, n, per, *after):
            for j in range(n):
                t1 = dve.run(lambda e, j=j: e.max(vals[:, j, 0:8], src[:, j, :]), *after)
                if j % per == per - 1:
                    yield
            for j in range(n):
                t = dve.run(lambda e, j=j: e.match_replace(work[:, j, :], vals[:, j, 0:8], src[:, j, :], -3e38), t1)
                if j % per == per - 1:
                    yield
            for j in range(n):
                t2 = dve.run(lambda e, j=j: e.max(vals[:, j, 8:16], work[:, j, :]), t)
                if j % per == per - 1:
                    yield
            for j in range(n):
                dve.run(lambda e, j=j: e.max_index(idxs[:, j, 0:8], vals[:, j, 0:8], src[:, j, :]), t2)
                dve.run(lambda e, j=j: e.max_index(idxs[:, j, 8:16], vals[:, j, 8:16], work[:, j, :]), t2)
                if j % (per // 2) == per // 2 - 1:
                    yield

        def routing(b):
            scb = t3(sc_store[b], 16)
            scwv = t3(scw, 16)
            v3 = t3(val, 16)
            i3 = t3(idx, 16).bitcast(U32)
            yield from top16(scb, scwv, v3, i3, 16, 8, t_sc[1], dve.last())
            dve.then(cp(idxf, idx.bitcast(U32)))
            vv = val.rearrange("p (h q a) -> p h q a", h=8, q=2)
            iv = idxf.rearrange("p (h q a) -> p h q a", h=8, q=2)
            shape = [P, 8, 16, 16]
            dve.then(tt(t4(cand, 8, 16), vv[:, :, 0, :].unsqueeze(3).to_broadcast(shape),
                        vv[:, :, 1, :].unsqueeze(2).to_broadcast(shape), ALU.add))
            yield
            bv = t3(best, 8)
            pu = t3(posu[:, 0:128], 8).bitcast(U32)
            yield from top16(t3(cand, 8), t3(candw, 8), bv, pu, 8, 4, dve.last())
            pall = posu[:, 0:128].bitcast(U32)
            dve.then(ts(posu[:, 128:256].bitcast(U32), pall, 4, None, ALU.logical_shift_right))
            dve.run(ts(posu[:, 256:384].bitcast(U32), pall, 15, None, ALU.bitwise_and))
            dve.then(cp(posf, posu[:, 128:384].bitcast(U32)))
            bex = scw[:, 256:384]
            dve.run(tt(t3(bex, 8), bv, bv[:, :, 0:1].to_broadcast([P, 8, 16]), ALU.subtract))
            t_e = act.run(af(bex, bex, ACT.Exp), dve.last())
            yield
            sel_i = [scw[:, 0:128], scw[:, 128:256]]
            for q in range(2):
                ps = t3(posf[:, q * P:(q + 1) * P], 8)
                o4 = t4(oh, 8, 16)
                dve.then(tt(o4, ps.unsqueeze(3).to_broadcast(shape),
                            K_("iota16").unsqueeze(1).unsqueeze(1).to_broadcast(shape), ALU.is_equal))
                dve.then(tt(t4(oh2, 8, 16), o4, iv[:, :, q, :].unsqueeze(2).to_broadcast(shape), ALU.mult))
                yield
                dve.then(lambda e, q=q: e.tensor_reduce(t3(sel_i[q], 8), t4(oh2, 8, 16), AX, ALU.add))
                yield
            dve.then(lambda e: e.tensor_reduce(scw[:, 384:392], t3(bex, 8), AX, ALU.add), t_e)
            dve.then(lambda e: e.reciprocal(scw[:, 392:400], scw[:, 384:392]))
            dve.then(tt(t3(bex, 8), t3(bex, 8), scw[:, 392:400].unsqueeze(2).to_broadcast([P, 8, 16]), ALU.mult))
            t_r = dve.last()
            for _ in range(3):
                yield
            bk = bank()
            pb = banks[bk]
            tok = tr_group(bk, [(pb[:, q * P:(q + 1) * P], s) for q, s in enumerate([sel_i[0], sel_i[1], bex])], t_r)
            t_i = dve.run(cp(t3(iT[:, :], 3)[:, :, b * P:(b + 1) * P], t3(pb[:, 0:384], 3)), tok)
            free[bk] = [t_i]
            gt = iT[:, 2 * T + b * P:2 * T + (b + 1) * P]
            dve.run(cp(col_b[:, b * P:(b + 1) * P], iT[:, T + b * P:T + (b + 1) * P]), t_i)
            for j in range(3):
                gj = gate3[:, j * T + b * P:j * T + (b + 1) * P]
                dve.then(cp(gj, gt))
                if j < 2:
                    dve.then(tt(gt, gt, gj, ALU.subtract))
            marks["route"] = dve.last()
            yield

        acts = t3(A2[:, :], P)

        oh_used = [[], []]
        t_iota = dve.run(cp(iota_b[:, :], K_("iota")))

        def gates(half, t_acts):
            lo = 64 * half
            for g in range(T // OB):
                z = g % 2
                t = g * OB
                o1 = oh1[:, z * OB * P:(z + 1) * OB * P]
                o3 = og[:, z * 3 * OB * 64:(z + 1) * 3 * OB * 64]
                for q in range(OB):
                    t_p = pool.run(ts(o1[:, q * P:(q + 1) * P], K_("iota"), iT[:, t + q:t + q + 1], None,
                                      ALU.is_equal), marks["route"], *oh_used[z])
                shape = [P, OB, 64]
                t_eq = dve.run(tt(t3(og_eq[:, :], OB), iota_b[:, lo:lo + 64].unsqueeze(1).to_broadcast(shape),
                                  col_b[:, t:t + OB].unsqueeze(2).to_broadcast(shape), ALU.is_equal),
                               marks["route"], t_iota, *oh_used[z])
                shape = [P, 3, OB, 64]
                t_d = dve.run(tt(t4(o3, 3, OB), t3(og_eq[:, :], OB).unsqueeze(1).to_broadcast(shape),
                                 t3(gate3[:, :], 3)[:, :, t:t + OB].unsqueeze(3).to_broadcast(shape), ALU.mult), t_eq)
                if g:
                    yield
                bk = bank()
                pb = banks[bk]
                tok = mm_group(bk, [(pb[:, q * 64:(q + 1) * 64], o1[:, q * P:(q + 1) * P],
                                     o3[:, (j * OB + q) * 64:(j * OB + q + 1) * 64], j == 0, j == 2)
                                    for q in range(OB) for j in range(3)], t_p, t_d)
                oh_used[z] = [tok]
                sl = acts[:, lo:lo + 64, g * OB:(g + 1) * OB].rearrange("p i t -> p t i")
                marks[f"g{half}"] = dve.run(tt(sl, sl, t3(pb[:, 0:64 * OB], OB), ALU.mult), tok, t_acts)
                free[bk] = [dve.last()]
            yield

        side.append(routing(0))
        side.append(routing(1))

        def gelu(n, pb, tok):
            waits = [t_sc[1]] if 256 * (n + 2) > route_from else []
            if 256 * (n + 2) > 15872:
                drain_routing()
                waits.append(marks["route"])
            return [act.run(af(acts[:, n:n + 2, :], pb, ACT.Gelu), tok, *waits)]

        def drain_routing():
            if "routed" not in marks:
                drain()
                marks["routed"] = 1

        pool_of[0] = 1
        lin_T("u", hTv, KD, [], gelu, 62, steps=(1,) * 13 + (2,))
        pool_of[0] = 0
        drain_routing()
        lin_T("u", hTv, KD, [], lambda n, pb, tok: gelu(n + 62, pb, tok), 2)
        side.append(gates(0, act.last()))
        lin_T("u", hTv, KD, [], lambda n, pb, tok: gelu(n + 64, pb, tok), 64, steps=(1,) * 31 + (2,))
        t_acts = act.last()
        t_hused = pe.last()
        drain()
        side.append(gates(1, t_acts))
        pool_of[0] = 6

        after = [t for i in range(4) for t in free[i]]
        acth = (t3(hTh[:, :], 8), t3(hTl[:, :], 8))
        act_used, act_there = {}, {}

        def cut_acts(n):
            if n > 127:
                return
            before = [act_used[n - 8]] if n >= 8 else [t_hused]
            half = marks["g0"] if n < 64 else marks["g1"]
            act_there[n] = parts([z[:, n % 8, :] for z in acth], acts[:, n, :], half, *before)

        for n in range(2):
            cut_acts(n)
        CON2_AT = 0
        at0 = NCON2 + D + 1536
        assert 8192 + at0 + 2048 <= 256 * 61 and 8192 + at0 + 4096 <= 256 * 72

        def a3(at, n):
            assert at0 + at + n <= 24576, (at, n)
            return A3[:, at0 + at:at0 + at + n]

        memx = a3(0, 2048)
        mscr = a3(2048, 2048)
        yT = two(sub(R3, 0, 2048), 8)
        mT = two(sub(R3, 2048, 4096), 8)

        def mem_norm(t_gone):
            dve.wait((s_mem, 32))
            sums = []
            for b in range(TB):
                for h in range(2):
                    sums.append(squares(memx, b, h, mscr, (s_mem, 32), t_gone))
                    yield
            yield from norm_steps(memx, "g_mem2", mT, mscr, sums[1::2], (4, 5, 6, 7), 2, slow=True)

        v_items, v_waits = [[], []], []
        for n in range(128):
            w, there = take("v")
            if n == 62:
                drain()
                pool_of[0] = 0
            cut_acts(n + 2)
            v_waits += [*there, act_there[n]]
            for b in range(TB):
                for h in range(2):
                    v_items[b] += three(banks[2 * b + h][:, :], [z[:, n % 8, b * P:(b + 1) * P] for z in acth],
                                        [z[:, h * 512:(h + 1) * 512] for z in w], n == 0, n == 127)
            if n == 126:
                continue
            tok = [pe.run(products(z), *v_waits, *after) for z in v_items]
            v_items, v_waits = [[], []], []
            act_used[n] = tok[1]
            release(tok[1], 2 if n == 127 else 1)
            step(2 if n in (20, 40) else 1)
            if n == 60:
                t_gone = [tok[1], act_there[n]]
                for b in range(TB):
                    load(s_mem, A3[:, at0 + b * D:at0 + (b + 1) * D], mem[b * P:(b + 1) * P, :], *t_gone)
            elif n == 66:
                load(s_gf, A3[:, NCON2:NCON2 + D], gf_d.partition_broadcast(P))
            elif n == 72:
                load(s_w2c, A3[:, NCON2 + D:NCON2 + D + 1536], w2c_d)
                side.append(mem_norm(tok[1]))
            elif n == 78:
                load(s_con2, A3[:, 0:NCON2], con2_d)

        C2 = pick(A3, 0, OFF2)
        gfin = A3[:, NCON2:NCON2 + D]
        wc = A3[:, NCON2 + D:NCON2 + D + 1536].rearrange("p (q h e) -> p q h e", q=3, h=4)
        kT2 = t3(memx, 8)
        v2 = mscr
        scr3 = a3(4096, 2048)
        hm = a3(4096, 1024)
        hm2 = a3(5120, 1024)
        uT = t3(a3(6144, 512), 2)
        aT = t3(a3(6656, 512), 2)
        gT = t3(a3(7168, 512), 2)
        xcT = t3(a3(7680, 1024), 4)
        ocT = t3(a3(8704, 1024), 4)
        vg = a3(9728, 512)
        xcv = t3(a3(10240, 1024), 4)
        qTm = t3(a3(11264, 1024), 4)
        kTm = t3(a3(12288, 1024), 4)
        vnm = a3(13312, 1024)
        knm = a3(14336, 512)
        rows = a3(14848, 2304)
        wTm = a3(17152, 384)
        cm = a3(17536, 512)
        conv_o = A3[:, NCON2:NCON2 + 512]
        conv_p = A3[:, NCON2 + 512:NCON2 + 1024]
        m_scr = [(wTm, cm, a3(18048, 256)), (a3(18304, 384), a3(18688, 512), hm2[:, 512:768])]

        def final_norm(g, sums, *after):
            out_ = []
            for b in range(TB):
                t = inv_rms(b, sums[b])
                for h in range(2):
                    s_ = xres[:, b * D + h * 512:b * D + (h + 1) * 512]
                    out_.append(dve.run(stt(s_, s_, small[:, 4 * b + 2:4 * b + 3], g[:, h * 512:(h + 1) * 512],
                                            ALU.mult, ALU.mult), t, *after))
            return out_

        t_v = tok

        def bridge():
            sums = add_residual(t_v, scr3)
            yield
            t_x = final_norm(gfin, sums, (s_gf, 16))
            yield
            sums = [squares(xres, b, h, scr3, t_x[2 * b + h]) for b in range(TB) for h in range(2)][1::2]
            yield
            yield from norm_steps(xres, "g_mix2", hTv, scr3, sums, (0, 1, 2, 3), 1)

        pool_of[0] = 2
        ahead(2)
        side.append(bridge())
        step()
        t_mT = normed["g_mem2"]

        def to(dst, n0=0):
            def f(n, pb, tok):
                return [act.run(af(dst[:, n0 + n:n0 + n + 2, :], pb, ACT.Copy), tok)]
            return f

        lin_T("w_xk", mT, KD, t_mT, to(kT2), 6)
        act.wait((s_con2, 16))
        dve.wait((s_con2, 16))
        pool.wait((s_con2, 16))
        pe.wait((s_con2, 16))
        wsT = C2("wsT")
        for h in range(4):
            t_ws = pool.run(tt(wsT[:, h * P:(h + 1) * P], wsT[:, h * P:(h + 1) * P], C2("causal"), ALU.mult))
        drain()
        pool_of[0] = 0
        t_h = normed["g_mix2"]
        before2 = all_done()
        t_wg = [parts([z[:, :] for z in wgp], C2("wgate"))]

        def row_(i, n=T):
            return rows[0:4, i * T:i * T + n]

        li, lf, bc, Rr, pm, mm_, emm, t0, t1 = (row_(i) for i in range(9))
        Rc = small[:, 160:168]

        def gate_rows():
            bg = bank()
            pbg = banks[bg]
            items = []
            for k in range(KD):
                items += three(pbg[0:36, 0:256], [z[:, 36 * k:36 * k + 36] for z in wgp], [z[:, k, :] for z in hTv],
                               k == 0, k == KD - 1)
            tok_g = mm_group(bg, items, *t_wg)
            dve.run(ts(li, pbg[0:4, 0:256], C2("bi")[0:4, :], None, ALU.add), tok_g)
            d = dve.run(ts(t0, pbg[32:36, 0:256], C2("bf")[0:4, :], None, ALU.add))
            free[bg] = [d]
            yield
            dve.then(ts(lf, t0, 0.0, None, ALU.min))
            dve.run(ts(t1, t0, 0.0, None, ALU.max))
            dve.then(tt(t1, lf, t1, ALU.subtract))
            act.run(af(t1, t1, ACT.Exp), dve.last())
            dve.then(ts(t1, t1, 1.0, None, ALU.add), act.last())
            act.run(af(t1, t1, ACT.Ln), dve.last())
            t_ln = act.last()
            yield
            dve.then(tt(lf, lf, t1, ALU.subtract), t_ln)
            one_row = C2("ones")[0:4, :]
            for c in range(2):
                s = slice(c * P, (c + 1) * P)
                dve.then(lambda e, s=s: e.tensor_tensor_scan(bc[:, s], one_row, lf[:, s], 0.0, ALU.mult, ALU.add))
            dve.then(tt(Rr, li, bc, ALU.subtract))
            for c in range(2):
                s = slice(c * P, (c + 1) * P)
                init = 0.0 if c == 0 else mm_[:, P - 1:P]
                dve.then(lambda e, s=s, init=init: e.tensor_tensor_scan(pm[:, s], one_row, Rr[:, s], init,
                                                                        ALU.mult, ALU.max))
                dve.then(tt(mm_[:, s], bc[:, s], pm[:, s], ALU.add))
            act.run(af(emm, mm_, ACT.Exp, scale=-1.0), dve.last())
            dve.then(ts(t0[:, P:T], pm[:, P:T], -1.0, mm_[:, P - 1:P], ALU.mult, ALU.add))
            marks["rows"] = act.run(af(t0[:, P:T], t0[:, P:T], ACT.Exp), dve.last())
            t_rows = dve.last()
            yield
            yield
            bk = bank()
            pb = banks[bk]
            tok = tr_group(bk, [(pb[:, c * 4:c * 4 + 4], Rr[:, c * P:(c + 1) * P]) for c in range(2)], t_rows)
            marks["Rc"] = dve.run(cp(Rc, pb[:, 0:8]), tok)
            free[bk] = [dve.last()]
            yield

        act.wait(*before2)
        dve.wait(*before2)

        def take2(n, pb, tok):
            if n < 4:
                marks["xc"] = act.run(af(xcT[:, n:n + 2, :], pb, ACT.Copy), tok)
            elif n < 6:
                marks["a"] = act.run(af(aT, pb, ACT.Copy), tok)
            elif n < 8:
                marks["g"] = act.run(af(gT, pb, ACT.Sigmoid), tok)
            elif n < 12:
                act.run(af(ocT[:, n - 8:n - 6, :], pb, ACT.Sigmoid), tok)
            else:
                act.run(af(uT, pb, ACT.Gelu), tok)
            return [act.last()]

        def conv(eng, dst, src, w, taps, *after):
            eng.then(ts(dst, src, w(taps - 1), None, ALU.mult), *after)
            for j in range(taps - 1):
                sft = taps - 1 - j
                eng.then(stt(dst[:, sft:T], src[:, 0:T - sft], w(j), dst[:, sft:T], ALU.mult, ALU.add))

        def standardise_T(src, n, meanmat, eps, out_, sq, ready):
            bk = bank()
            pb = banks[bk]
            tok = mm_group(bk, [(pb[:, 0:n], meanmat, src, True, True)], ready)
            d = dve.run(tt(out_, src, pb[:, 0:n], ALU.subtract), tok)
            free[bk] = [d]
            a = act.run(af(sq, out_, ACT.Square), d)
            yield
            yield
            bk = bank()
            pb = banks[bk]
            tok = mm_group(bk, [(pb[:, 0:n], meanmat, sq, True, True)], a)
            d = dve.run(ts(sq, pb[:, 0:n], eps, None, ALU.add), tok)
            free[bk] = [d]
            a = act.run(af(sq, sq, ACT.Sqrt), d)
            yield
            dve.run(lambda e: e.reciprocal(sq, sq), a)
            marks["std"] = dve.then(tt(out_, out_, sq, ALU.mult))

        def mixer_a():
            stg = small[:, 176:208]
            t_vg = marks["vg"]
            for b in range(TB):
                s = vg[:, b * 256:(b + 1) * 256]
                o = stg[:, 16 * b:16 * b + 16]
                dve.run(lambda e, s=s, o=o: e.bn_stats(o[:, 0:6], s), t_vg)
                dve.then(lambda e, o=o: e.bn_aggr(o[:, 6:8], o[:, 0:6]))
                dve.then(ts(o[:, 8:9], o[:, 7:8], LN_EPS, None, ALU.add))
                pool.run(tt(o[:, 9:10], o[:, 8:9], small[:, 250:251], ALU.pow), dve.last())
                dve.run(ts(s, s, o[:, 6:7], o[:, 9:10], ALU.subtract, ALU.mult), pool.last())
                dve.then(tt(s, s, C2("lng"), ALU.mult))
                dve.then(tt(s, s, C2("lnb"), ALU.add))
                yield
            t_ln = dve.last()
            yield
            bk = bank()
            pb = banks[bk]
            items = []
            for h in range(4):
                for b in range(TB):
                    o = (h // 2) * 256 + b * P
                    items.append((pb[64 * (h % 2):64 * (h % 2) + 64, o:o + P],
                                  vg[:, b * 256 + h * 64:b * 256 + h * 64 + 64], wsT[:, h * P:(h + 1) * P],
                                  True, True))
            tok = mm_group(bk, items, t_ln, t_ws)
            bsv = t3(C2("bs"), 2)
            ya = t3(vg, 2)
            for b in range(TB):
                dve.run(tt(ya[:, :, b * P:(b + 1) * P], t3(pb[:, :], 2)[:, :, b * P:(b + 1) * P], bsv, ALU.add), tok)
            free[bk] = [dve.last()]
            dve.then(tt(ya, ya, uT, ALU.mult), marks["z"])
            marks["y_a"] = parts([z[:, 0:2, :] for z in yT], ya, dve.last())
            yield

        def mixer_b():
            t_a = dve.run(tt(aT, aT, gT, ALU.mult), marks["g"], marks["a"])
            t_j = [t_a, t_a]
            for i in range(30, -1, -1):
                for j in range(2):
                    o = conv_o[:, j * T:(j + 1) * T]
                    w = C2("cbw", 31 * j + i, 31 * j + i + 1)
                    sft = 30 - i
                    if sft == 0:
                        ins = ts(o, aT[:, j, :], w, C2("cbb", j, j + 1), ALU.mult, ALU.add)
                    else:
                        ins = stt(o[:, sft:T], aT[:, j, 0:T - sft], w, o[:, sft:T], ALU.mult, ALU.add)
                    t_j[j] = dve.run(ins, t_j[j])
                if i % 4 == 0:
                    yield
            t_c = dve.last()
            yield
            yield from standardise_T(conv_o, 512, C2("mean64"), LN_EPS, conv_o, conv_p, t_c)
            for j in range(2):
                act.run(af(conv_o[:, j * T:(j + 1) * T], conv_o[:, j * T:(j + 1) * T], ACT.Silu,
                           bias=C2("gnb", j, j + 1), scale=C2("gng", j, j + 1)), marks["std"])
            marks["y_b"] = parts([z[:, 2:4, :] for z in yT], t3(conv_o, 2), act.last())
            yield

        def mixer_c():
            for j2 in range(2):
                t_j = [marks["xc"]] * 2
                for i in range(3, -1, -1):
                    for q in range(2):
                        j = 2 * j2 + q
                        o, w, sft = hm[:, j * T:(j + 1) * T], C2("ccw", 4 * j + i, 4 * j + i + 1), 3 - i
                        if sft == 0:
                            ins = ts(o, xcT[:, j, :], w, None, ALU.mult)
                        else:
                            ins = stt(o[:, sft:T], xcT[:, j, 0:T - sft], w, o[:, sft:T], ALU.mult, ALU.add)
                        t_j[q] = dve.run(ins, t_j[q])
                for q in range(2):
                    j = 2 * j2 + q
                    t_xc = act.run(af(xcv[:, j, :], hm[:, j * T:(j + 1) * T], ACT.Silu, bias=C2("ccb", j, j + 1)),
                                   t_j[q])
                yield
            yield
            for q, dst in enumerate([qTm, kTm]):
                for j in range(2):
                    bk = bank()
                    pb = banks[bk]
                    tok = mm_group(bk, [(pb[:, i * 256:(i + 1) * 256], wc[:, q, 2 * j + i, :], xcv[:, 2 * j + i, :],
                                         True, True) for i in range(2)], (s_w2c, 16), t_xc)
                    act.run(af(dst[:, 2 * j:2 * j + 2, :], t3(pb[:, :], 2), ACT.Copy,
                               scale=float(np.float32(P ** -0.5)) if q == 0 else 1.0), tok)
                    free[bk] = [act.last()]
                yield
            for b in range(TB):
                bk = bank()
                pb = banks[bk]
                tok = mm_group(bk, [(pb[:, h * P:(h + 1) * P], xcT[:, h, b * P:(b + 1) * P], wc[:, 2, h, :],
                                     True, True) for h in range(4)], t_xc)
                act.run(af(vnm[:, b * 512:(b + 1) * 512], pb[:, :], ACT.Copy), tok)
                free[bk] = [act.last()]
            bk = bank()
            pb = banks[bk]
            tok = mm_group(bk, [(pb[:, h * P:(h + 1) * P], xcv[:, h, 0:P], wc[:, 1, h, :], True, True)
                                for h in range(4)])
            act.run(af(knm, pb[:, :], ACT.Copy), tok)
            free[bk] = [act.last()]
            t_qkv = act.last()
            yield
            yield
            side.append(mixer_heads(0, t_qkv))
            side_d.append(mixer_heads(1, t_qkv))

        def mixer_heads(pair, t_qkv):
            wTm, cm, den = m_scr[pair]
            while "rows" not in marks or "Rc" not in marks:
                yield
            for h in (2 * pair, 2 * pair + 1):
                selh = C2("sel", h * P, (h + 1) * P)[0:4, :]
                bk = bank()
                pb = banks[bk]
                tok = mm_group(bk, [(pb[:, 0:256], selh, pm, True, True),
                                    (pb[:, 256:384], selh, t0[:, P:T], True, True)], marks["rows"])
                t_prev = tok
                wt = wTm[:, 0:256]
                for c in range(2):
                    s = slice(c * P, (c + 1) * P)
                    d = dve.run(ts(wt[:, s], pb[:, s], Rc[:, 4 * c + h:4 * c + h + 1], 0.0, ALU.subtract, ALU.max),
                                tok, t_prev)
                winter = wTm[:, 256:384]
                a = act.run(af(wt, wt, ACT.Exp, scale=-1.0), d)
                a = act.run(af(winter, pb[:, 256:384], ACT.Copy))
                free[bk] = [a]
                yield
                for c in range(2):
                    s = slice(c * P, (c + 1) * P)
                    dve.run(tt(wt[:, s], wt[:, s], C2("causal"), ALU.mult), a, dve.last())
                ksc = cm[:, 0:128]
                dve.then(ts(ksc, knm[:, h * P:(h + 1) * P], wt[:, P - 1:P], None, ALU.mult), t_qkv)
                qw = cm[:, 128:256]
                t_kq = dve.run(tt(qw, qTm[:, h, P:T], winter, ALU.mult))
                bk = bank()
                pb = banks[bk]
                tok = mm_group(bk, [(pb[:, c * P:(c + 1) * P], kTm[:, h, c * P:(c + 1) * P],
                                     qTm[:, h, c * P:(c + 1) * P], True, True) for c in range(2)], t_qkv)
                t_wt = dve.then(tt(wt, wt, pb[:, 0:256], ALU.mult), tok)
                free[bk] = [t_wt]
                yield
                bk = bank()
                pb = banks[bk]
                tok = mm_group(bk, [(pb[:, 0:P], ksc, vnm[:, h * P:(h + 1) * P], True, True),
                                    (pb[:, P:2 * P], ksc, C2("ones"), True, True)], t_kq)
                cn = cm[:, 256:512]
                t_cn = act.run(af(cn, pb[:, 0:256], ACT.Copy), tok)
                free[bk] = [t_cn]
                yield
                bk = bank()
                pb = banks[bk]
                items = []
                for c in range(2):
                    s = slice(c * P, (c + 1) * P)
                    s2 = slice(256 + c * P, 256 + (c + 1) * P)
                    items.append((pb[:, s], vnm[:, c * 512 + h * P:c * 512 + (h + 1) * P], wt[:, s], True, c == 0))
                    if c:
                        items.append((pb[:, s], cn[:, 0:P], qw, False, True))
                    items.append((pb[:, s2], C2("ones"), wt[:, s], True, c == 0))
                    if c:
                        items.append((pb[:, s2], cn[:, P:2 * P], qw, False, True))
                tok = mm_group(bk, items, t_wt, t_cn)
                bk2 = bank()
                pb2 = banks[bk2]
                tok2 = mm_group(bk2, [(pb2[:, 0:256], selh, emm, True, True)])
                dve.run(ts(den, pb[:, 256:512], -1.0, None, ALU.mult), tok)
                dve.then(tt(den, den, pb[:, 256:512], ALU.max))
                dve.then(tt(den, den, pb2[:, 0:256], ALU.max), tok2)
                free[bk2] = [dve.last()]
                dve.then(lambda e: e.reciprocal(den, den))
                dve.then(tt(hm[:, h * T:(h + 1) * T], pb[:, 0:256], den, ALU.mult))
                free[bk] = [dve.last()]
                yield
            j = pair
            yield from standardise_T(hm[:, j * 512:(j + 1) * 512], 512, C2("mean128"), LN_EPS,
                                     hm[:, j * 512:(j + 1) * 512], hm2[:, j * 512:(j + 1) * 512], dve.last())
            while "oc" not in marks:
                yield
            for h in (2 * pair, 2 * pair + 1):
                o = hm[:, h * T:(h + 1) * T]
                o2 = hm2[:, h * T:(h + 1) * T]
                dve.run(ts(o2, xcv[:, h, :], C2("skip", h, h + 1), None, ALU.mult), marks["oc"], dve.last())
                dve.then(stt(o2, o, C2("hng", h, h + 1), o2, ALU.mult, ALU.add))
                t_y = dve.then(tt(o2, o2, ocT[:, h, :], ALU.mult))
                yield
            marks[f"y_c{pair}"] = parts([z[:, 4 + 2 * pair:6 + 2 * pair, :] for z in yT],
                                        t3(hm2[:, pair * 512:(pair + 1) * 512], 2), t_y)
            yield

        lin_T("w2_t", hTv, KD, t_h, take2, 4)
        pool_of[0] = 1
        side_c.append(gate_rows())
        side.append(mixer_c())
        lin_T("w2_t", hTv, KD, [], lambda n, pb, tok: take2(n + 4, pb, tok), 4)
        side_b.append(mixer_b())
        bv_ = bank()
        held.add(bv_)
        for i in range(2):
            w, there = take("w2_v")
            wv = [t3(z, 4) for z in w]
            items = []
            for b in range(TB):
                for k in range(4):
                    items += three(banks[bv_][:, b * 256:(b + 1) * 256],
                                   [z[:, 4 * i + k, b * P:(b + 1) * P] for z in hTv], [z[:, k, :] for z in wv],
                                   i == 0 and k == 0 and b == 0, i == 1 and k == 3)
            tok = mm_group(bv_, items, *there)
            release(tok)
            if i == 0:
                step()
        marks["vg"] = act.run(af(vg, banks[bv_][:, :], ACT.Gelu), tok)
        free[bv_] = [marks["vg"]]
        held.discard(bv_)
        step()
        lin_T("w2_u", hTv, KD, [], lambda n, pb, tok: take2(n + 12, pb, tok), 2)
        marks["z"] = act.last()
        side_c.append(mixer_a())
        tok = lin_A("w_xv", mT, KD, D, [])
        for b in range(TB):
            for h in range(2):
                act.run(af(v2[:, b * D + h * 512:b * D + (h + 1) * 512], banks[2 * b + h][:, :], ACT.Copy), tok[b])
                free[2 * b + h] = [act.last()]

        lin_T("w2_o", hTv, KD, [], lambda n, pb, tok: take2(n + 8, pb, tok), 4)
        marks["oc"] = act.last()

        def mixed(k):
            name = ["y_a", "y_b", "y_c0", "y_c1"][k // 2]
            while name not in marks:
                step()
            return [marks[name]]

        tok = lin_A("w2_out", yT, KD, D, mixed)
        drain()
        pool_of[0] = 0
        xs = a3(8704, 2048)
        x_sums = add_residual(tok, xs)

        normx = norm_steps(xres, "g_x2", hTv, xs, x_sums, (0, 1, 2, 3), 1)
        next(normx)
        side.append(normx)
        lin_T("w_xk2", mT, KD, [], to(kT2, 6), 2)
        drain()
        qT2 = t3(a3(6144, 2048), 8)
        p2 = t4(a3(8192, 2048), 4, 2)
        pT2 = a3(10240, 2048).rearrange("p (a h t) -> p a h t", a=2, h=4)
        oT2 = yT
        sx = small[:, 200:248]
        t_q2, t_o = [], {}

        def take_xq(n, pb, tok):
            t_q2.append(act.run(af(qT2[:, n:n + 2, :], pb, ACT.Copy), tok))
            return [t_q2[-1]]

        def cross():
            for h2 in range(2):
                while len(t_q2) < 2 * (h2 + 1):
                    yield
                t_p = []
                for b in range(TB):
                    g = 2 * h2 + b
                    mx, nm, sm_, rc = (sx[:, 8 * g + 2 * i:8 * g + 2 * i + 2] for i in range(4))
                    bk = bank()
                    pb = t3(banks[bk][:, :], 2)
                    tok = mm_group(bk, [(pb[:, q, :], qT2[:, 2 * (2 * h2 + q) + k, b * P:(b + 1) * P],
                                         kT2[:, 2 * (2 * h2 + q) + k, :], k == 0, k == 1)
                                        for q in range(2) for k in range(2)], t_q2[2 * h2 + 1])
                    d = dve.run(lambda e, mx=mx, pb=pb: e.tensor_reduce(mx, pb, AX, ALU.max), tok)
                    d = dve.run(ts(nm, mx, -1.0 / 16.0, None, ALU.mult), d)
                    for q in range(2):
                        a = act.run(af(p2[:, g, q, :], pb[:, q, :], ACT.Exp, bias=nm[:, q:q + 1], scale=1.0 / 16.0,
                                       accum=sm_[:, q:q + 1]), d)
                    free[bk] = [a]
                    dve.run(lambda e, rc=rc, sm_=sm_: e.reciprocal(rc, sm_), a)
                    t_p.append(dve.then(tt(p2[:, g, :, :], p2[:, g, :, :],
                                           rc.unsqueeze(2).to_broadcast([P, 2, 256]), ALU.mult)))
                    yield
                for b in range(TB):
                    bk = bank()
                    pb = banks[bk]
                    tok = tr_group(bk, [(pb[:, (2 * a + q) * P:(2 * a + q + 1) * P],
                                         p2[:, 2 * h2 + b, q, a * P:(a + 1) * P])
                                        for a in range(2) for q in range(2)], t_p[b])
                    t_pT = act.run(af(pT2[:, :, 2 * h2:2 * h2 + 2, b * P:(b + 1) * P], t4(pb[:, :], 2, 2), ACT.Copy),
                                   tok)
                    free[bk] = [t_pT]
                yield
                for h in range(2 * h2, 2 * h2 + 2):
                    bk = bank()
                    pb = banks[bk]
                    tok = mm_group(bk, [(pb[:, j * 256:(j + 1) * 256],
                                         v2[:, a * D + (2 * h + j) * P:a * D + (2 * h + j + 1) * P],
                                         pT2[:, a, h, :], a == 0, a == 1) for j in range(2) for a in range(2)], t_pT)
                    t_o[h] = parts([z[:, 2 * h:2 * h + 2, :] for z in oT2], t3(pb[:, :], 2), tok)
                    free[bk] = [t_o[h]]
                yield

        def head_ready(k):
            while k // 2 not in t_o:
                step()
            return [t_o[k // 2]]

        side.append(cross())
        lin_T("w_xq", hTv, KD, normed["g_x2"], take_xq, 8)
        tok = lin_A("w_xo", oT2, KD, D, head_ready)
        xs = A4[:, 2048:4096]
        gF = A4[:, 0:1024]
        cF = A4[:, 1024:2048]
        gfin2 = A4[:, 6144:7168]
        x_sums = add_residual(tok, xs)
        done = all_done()
        aF = two((R4[0][:, :], R4[1][:, :]), 22)
        load(s_gf2, gfin2, gf2_d.partition_broadcast(P), *done)
        t_h = norm_to_T(xres, "g_ffn2", hTv, xs, x_sums, early=0)

        t_ffn = []

        def ffn(n, pb, tok):
            j = n // 2
            s = (j % 4) * T
            g, c = gF[:, s:s + T], cF[:, s:s + T]
            before = [t_ffn[j - 4]] if j >= 4 else []
            a = act.run(af(g, pb[:, 0, :], ACT.Copy), tok, *before)
            conv(dve, c, g, lambda i: K_("cfw", 3 * j + i, 3 * j + i + 1), 3, a)
            t_conv = dve.last()
            read, tok_ = [], {}

            def gate():
                tok_["g"] = act.run(af(g, c, ACT.Gelu, bias=K_("cfb", j, j + 1)), t_conv)

            def product():
                read.append(dve.run(tt(c, g, pb[:, 1, :], ALU.mult), tok_["g"]))
                tok_["h"] = act.run(af(aF[0][:, j, :], c, ACT.Copy), read[0])

            def rest():
                t_ffn.append(dve.run(tt(aF[1][:, j, :], c, aF[0][:, j, :].bitcast(F32), ALU.subtract), tok_["h"]))

            later.extend([(unit_no[0] + 2, gate), (unit_no[0] + 3, product), (unit_no[0] + 4, rest)])
            return read

        pool_of[0] = 2
        lin_T("w_up", hTv, KD, t_h, ffn, 44)

        def ffn_ready(k):
            while len(t_ffn) <= k:
                step(0)
            return [t_ffn[k]]

        pool_of[0] = 0
        tok = lin_A("w_down", aF, 22, D, ffn_ready)
        x_sums = add_residual(tok, xs)
        t_x = final_norm(gfin2, x_sums, (s_gf2, 16))
        for b in range(TB):
            for h in range(2):
                load(s_out, out[b * P:(b + 1) * P, h * 512:(h + 1) * 512],
                     xres[:, b * D + h * 512:b * D + (h + 1) * 512], t_x[2 * b + h])
        sp.work.append(lambda e: e.wait_ge(s_out, 64))
        assert taken[0] == len(units) == cut[0]

        block = ctx.enter_context(nc.Block())

        @block.sync
        def _(e):
            sp.emit(e)

        @block.tensor
        def _(e):
            pe.emit(e)

        @block.vector
        def _(e):
            dve.emit(e)

        @block.scalar
        def _(e):
            act.emit(e)

        @block.gpsimd
        def _(e):
            pool.emit(e)


def fill(table, n, values):
    c = np.zeros((P, n), np.float32)
    for name, a in values.items():
        o, w = table[name]
        c[0:a.shape[0], o:o + w] = a
    return c


def shape_constants():
    i = np.arange(P)
    dist = i[:, None] + P - np.arange(256)[None, :]
    causal = i[:, None] <= i[None, :]
    sel = np.zeros((4, 4, P), np.float32)
    for h in range(4):
        sel[h, h] = 1.0
    return {
        "ident": np.eye(P), "mean128": np.full((P, P), 1.0 / 128),
        "mean64": (i[:, None] // 64 == i[None, :] // 64) / 64.0, "ones": np.ones((P, P)), "dist": dist,
        "wmask": np.where((dist >= 0) & (dist < P), 0.0, NEG),
        "hmask": causal & (i[:, None] // 32 == i[None, :] // 32), "causal": causal, "sel": sel.reshape(4, 512),
        "iota": np.broadcast_to(np.arange(P), (P, P)), "iota16": np.broadcast_to(np.arange(16), (P, 16)),
        "reset": np.broadcast_to(np.arange(1024) % 32 != 0, (P, 1024)),
    }


def tiles_T(w):
    K, N = w.shape[0] // P, w.shape[1] // P
    per = UNIT // (K * P)
    a = w.reshape(K, P, N, P).transpose(2, 1, 0, 3)
    return np.ascontiguousarray(a.reshape(N // per, per, P, K * P).transpose(0, 2, 1, 3).reshape(N // per, P, -1))


def tiles_A(w):
    K, N = w.shape[0] // P, w.shape[1]
    per = UNIT // N
    return np.ascontiguousarray(w.reshape(K // per, per, P, N).transpose(0, 2, 1, 3).reshape(K // per, P, per * N))


def cols(v, n):
    return np.asarray(v).reshape(n, P).T


def rep(v):
    return np.broadcast_to(v, (P, v.shape[-1]))


def gate_columns(w):
    o = np.zeros((P, KD, 36), np.float32)
    for q in range(2):
        o[:, :, 32 * q:32 * q + 4] = w[:, 4 * q:4 * q + 4].reshape(KD, P, 4).transpose(1, 0, 2)
    return o.reshape(P, KD * 36)


def layout(a):
    w = a["w_in"][0]
    heads = [c for j in range(4) for h in (j, j + 4) for c in range(h * 64, h * 64 + 64)]
    s = {}
    s["w_in_t"] = tiles_T(np.concatenate([w[:, heads], w[:, 512:1792], w[:, 2304:2816]], 1))
    s["w_in_hi"] = tiles_A(w[:, 1792:2304])
    s["w_in_g"] = tiles_T(w[:, 2816:4864])
    s["w_ap"] = tiles_T(a["w_attn_proj"][0][heads])
    s["w_hp"] = tiles_T(a["w_hgrn_proj"][0])
    s["w_out"] = tiles_A(a["w_out"][0])
    s["w_pq"] = tiles_T(a["w_peer_q"][0])
    u = a["peer_u"][0].reshape(P, P, KD, P)
    s["u"] = np.ascontiguousarray(u.transpose(1, 3, 2, 0).reshape(P, P, 1024))
    s["v"] = np.ascontiguousarray(a["peer_v"][0].reshape(P, P, 1024).transpose(1, 0, 2))
    w2 = a["w_in_2"][0]
    s["w2_t"] = tiles_T(np.concatenate([w2[:, 1024:1536], w2[:, 512:1024]], 1))
    s["w2_u"] = tiles_T(w2[:, 0:256])
    s["w2_o"] = tiles_T(w2[:, 1536:2048])
    s["w2_v"] = tiles_A(w2[:, 256:512])
    s["w2_out"] = tiles_A(a["w_out_2"][0])
    s["w_xk"] = tiles_T(a["w_xkv_2"][0][:, 0:768])
    s["w_xk2"] = tiles_T(a["w_xkv_2"][0][:, 768:D])
    s["w_xv"] = tiles_A(a["w_xkv_2"][0][:, D:2 * D])
    s["w_xq"] = tiles_T(a["w_xq_2"][0])
    s["w_xo"] = tiles_A(a["w_xo_2"][0])
    up = tiles_T(a["w_up_2"][0])
    s["w_up"] = np.ascontiguousarray(up.reshape(2, 22, P, UNIT).transpose(1, 0, 2, 3).reshape(44, P, UNIT))
    s["w_down"] = tiles_A(a["w_down_2"][0])

    c = shape_constants()
    v = {
        "g_mix": cols(a["norm_mix_g"], 8), "g_ffn": cols(a["norm_ffn_g"], 8), "g_mix2": cols(a["norm_mix_g_2"], 8),
        "g_x2": cols(a["norm_x_g_2"], 8), "g_mem2": cols(a["norm_mem_g_2"], 8), "g_ffn2": cols(a["norm_ffn_g_2"], 8),
        "lb": cols(a["hgrn_lb_logits"], 8), "g_hgrn": cols(a["hgrn_norm_g"], 1),
        "cbw": a["conv_b_w_2"][0].reshape(31, 2, P).transpose(2, 1, 0).reshape(P, 62),
        "cbb": cols(a["conv_b_b_2"], 2), "gng": cols(a["gn_b_g_2"], 2), "gnb": cols(a["gn_b_b_2"], 2),
        "ccw": a["conv_c_w_2"][0].reshape(4, 4, P).transpose(2, 1, 0).reshape(P, 16),
        "ccb": cols(a["conv_c_b_2"], 4), "hng": cols(a["hn_c_g_2"], 4), "skip": cols(a["skip_c_2"], 4),
        "cfw": a["conv_f_w_2"][0].reshape(3, 22, P).transpose(2, 1, 0).reshape(P, 66),
        "cfb": cols(a["conv_f_b_2"], 22), "bi": a["b_igate_2"].reshape(4, 1), "bf": a["b_fgate_2"].reshape(4, 1),
        "bs": np.broadcast_to(a["b_s_2"][0].reshape(2, 2, 1, P), (2, 2, 64, P)).transpose(1, 2, 0, 3).reshape(P, 256),
        "wgate": gate_columns(w2[:, 2048:2056]),
        "wsT": a["w_s_2"][0].transpose(2, 0, 1).reshape(P, 512),
        "lng": rep(a["ln_a_g_2"]), "lnb": rep(a["ln_a_b_2"]), "sinks": rep(a["attn_sinks"]),
    }
    v.update(c)
    o = {}
    for name, table, off, n in (("keep", KEEP, KOFF, NKEEP), ("con0", CON0, OFF0, NCON0), ("con1", CON1, OFF1, NCON1),
                                ("con2", CON2, OFF2, NCON2)):
        o[name] = fill(off, n, {k: v[k] for k, _ in table})
    o["keys"] = np.ascontiguousarray(a["peer_keys"][0].transpose(3, 1, 0, 2).reshape(P, 2048))
    o["w2c"] = np.concatenate([a[n][0].transpose(1, 0, 2).reshape(P, 512)
                               for n in ("w_q_c_2", "w_k_c_2", "w_v_c_2")], 1)
    o["gf"] = a["norm_final_g"]
    o["gf2"] = a["final_g_2"]
    return s, o


def kernel(**inputs):
    import numpy as _np
    import concourse.bacc as _bacc
    from concourse import mybir as _mybir
    from concourse.bass_utils import run_bass_kernel_spmd as _run

    a = {k: _np.asarray(v) for k, v in inputs.items()}
    s, o = layout(a)
    nc = _bacc.Bacc("TRN2", target_bir_lowering=False, num_devices=1)
    arrays = {"x": _np.ascontiguousarray(a["x"][0]), "mem": _np.ascontiguousarray(a["mem_2"][0])}
    arrays.update(o)
    arrays.update(s)
    aps = {k: nc.dram_tensor(f"in_{k}", list(z.shape), _mybir.dt.float32, kind="ExternalInput").ap()
           for k, z in arrays.items()}
    out = nc.dram_tensor("out", [T, D], _mybir.dt.float32, kind="ExternalOutput").ap()
    build(nc, aps["x"], aps["mem"], {k: aps[k] for k in s}, aps["keep"], aps["con0"], aps["con1"], aps["con2"],
          aps["keys"], aps["w2c"], aps["gf"], aps["gf2"], out)
    r = _run(nc, [{f"in_{k}": z for k, z in arrays.items()}], core_ids=[0])
    return r.results[0]["out"].reshape(1, T, D)
```
